# Optimizing a Trainium2 kernel written in Bass

```python
import jax, jax.numpy as jnp
from jax import lax
import numpy as np

D_MODEL = 1024
BATCH = 1
SEQ = 1024
DEPTH = 1
DEC_BATCH = 8
DEC_SEQ = 16
PAST_LEN = 512

CHUNK = 64
LEFT_CHUNKS = 8
BAND_CHUNKS = LEFT_CHUNKS + 1
HEAD_DIM = 64
N_HEADS_A = 8
N_HEADS_B = 8
D_A = N_HEADS_A * HEAD_DIM
D_B = N_HEADS_B * HEAD_DIM
D_MIX = D_A + D_B
N_IDX_HEADS = 8
IDX_DIM = 32
TOPK_MAX = 256
MAX_REL = 128
N_REL = 2 * MAX_REL + 1
D_FF = 2816
ROPE_THETA = 10000.0
EPS = 1e-6
Q_BLOCK = 128
PROJ_SIZES = (D_A, D_A, D_A, D_B, D_B, D_B, N_IDX_HEADS * IDX_DIM, IDX_DIM, N_IDX_HEADS)
D_IN = sum(PROJ_SIZES)

kernel_name = "hybrid_chunk_band_dsa_streaming_step"

def _rmsnorm(x, g):
    xf = x.astype(jnp.float32)
    y = xf * lax.rsqrt(jnp.mean(xf * xf, axis=-1, keepdims=True) + EPS)
    return (y * g.astype(jnp.float32)).astype(x.dtype)

def _swiglu(h, wg, wu, wd):
    return (jax.nn.silu(h @ wg) * (h @ wu)) @ wd

def _macaron_ffn(x, g, wg, wu, wd):
    return x + 0.5 * _swiglu(_rmsnorm(x, g), wg, wu, wd)

def _rope(x, pos):
    half = x.shape[-1] // 2
    inv = ROPE_THETA ** (-jnp.arange(half, dtype=jnp.float32) / half)
    ang = pos.astype(jnp.float32)[:, None] * inv[None, :]
    cos, sin = jnp.cos(ang), jnp.sin(ang)
    if x.ndim == 4:
        cos, sin = cos[:, None, :], sin[:, None, :]
    xf = x.astype(jnp.float32)
    x1, x2 = xf[..., :half], xf[..., half:]
    return jnp.concatenate([x1 * cos - x2 * sin, x2 * cos + x1 * sin], axis=-1).astype(x.dtype)

def _mixer_inputs(x, pos, g, w_in):
    b, n, _ = x.shape
    p = _rmsnorm(x, g) @ w_in
    cuts = [int(c) for c in np.cumsum(PROJ_SIZES)[:-1]]
    qa, ka, va, qb, kb, vb, qi, ki, wi = jnp.split(p, cuts, axis=-1)
    hA = lambda t: t.reshape(b, n, N_HEADS_A, HEAD_DIM)
    hB = lambda t: t.reshape(b, n, N_HEADS_B, HEAD_DIM)
    qi = qi.reshape(b, n, N_IDX_HEADS, IDX_DIM)
    return (hA(qa), hA(ka), hA(va), _rope(hB(qb), pos), _rope(hB(kb), pos), hB(vb),
            _rope(qi, pos), _rope(ki, pos), wi)

def _rel_bias(rel_bias, dist):
    return rel_bias[:, jnp.clip(dist, -MAX_REL, MAX_REL) + MAX_REL].astype(jnp.float32)

def _band_attn_prompt(q, k, v, rel_bias):
    b, s, h, d = q.shape
    nc = s // CHUNK
    chunked = lambda t: t.reshape(b, nc, CHUNK, h, d)
    pad = ((0, 0), (LEFT_CHUNKS, 0), (0, 0), (0, 0), (0, 0))
    kc = jnp.pad(chunked(k), pad)
    vc = jnp.pad(chunked(v), pad)
    k_band = jnp.concatenate([kc[:, j:j + nc] for j in range(BAND_CHUNKS)], axis=2)
    v_band = jnp.concatenate([vc[:, j:j + nc] for j in range(BAND_CHUNKS)], axis=2)
    qi = jnp.arange(CHUNK)
    kj = jnp.arange(BAND_CHUNKS * CHUNK)
    dist = LEFT_CHUNKS * CHUNK + qi[:, None] - kj[None, :]
    bias = _rel_bias(rel_bias, dist)
    valid = (jnp.arange(nc)[:, None] + kj[None, :] // CHUNK) >= LEFT_CHUNKS
    sc = jnp.einsum('bcqhd,bckhd->bchqk', chunked(q), k_band).astype(jnp.float32) * (d ** -0.5)
    sc = jnp.where(valid[None, :, None, None, :], sc + bias[None, None], -jnp.inf)
    p = jax.nn.softmax(sc, axis=-1).astype(v.dtype)
    o = jnp.einsum('bchqk,bckhd->bcqhd', p, v_band)
    return o.reshape(b, s, h * d)

def _band_attn_sample(q, k_new, v_new, k_cache, v_cache, rel_bias):
    b, n, h, d = q.shape
    L = k_cache.shape[1]
    k = jnp.concatenate([k_cache, k_new], axis=1)
    v = jnp.concatenate([v_cache, v_new], axis=1)
    dist = (L + jnp.arange(n))[:, None] - jnp.arange(L + n)[None, :]
    sc = jnp.einsum('bqhd,bkhd->bhqk', q, k).astype(jnp.float32) * (d ** -0.5)
    sc = sc + _rel_bias(rel_bias, dist)[None]
    p = jax.nn.softmax(sc, axis=-1).astype(v.dtype)
    o = jnp.einsum('bhqk,bkhd->bqhd', p, v)
    return o.reshape(b, n, h * d)

def _dsa_attend(q, qi, wi, k, v, ki, adm, k_sel):
    isc = jax.nn.relu(jnp.einsum('bqhd,bsd->bqhs', qi, ki).astype(jnp.float32) * (IDX_DIM ** -0.5))
    isc = jnp.einsum('bqhs,bqh->bqs', isc, wi.astype(jnp.float32) * (N_IDX_HEADS ** -0.5))
    isc = jnp.where(adm, isc, -jnp.inf)
    _, idx = lax.top_k(isc, k_sel)
    valid = jnp.take_along_axis(jnp.broadcast_to(adm, isc.shape), idx, axis=-1)
    kg = jax.vmap(lambda kk, ii: kk[ii])(k, idx)
    vg = jax.vmap(lambda vv, ii: vv[ii])(v, idx)
    sc = jnp.einsum('bqhd,bqkhd->bqhk', q, kg).astype(jnp.float32) * (q.shape[-1] ** -0.5)
    sc = jnp.where(valid[:, :, None, :], sc, -jnp.inf)
    p = jax.nn.softmax(sc, axis=-1).astype(v.dtype)
    return jnp.einsum('bqhk,bqkhd->bqhd', p, vg)

def _dsa_prompt(q, k, v, qi, ki, wi, k_sel):
    b, s, h, d = q.shape
    nb = s // Q_BLOCK
    to_blocks = lambda t: jnp.moveaxis(t.reshape((b, nb, Q_BLOCK) + t.shape[2:]), 1, 0)
    key_chunk = jnp.arange(s) // CHUNK

    def block(args):
        qb, qib, wib, bi = args
        qpos = bi * Q_BLOCK + jnp.arange(Q_BLOCK)
        adm = key_chunk[None, :] <= (qpos // CHUNK)[:, None]
        return _dsa_attend(qb, qib, wib, k, v, ki, adm[None], k_sel)

    o = lax.map(block, (to_blocks(q), to_blocks(qi), to_blocks(wi), jnp.arange(nb)))
    return jnp.moveaxis(o, 0, 1).reshape(b, s, h * d)

def _dsa_sample(q, k_new, v_new, qi, ki_new, wi, k_cache, v_cache, ki_cache, k_sel):
    n = q.shape[1]
    k = jnp.concatenate([k_cache, k_new], axis=1)
    v = jnp.concatenate([v_cache, v_new], axis=1)
    ki = jnp.concatenate([ki_cache, ki_new], axis=1)
    adm = jnp.ones((1, n, k.shape[1]), dtype=bool)
    o = _dsa_attend(q, qi, wi, k, v, ki, adm, k_sel)
    return o.reshape(q.shape[0], n, -1)

def setup_inputs(seed: int = 0) -> dict:
    key = jax.random.key(seed)
    ks = jax.random.split(key, 20)
    f32 = jnp.float32
    nrm = lambda k, shape, scale: jax.random.normal(k, shape, f32) * scale
    a_len = min(LEFT_CHUNKS * CHUNK, PAST_LEN)
    return {
        "x_prompt": nrm(ks[0], (BATCH, SEQ, D_MODEL), 1.0),
        "x_sample": nrm(ks[1], (DEC_BATCH, DEC_SEQ, D_MODEL), 1.0),
        "cache_a_k": nrm(ks[2], (DEPTH, DEC_BATCH, a_len, N_HEADS_A, HEAD_DIM), 1.0),
        "cache_a_v": nrm(ks[3], (DEPTH, DEC_BATCH, a_len, N_HEADS_A, HEAD_DIM), 1.0),
        "cache_b_k": nrm(ks[4], (DEPTH, DEC_BATCH, PAST_LEN, N_HEADS_B, HEAD_DIM), 1.0),
        "cache_b_v": nrm(ks[5], (DEPTH, DEC_BATCH, PAST_LEN, N_HEADS_B, HEAD_DIM), 1.0),
        "cache_idx_k": nrm(ks[6], (DEPTH, DEC_BATCH, PAST_LEN, IDX_DIM), 1.0),
        "ffn1_norm": 1.0 + nrm(ks[7], (DEPTH, D_MODEL), 0.01),
        "ffn1_w_gate": nrm(ks[8], (DEPTH, D_MODEL, D_FF), D_MODEL ** -0.5),
        "ffn1_w_up": nrm(ks[9], (DEPTH, D_MODEL, D_FF), D_MODEL ** -0.5),
        "ffn1_w_down": nrm(ks[10], (DEPTH, D_FF, D_MODEL), D_FF ** -0.5),
        "mix_norm": 1.0 + nrm(ks[11], (DEPTH, D_MODEL), 0.01),
        "w_in": nrm(ks[12], (DEPTH, D_MODEL, D_IN), D_MODEL ** -0.5),
        "rel_bias": nrm(ks[13], (DEPTH, N_HEADS_A, N_REL), 0.1),
        "w_out": nrm(ks[14], (DEPTH, D_MIX, D_MODEL), D_MIX ** -0.5),
        "ffn2_norm": 1.0 + nrm(ks[15], (DEPTH, D_MODEL), 0.01),
        "ffn2_w_gate": nrm(ks[16], (DEPTH, D_MODEL, D_FF), D_MODEL ** -0.5),
        "ffn2_w_up": nrm(ks[17], (DEPTH, D_MODEL, D_FF), D_MODEL ** -0.5),
        "ffn2_w_down": nrm(ks[18], (DEPTH, D_FF, D_MODEL), D_FF ** -0.5),
        "final_norm": 1.0 + nrm(ks[19], (D_MODEL,), 0.01),
    }

def reference(x_prompt, x_sample, cache_a_k, cache_a_v, cache_b_k, cache_b_v, cache_idx_k,
              ffn1_norm, ffn1_w_gate, ffn1_w_up, ffn1_w_down, mix_norm, w_in, rel_bias, w_out,
              ffn2_norm, ffn2_w_gate, ffn2_w_up, ffn2_w_down, final_norm):
    s = x_prompt.shape[1]
    n = x_sample.shape[1]
    past = cache_b_k.shape[2]
    pos_p = jnp.arange(s)
    pos_s = past + jnp.arange(n)
    k_sel_p = min(TOPK_MAX, s // 4)
    k_sel_s = min(TOPK_MAX, (past + n) // 4)
    a_keep = min(LEFT_CHUNKS * CHUNK, s)

    yp, ys = x_prompt, x_sample
    akp, avp, bkp, bvp, ikp = [], [], [], [], []
    aks, avs, bks, bvs, iks = [], [], [], [], []
    for l in range(DEPTH):
        yp = _macaron_ffn(yp, ffn1_norm[l], ffn1_w_gate[l], ffn1_w_up[l], ffn1_w_down[l])
        qa, ka, va, qb, kb, vb, qi, ki, wi = _mixer_inputs(yp, pos_p, mix_norm[l], w_in[l])
        o_a = _band_attn_prompt(qa, ka, va, rel_bias[l])
        o_b = _dsa_prompt(qb, kb, vb, qi, ki, wi, k_sel_p)
        yp = yp + jnp.concatenate([o_a, o_b], axis=-1) @ w_out[l]
        yp = _macaron_ffn(yp, ffn2_norm[l], ffn2_w_gate[l], ffn2_w_up[l], ffn2_w_down[l])
        akp.append(ka[:, s - a_keep:])
        avp.append(va[:, s - a_keep:])
        bkp.append(kb)
        bvp.append(vb)
        ikp.append(ki)

        ys = _macaron_ffn(ys, ffn1_norm[l], ffn1_w_gate[l], ffn1_w_up[l], ffn1_w_down[l])
        qa, ka, va, qb, kb, vb, qi, ki, wi = _mixer_inputs(ys, pos_s, mix_norm[l], w_in[l])
        o_a = _band_attn_sample(qa, ka, va, cache_a_k[l], cache_a_v[l], rel_bias[l])
        o_b = _dsa_sample(qb, kb, vb, qi, ki, wi, cache_b_k[l], cache_b_v[l], cache_idx_k[l], k_sel_s)
        ys = ys + jnp.concatenate([o_a, o_b], axis=-1) @ w_out[l]
        ys = _macaron_ffn(ys, ffn2_norm[l], ffn2_w_gate[l], ffn2_w_up[l], ffn2_w_down[l])
        aks.append(ka)
        avs.append(va)
        bks.append(kb)
        bvs.append(vb)
        iks.append(ki)

    yp = _rmsnorm(yp, final_norm)
    ys = _rmsnorm(ys, final_norm)
    return (yp, ys,
            jnp.stack(akp), jnp.stack(avp), jnp.stack(bkp), jnp.stack(bvp), jnp.stack(ikp),
            jnp.stack(aks), jnp.stack(avs), jnp.stack(bks), jnp.stack(bvs), jnp.stack(iks))


_drawn_inputs = setup_inputs


def setup_inputs(seed=0):
    import zlib

    import numpy as np

    out = dict(_drawn_inputs(seed))
    spreads = {}
    factors = {'ffn1_norm': 6.085,
     'mix_norm': 4.82,
     'rel_bias': 8.0,
     'ffn2_norm': 37.512,
     'final_norm': 32.196,
     'cache_a_k': 7.082,
     'cache_a_v': 8.0,
     'cache_b_v': 2.819}
    for name, (base, spread) in spreads.items():
        noise = np.random.default_rng([zlib.crc32(name.encode()), seed]).standard_normal(out[name].shape)
        drawn = base * np.exp(spread * noise) if base else spread * noise
        out[name] = __import__('jax').numpy.asarray(drawn.astype(out[name].dtype))
    for name, factor in factors.items():
        out[name] = (out[name] * factor).astype(out[name].dtype)
    return out
```

```python
from contextlib import ExitStack

import numpy as np

import concourse.bass as bass
from concourse import mybir

F32 = mybir.dt.float32
F32R = mybir.dt.float32r
BF16 = mybir.dt.bfloat16
ALU = mybir.AluOpType
ACT = mybir.ActivationFunctionType
AX = mybir.AxisListType

P = 128
D = 1024
KT = D // P
SEQ, DEC_B, DEC_S, PAST = 1024, 8, 16, 512
NP = SEQ // P
NT = NP + 1
ROWS = NT * P
FF = 2816
FB = 256
FSTEPS = FF // FB
CH = 3
NCH = NT // CH
CW = CH * P
H, HD = 8, 64
HT = H * HD // P
CHUNK, LEFT = 64, 8
IH, ID = 8, 32
TOPK = 256
SEL_S = min(TOPK, (PAST + DEC_S) // 4)
MAXREL = 128
BAND = LEFT * CHUNK + P
KS = PAST + DEC_S
N_QKV = 3 * H * HD
N_IDX = IH * ID + ID + IH
EPS = 1e-6
NEG = -1.0e30
GONE = -3.0e38
UNSEEN = -2.0e38
FIRST = 3.0e38


SBUF_START, SBUF_END = 16512, 229344


class Plan:

    def __init__(self, nc, tag, at):
        self.nc, self.tag, self.at = nc, tag, at

    def __call__(self, name, shape, dtype):
        size = int(np.prod(shape[1:])) * mybir.dt.size(dtype)
        t = self.nc.alloc_sbuf_tensor_at(f"{self.tag}_{name}", shape, dtype, offset=self.at)
        self.at += -(-size // 32) * 32
        assert self.at <= SBUF_END, (self.tag, name, self.at - SBUF_END)
        return t


def add_norm(nc, sb, pb, sem, tag, x_sb, g_dram, xT_hi, xT_lo, ident, x_ready):
    xn = sb(f"{tag}_xn", [P, 2, D], F32)
    g_bc = sb(f"{tag}_g", [P, D], F32)
    st = sb(f"{tag}_st", [P, 6, NT], F32)
    SS, V, SD, R, A, B = range(6)
    xp = pb(f"{tag}_xp", [P, 2, D])
    junk = pb(f"{tag}_junk", [P, 2, D])
    s_g = sem(f"{tag}_g_loaded")
    s_ss = sem(f"{tag}_squares_summed")
    s_v = sem(f"{tag}_mean_ready")
    s_sd = sem(f"{tag}_root_ready")
    s_ch = sem(f"{tag}_newton_step")
    s_xn = sem(f"{tag}_row_normed")
    s_tr = sem(f"{tag}_transposed")
    s_hi = sem(f"{tag}_hi_ready")
    s_lo = sem(f"{tag}_lo_ready")
    cols = lambda k, g: st[:, k, g * CH:(g + 1) * CH]

    def load(sp):
        sp.dma_start(g_bc[:], g_dram.partition_broadcast(P)).then_inc(s_g, 16)

    def act_squares(act, g):
        for t in range(g * CH, (g + 1) * CH):
            x_ready(act, t)
            if t >= 2:
                act.wait_ge(s_ss, t - 1)
            act.activation(junk[:, t % 2, :], x_sb[:, t, :], ACT.Square, accum_out=st[:, SS, t:t + 1]).then_inc(s_ss, 1)

    def act_root(act, g):
        act.wait_ge(s_v, 2 * g + 1)
        act.activation(cols(SD, g), cols(V, g), ACT.Sqrt).then_inc(s_sd, 1)

    def act_all(act):
        act_squares(act, 0)
        act_root(act, 0)
        for g in range(NCH):
            if g + 1 < NCH:
                act_squares(act, g + 1)
            for t in range(g * CH, (g + 1) * CH):
                act.wait_ge(s_tr, t + 1)
                act.activation(xT_hi[:, :, t * P:(t + 1) * P],
                               xp[:, t % 2, :].rearrange("p (k c) -> p k c", k=KT), ACT.Copy).then_inc(s_hi, 1)
            if g + 1 < NCH:
                act_root(act, g + 1)

    def dve_stats(dve, g):
        n = 4 * g
        dve.wait_ge(s_ss, CH * (g + 1))
        dve.tensor_scalar(cols(V, g), cols(SS, g), 1.0 / D, EPS, ALU.mult, ALU.add).then_inc(s_v, 1)
        dve.wait_ge(s_sd, g + 1)
        dve.reciprocal(cols(R, g), cols(SD, g)).then_inc(s_ch, 1)
        dve.wait_ge(s_ch, n + 1)
        dve.tensor_tensor(cols(A, g), cols(R, g), cols(R, g), ALU.mult).then_inc(s_ch, 1)
        dve.wait_ge(s_ch, n + 2)
        dve.tensor_tensor(cols(B, g), cols(A, g), cols(V, g), ALU.mult).then_inc(s_ch, 1)
        dve.wait_ge(s_ch, n + 3)
        dve.tensor_scalar(cols(A, g), cols(B, g), -0.5, 1.5, ALU.mult, ALU.add).then_inc(s_ch, 1)
        dve.wait_ge(s_ch, n + 4)
        dve.tensor_tensor(cols(SS, g), cols(R, g), cols(A, g), ALU.mult).then_inc(s_v, 1)

    def dve_all(dve):
        dve_stats(dve, 0)
        dve.wait_ge(s_g, 16)
        for g in range(NCH):
            for t in range(g * CH, (g + 1) * CH):
                x_ready(dve, t)
                if t == g * CH:
                    dve.wait_ge(s_v, 2 * g + 2)
                if t >= 2:
                    dve.wait_ge(s_tr, t - 1)
                dve.scalar_tensor_tensor(xn[:, t % 2, :], x_sb[:, t, :], st[:, SS, t:t + 1], g_bc[:],
                                         ALU.mult, ALU.mult).then_inc(s_xn, 1)
            for t in range(g * CH, (g + 1) * CH):
                dve.wait_ge(s_hi, t + 1)
                src = xp[:, t % 2, :].rearrange("p (k c) -> p k c", k=KT)
                cs = slice(t * P, (t + 1) * P)
                dve.tensor_tensor(xT_lo[:, :, cs], src, xT_hi[:, :, cs].bitcast(F32), ALU.subtract).then_inc(s_lo, 1)
            if g + 1 < NCH:
                dve_stats(dve, g + 1)

    def pe_all(pe):
        for t in range(NT):
            pe.wait_ge(s_xn, t + 1)
            if t >= 2:
                pe.wait_ge(s_lo, t - 1)
            for k in range(KT):
                last = pe.transpose(xp[:, t % 2, k * P:(k + 1) * P], xn[:, t % 2, k * P:(k + 1) * P], ident[:])
            last.then_inc(s_tr, 1)

    def done(eng):
        eng.wait_ge(s_lo, NT)

    return dict(load=load, act=act_all, dve=dve_all, pe=pe_all, done=done)


def three_pass(pe, out, a, b, first, last):
    pe.matmul(out, a[0], b[0], start=first, stop=False)
    pe.matmul(out, a[0], b[1], start=False, stop=False)
    return pe.matmul(out, a[1], b[0], start=False, stop=last)


def ffn_phase(nc, tag, at_selb, at, x_sb, ident, load_x, g_dram, wg, wu, wd):
    wg_v = wg.rearrange("a (k p) f -> p (a k) f", p=P)
    wu_v = wu.rearrange("a (k p) f -> p (a k) f", p=P)
    wd_v = wd.rearrange("a (n p) d -> p (a n) d", p=P)
    with ExitStack() as ctx:
        sem = lambda n: ctx.enter_context(nc.semaphore(f"{tag}_{n}"))
        keep = Plan(nc, tag, at)
        xT_hi = keep("xT_hi", [P, KT, ROWS], F32R)
        xT_lo = keep("xT_lo", [P, KT, ROWS], F32R)
        raw_g = keep("raw_g", [P, KT, FB], F32)
        raw_u = keep("raw_u", [P, KT, FB], F32)
        raw_d = Plan(nc, tag, at_selb)("raw_d", [P, 2, D], F32)
        sp_g = [[keep(f"g{'hl'[q]}{f}", [P, KT, P], F32R) for f in range(2)] for q in range(2)]
        sp_u = [[keep(f"u{'hl'[q]}{f}", [P, KT, P], F32R) for f in range(2)] for q in range(2)]
        sp_d = [keep(f"d{'hl'[q]}", [P, 2, D], F32R) for q in range(2)]
        s_x = [sem(f"x_loaded{t}") for t in range(NT)] if load_x else None
        with ExitStack() as over:
            pb = lambda n, s: over.enter_context(nc.psum_tensor(f"{tag}_{n}", s, F32))
            norm = add_norm(nc, Plan(nc, tag, keep.at), pb, sem, "n", x_sb, g_dram, xT_hi, xT_lo, ident,
                            (lambda e, t: e.wait_ge(s_x[t], 16)) if load_x else (lambda e, t: None))
        h_hi = keep("h_hi", [P, 2, ROWS], F32R)
        h_lo = keep("h_lo", [P, 2, ROWS], F32R)
        silu = keep("silu", [P, 2, CW], F32)
        pg = [ctx.enter_context(nc.psum_tensor(f"{tag}_pg{i}", [P, 512], F32)) for i in range(2)]
        pu = [ctx.enter_context(nc.psum_tensor(f"{tag}_pu{i}", [P, 512], F32)) for i in range(2)]
        py = [ctx.enter_context(nc.psum_tensor(f"{tag}_py{i}", [P, 512], F32)) for i in range(3)]

        s_rg, s_ru, s_rd = sem("gate_loaded"), sem("up_loaded"), sem("down_loaded")
        s_whi = sem("weights_hi")
        s_gu = sem("gate_up_split")
        s_dn = sem("down_split")
        s_gud = sem("gate_up_done")
        s_silu = sem("silu_ready")
        s_free = sem("gate_up_read")
        s_hf = sem("hidden_ready")
        s_hh = sem("hidden_hi")
        s_h = sem("hidden_split")
        s_y = sem("down_done")
        s_acc = sem("y_added")
        NY = NT * 2

        @(block := ctx.enter_context(nc.Block())).sync
        def _(sp):
            if load_x:
                load_x(sp, s_x)
            norm["load"](sp)
            for s, dst, src in ((s_rg, raw_g, wg_v[:, :, 0:FB]), (s_ru, raw_u, wu_v[:, :, 0:FB]),
                                (s_rd, raw_d, wd_v[:, 0:2, :])):
                sp.dma_start(dst[:], src).then_inc(s, 16)
            with sp.Fori(1, FSTEPS) as i:
                sp.wait_ge(s_gu, 2 * i)
                sp.dma_start(raw_g[:], wg_v[:, :, bass.ds(i * FB, FB)]).then_inc(s_rg, 16)
                sp.dma_start(raw_u[:], wu_v[:, :, bass.ds(i * FB, FB)]).then_inc(s_ru, 16)
                sp.wait_ge(s_dn, i)
                sp.dma_start(raw_d[:], wd_v[:, bass.ds(2 * i, 2), :]).then_inc(s_rd, 16)

        def act_gate_up_hi(act, j, f):
            fs = slice(f * P, (f + 1) * P)
            act.wait_ge(s_rg, 16 * j + 16)
            act.activation(sp_g[0][f][:], raw_g[:, :, fs], ACT.Copy).then_inc(s_whi, 1)
            act.wait_ge(s_ru, 16 * j + 16)
            act.activation(sp_u[0][f][:], raw_u[:, :, fs], ACT.Copy).then_inc(s_whi, 1)

        def act_down_hi(act, j):
            act.wait_ge(s_rd, 16 * j + 16)
            act.activation(sp_d[0][:], raw_d[:], ACT.Copy).then_inc(s_whi, 1)

        def act_silu(act, i, f):
            for c in range(NCH):
                k = NCH * f + c
                act.wait_ge(s_gud, 2 * NCH * i + k + 1)
                act.wait_ge(s_h, 2 * NCH * i + k + 1)
                act.activation(silu[:, k % 2, :], pg[k % 2][:, 0:CW], ACT.Silu).then_inc(s_silu, 1)

        def act_step(act, i, more):
            act_silu(act, i, 0)
            if more:
                act.wait_ge(s_gud, 2 * NCH * i + NCH)
                act_gate_up_hi(act, i + 1, 0)
            act_silu(act, i, 1)
            if more:
                act.wait_ge(s_gud, 2 * NCH * i + 2 * NCH)
                act_gate_up_hi(act, i + 1, 1)
                act.wait_ge(s_y, NY * i + 2 * NY)
                act_down_hi(act, i + 1)

        @block.scalar
        def _(act):
            norm["act"](act)
            act_gate_up_hi(act, 0, 0)
            act_gate_up_hi(act, 0, 1)
            act_down_hi(act, 0)
            with act.Fori(0, FSTEPS - 1) as i:
                act_step(act, i, True)
            act_step(act, FSTEPS - 1, False)

        def dve_gate_up_lo(dve, j, f):
            fs = slice(f * P, (f + 1) * P)
            dve.wait_ge(s_whi, 5 * j + 2 * f + 1)
            dve.tensor_tensor(sp_g[1][f][:], raw_g[:, :, fs], sp_g[0][f][:].bitcast(F32), ALU.subtract)
            dve.wait_ge(s_whi, 5 * j + 2 * f + 2)
            dve.tensor_tensor(sp_u[1][f][:], raw_u[:, :, fs], sp_u[0][f][:].bitcast(F32), ALU.subtract).then_inc(s_gu, 1)

        def dve_down_lo(dve, j):
            dve.wait_ge(s_whi, 5 * j + 5)
            dve.tensor_tensor(sp_d[1][:], raw_d[:], sp_d[0][:].bitcast(F32), ALU.subtract).then_inc(s_dn, 1)

        def dve_hidden(dve, i, f):
            for c in range(NCH):
                k = NCH * f + c
                n = 2 * NCH * i + k + 1
                cs = slice(c * CW, (c + 1) * CW)
                dve.wait_ge(s_silu, n)
                dve.tensor_tensor(silu[:, k % 2, :], silu[:, k % 2, :], pu[k % 2][:, 0:CW], ALU.mult).then_inc(s_free, 1)
                dve.wait_ge(s_y, NY * i + 2 * CH * (c + 1))
                dve.wait_ge(s_free, n + 2)
                dve.tensor_copy(h_hi[:, f, cs], silu[:, k % 2, :]).then_inc(s_hh, 1)
                dve.wait_ge(s_hh, n)
                dve.tensor_tensor(h_lo[:, f, cs], silu[:, k % 2, :], h_hi[:, f, cs].bitcast(F32), ALU.subtract).then_inc(s_h, 1)

        def dve_step(dve, i, more):
            dve_hidden(dve, i, 0)
            if more:
                dve_gate_up_lo(dve, i + 1, 0)
            dve_hidden(dve, i, 1)
            if more:
                dve_gate_up_lo(dve, i + 1, 1)
            for k in range(NY):
                t, half = k // 2, k % 2
                xs = x_sb[:, t, half * 512:(half + 1) * 512]
                dve.wait_ge(s_y, NY * i + NY + k + 1)
                dve.scalar_tensor_tensor(xs, py[k % 3][:], 0.5, xs, ALU.mult, ALU.add).then_inc(s_acc, 1)
            if more:
                dve_down_lo(dve, i + 1)

        @block.vector
        def _(dve):
            dve.sem_inc(s_free, 2)
            dve.sem_inc(s_h, 2)
            dve.sem_inc(s_acc, 3)
            norm["dve"](dve)
            dve_gate_up_lo(dve, 0, 0)
            dve_gate_up_lo(dve, 0, 1)
            dve_down_lo(dve, 0)
            with dve.Fori(0, FSTEPS - 1) as i:
                dve_step(dve, i, True)
            dve_step(dve, FSTEPS - 1, False)

        def pe_step(pe, i):
            for f in range(2):
                pe.wait_ge(s_gu, 2 * i + f + 1)
                for c in range(NCH):
                    k = NCH * f + c
                    cs = slice(c * CW, (c + 1) * CW)
                    pe.wait_ge(s_free, 2 * NCH * i + k + 1)
                    for w, out in ((sp_g, pg), (sp_u, pu)):
                        for kt in range(KT):
                            last = three_pass(pe, out[k % 2][:, 0:CW], (w[0][f][:, kt, :], w[1][f][:, kt, :]),
                                              (xT_hi[:, kt, cs], xT_lo[:, kt, cs]), kt == 0, kt == KT - 1)
                    last.then_inc(s_gud, 1)
            pe.wait_ge(s_dn, i + 1)
            for k in range(NY):
                t, half = k // 2, k % 2
                ts, hs = slice(t * P, (t + 1) * P), slice(half * 512, (half + 1) * 512)
                if k % (2 * CH) == 0:
                    pe.wait_ge(s_h, 2 * NCH * i + NCH + t // CH + 3)
                pe.wait_ge(s_acc, NY * i + k + 1)
                for f in range(2):
                    last = three_pass(pe, py[k % 3][:], (h_hi[:, f, ts], h_lo[:, f, ts]),
                                      (sp_d[0][:, f, hs], sp_d[1][:, f, hs]), f == 0, f == 1)
                last.then_inc(s_y, 1)

        @block.tensor
        def _(pe):
            pe.sem_inc(s_y, NY)
            norm["pe"](pe)
            norm["done"](pe)
            with pe.Fori(0, FSTEPS) as i:
                pe_step(pe, i)


WC = 256
NCHUNK = 2 * N_QKV // WC
IDX_AT = 2 * N_QKV
IC = 4 * ID
SELB_AT = [P * t * (t + 1) // 2 for t in range(NP + 1)]


def late_scores(nc, at):
    plan = Plan(nc, "r", at)
    acc = {NP - 1: plan("late_acc7", [P, SEQ], F32)}
    plan.at += 3 * BAND * 4
    acc[NP - 2] = plan("late_acc6", [P, SEQ - P], F32)
    return acc


def rel_rows(dve, rb, ur, s, n0):
    dve.tensor_copy(ur[:, 0:4 * P], rb[:, 2 * MAXREL:2 * MAXREL + 1].broadcast_to([H, 4 * P])).then_inc(s, 1)
    dve.wait_ge(s, n0 + 1)
    dve.tensor_copy(ur[:, 4 * P - 1:6 * P - 1], rb[:, 2 * MAXREL:0:-1]).then_inc(s, 1)
    dve.tensor_copy(ur[:, 6 * P - 1:6 * P], rb[:, 0:1]).then_inc(s, 1)


def wi_phase(nc, at_x, at, x_sb, ident, selb, late_acc, g_dram, w_in, rel_bias, urel, cos, sin, cache_idx, x_mid, proj, idx_p, idx_s):
    tag = "w"
    w_v = w_in.rearrange("a (k p) n -> p (a k) n", p=P)
    proj_v = proj.rearrange("(t p) n -> p t n", p=P)
    with ExitStack() as ctx:
        sem = lambda n: ctx.enter_context(nc.semaphore(f"{tag}_{n}"))
        keep = Plan(nc, tag, at)
        xT_hi = keep("xT_hi", [P, KT, ROWS], F32R)
        xT_lo = keep("xT_lo", [P, KT, ROWS], F32R)
        raw = keep("raw", [P, KT, N_IDX], F32)
        w_hi = [keep(f"w_hi{i}", [P, KT, w], F32R) for i, w in enumerate((N_IDX, WC))]
        w_lo = [keep(f"w_lo{i}", [P, KT, w], F32R) for i, w in enumerate((N_IDX, WC))]
        with ExitStack() as over:
            pb = lambda n, s: over.enter_context(nc.psum_tensor(f"{tag}_{n}", s, F32))
            beside = Plan(nc, tag, keep.at)
            norm = add_norm(nc, beside, pb, sem, "n", x_sb, g_dram, xT_hi, xT_lo, ident,
                            lambda e, t: None)
        rb = beside("rb", [H, 2 * MAXREL + 1], F32)
        ur = beside("ur", [H, 6 * P], F32)
        at_stage = keep.at
        stage = [keep(f"stage{i}", [P, NT, WC], F32) for i in range(2)]
        early = Plan(nc, tag, at_stage)
        rx_i = early("rx_i", [P, 2, NT * 9 * ID // 2], F32)
        early = Plan(nc, tag, at_stage)
        bdq = [early(f"bdq{g}", [P, IH, P], F32) for g in range(2)]
        early = Plan(nc, tag, at_stage + NT * WC * 4)
        spread = early("spread", [P, IH, DEC_B, ID], F32)
        kspread = early("kspread", [P, DEC_B, ID], F32)
        assert early.at <= keep.at
        idx = keep("idx", [P, NT, N_IDX], F32)
        cs_t = keep("cos", [P, NT, HD // 2], F32)
        sn_t = keep("sin", [P, NT, HD // 2], F32)
        rx = Plan(nc, tag, keep.at)("rx", [P, 2, NT * WC // 2], F32)
        kc = keep("kc", [P, PAST // P, DEC_B, ID], F32)
        kcT = [keep(f"kcT{g}", [P, KS], F32) for g in range(2)]
        ksum = keep("ksum", [P, 2, P], F32)
        ix = Plan(nc, tag, at_x)
        acc = [None, ix("acc1", [P, SEQ], F32)]
        gap = Plan(nc, tag, ix.at)
        ix = Plan(nc, tag, ix.at + 3 * BAND * 4)
        acc[0] = ix("acc0", [P, SEQ], F32)
        qi4 = gap("qi4", [P, IH, 4, ID], F32R)
        own = gap("own", [P, DEC_B], F32)
        m8 = gap("m8", [P, 3, 8], F32)
        acc_s = gap("acc_s", [P, KS + 4], F32)
        assert gap.at <= at_x + 4 * SEQ + 3 * BAND * 4
        kiT = ix("kiT", [P, SEQ], F32R)
        qiT = [ix(f"qiT{i}", [P, IH, P], F32R) for i in range(2)]
        ki4 = Plan(nc, tag, ix.at)("ki4", [P, NP, 4, ID], F32R)
        relu = ix("relu", [P, 2, SEQ], F32)
        assert ix.at <= at_x + NT * D * 4
        pw = [ctx.enter_context(nc.psum_tensor(f"{tag}_pw{i}", [P, 512], F32)) for i in range(3)]
        ps = [ctx.enter_context(nc.psum_tensor(f"{tag}_ps{i}", [P, D], F32)) for i in range(2)]

        s_raw, s_whi, s_wlo = sem("w_loaded"), sem("w_hi"), sem("w_split")
        s_grp, s_ev = sem("group_done"), sem("group_read")
        s_rot = sem("rope_step")
        s_rdy = [sem(f"stage_ready{i}") for i in range(2)]
        s_put = [sem(f"stage_stored{i}") for i in range(2)]
        s_xst = sem("x_stored")
        s_tab = sem("tables_loaded")
        s_kc = sem("cached_keys_loaded")
        s_iout = sem("idx_keys_stored")
        s_ich = sem("idx_step")
        s_rel, s_ur = sem("rel_bias_moved"), sem("ur_step")
        s_own = sem("own_mask")
        s_idx = sem("idx_rows_ready")
        s_pf, s_pd = sem("pair_filled"), sem("pair_read")
        s_rlf = sem("relu_read")
        s_q4 = sem("queries_expanded")
        s_sel = sem("selection_step")
        s_acc = sem("scores_step")

        TILES = list(range(TOPK // P, NP))
        PAIRS = [TILES[i:i + 2] for i in range(0, len(TILES), 2)]
        unit_of, n_units = {}, 0
        def take(key):
            nonlocal n_units
            unit_of[key] = n_units
            n_units += 1
        take("keys")
        for t in PAIRS[0]:
            take(("q", t))
            for h in range(IH):
                take((t, h))
        for key in ("bdq0", "bdq1", "kc", "kn"):
            take(key)
        for h in range(IH):
            take(("s", h))
        for t in PAIRS[1] + PAIRS[2]:
            take(("q", t))
            for h in range(IH):
                take((t, h))
        relu_of = {k: n for n, k in enumerate(k for k in sorted(unit_of, key=unit_of.get) if isinstance(k, tuple) and k[0] != "q")}
        tile_no = {t: n for n, t in enumerate(TILES)}
        def col(c):
            return (c - 1) * WC

        block = ctx.enter_context(nc.Block())

        @block.sync
        def _(sp):
            sp.dma_start(rb[:], rel_bias[0]).then_inc(s_rel, 16)
            norm["load"](sp)
            sp.dma_start(raw[:], w_v[:, :, IDX_AT:IDX_AT + N_IDX]).then_inc(s_raw, 16)
            sp.dma_start(cs_t[:], cos.rearrange("(t p) f -> p t f", p=P)).then_inc(s_tab, 16)
            sp.dma_start(sn_t[:], sin.rearrange("(t p) f -> p t f", p=P)).then_inc(s_tab, 16)
            sp.dma_start(x_mid.rearrange("(t p) d -> p t d", p=P), x_sb[:]).then_inc(s_xst, 16)
            sp.wait_ge(s_ur, 3)
            sp.dma_start(urel, ur[:]).then_inc(s_rel, 16)
            for kt in range(PAST // P):
                sp.dma_start(kc[:, kt, :, :], cache_idx[0].rearrange("b (k p) d -> p k b d", p=P)[:, kt]).then_inc(s_kc, 16)
            sp.wait_ge(s_wlo, 1)
            sp.dma_start(raw[:, :, 0:WC], w_v[:, :, 0:WC]).then_inc(s_raw, 16)
            sp.wait_ge(s_idx, 1)
            sp.dma_start(idx_p.rearrange("a b (t p) d -> p (a b t) d", p=P), idx[:, 0:NP, IH * ID:IH * ID + ID]).then_inc(s_iout, 16)
            sp.dma_start(idx_s.rearrange("a b s d -> (a b s) d"), idx[:, NP, IH * ID:IH * ID + ID]).then_inc(s_iout, 16)
            with sp.Fori(1, NCHUNK) as c:
                sp.wait_ge(s_wlo, c + 1)
                sp.dma_start(raw[:, :, 0:WC], w_v[:, :, bass.ds(c * WC, WC)]).then_inc(s_raw, 16)
            sp.wait_ge(s_iout, 32)
            sp.wait_ge(s_xst, 16)

        def act_hi(act, c, slot, w):
            act.wait_ge(s_raw, 16 * c + 16)
            if not (isinstance(c, int) and c < 2):
                act.wait_ge(s_grp, NT * c - NT)
            act.activation(w_hi[slot][:, :, 0:w], raw[:, :, 0:w], ACT.Copy).then_inc(s_whi, 1)

        def act_unit(act, key, dst, src_cols, func, scale):
            u = unit_of[key]
            act.wait_ge(s_pf, u + 1)
            act.activation(dst, ps[u % 2][:, 0:src_cols] if len(dst.shape) == 2 else
                           ps[u % 2][:, 0:src_cols].rearrange("p (h c) -> p h c", c=P), func, scale=scale).then_inc(s_pd, 1)

        def act_tile(act, t):
            n = tile_no[t]
            if n >= 2:
                act.wait_ge(s_pf, unit_of[(TILES[n - 2], IH - 1)] + 1)
            act_unit(act, ("q", t), qiT[n % 2][:], D, ACT.Copy, 1.0)
            for h in range(IH):
                r = relu_of[(t, h)]
                if r >= 2:
                    act.wait_ge(s_rlf, r - 1)
                act_unit(act, (t, h), relu[:, r % 2, 0:P * (t + 1)], P * (t + 1), ACT.Relu, 1.0 / 16)

        def act_evac(act, c, slot, k):
            if not (isinstance(k, int) and k == 0):
                act.wait_ge(s_put[slot], 16 * k)
            for t in range(NT):
                act.wait_ge(s_grp, NT * c + t + 1)
                act.activation(stage[slot][:, t, :], pw[t % 3][:, 0:WC], ACT.Copy).then_inc(s_ev, 1)

        def act_step(act, i, last=False):
            act_hi(act, 2 * i + 2, 0, WC)
            act_evac(act, 2 * i + 1, 1, i)
            if not last:
                act_hi(act, 2 * i + 3, 1, WC)
            act_evac(act, 2 * i + 2, 0, i)

        @block.scalar
        def _(act):
            norm["act"](act)
            act_hi(act, 0, 0, N_IDX)
            for t in range(NT):
                act.wait_ge(s_grp, t + 1)
                act.activation(idx[:, t, :], pw[t % 3][:, 0:N_IDX], ACT.Copy).then_inc(s_ev, 1)
            act_hi(act, 1, 1, WC)
            act_unit(act, "keys", kiT[:], SEQ, ACT.Copy, 1.0)
            for t in PAIRS[0]:
                act_tile(act, t)
            act_unit(act, "bdq0", bdq[0][:], D, ACT.Copy, 1.0)
            act_unit(act, "bdq1", bdq[1][:], D, ACT.Copy, 1.0)
            u = unit_of["kc"]
            act.wait_ge(s_pf, u + 1)
            for g in range(2):
                i = act.activation(kcT[g][:, 0:PAST], ps[u % 2][:, g * PAST:(g + 1) * PAST], ACT.Copy)
            i.then_inc(s_pd, 1)
            act_unit(act, "kn", ksum[:], 2 * P, ACT.Copy, 1.0)
            for h in range(IH):
                r = relu_of[("s", h)]
                act.wait_ge(s_rlf, r - 1)
                act_unit(act, ("s", h), relu[:, r % 2, 0:KS], KS, ACT.Relu, 1.0 / 16)
            with act.Fori(0, 2) as i:
                act_step(act, i)
            for t in PAIRS[1]:
                act_tile(act, t)
            with act.Fori(2, 4) as i:
                act_step(act, i)
            for t in PAIRS[2]:
                act_tile(act, t)
            act_step(act, 4)
            act_step(act, 5, True)

        def pool_lo(pool, c, slot, w):
            pool.wait_ge(s_whi, c + 1)
            pool.tensor_tensor(w_lo[slot][:, :, 0:w], raw[:, :, 0:w], w_hi[slot][:, :, 0:w].bitcast(F32), ALU.subtract).then_inc(s_wlo, 1)

        def rotate(eng, x, tmp, cosv, sinv, s, n0):
            half = x.shape[3] // 2
            x1, x2 = x[:, :, :, 0:half], x[:, :, :, half:2 * half]
            a, b = (tmp[:, q, 0:x.shape[1] * x.shape[2] * half].rearrange("p (t h f) -> p t h f", t=x.shape[1], h=x.shape[2]) for q in range(2))
            cb = cosv.unsqueeze(2).broadcast_to([P, x.shape[1], x.shape[2], half])
            sb_ = sinv.unsqueeze(2).broadcast_to([P, x.shape[1], x.shape[2], half])
            eng.tensor_tensor(a, x1, sb_, ALU.mult)
            eng.tensor_tensor(b, x2, sb_, ALU.mult).then_inc(s, 1)
            eng.wait_ge(s, n0 + 1)
            eng.tensor_tensor(x1, x1, cb, ALU.mult)
            eng.tensor_tensor(x2, x2, cb, ALU.mult).then_inc(s, 1)
            eng.wait_ge(s, n0 + 2)
            eng.tensor_tensor(x1, x1, b, ALU.subtract)
            return eng.tensor_tensor(x2, x2, a, ALU.add)

        def pool_chunk(pool, c, slot, k, rope, n_rope):
            pool.wait_ge(s_ev, NT * (c + 1))
            if rope:
                x = stage[slot][:].rearrange("p t (h f) -> p t h f", f=HD)
                rotate(pool, x, rx, cs_t[:], sn_t[:], s_rot, n_rope).then_inc(s_rdy[slot], 1)
                pool.wait_ge(s_rdy[slot], k)
            dst = proj_v[:, :, bass.ds((c - 1) * WC, WC)] if not isinstance(c, int) else proj_v[:, :, (c - 1) * WC:c * WC]
            pool.dma_start(dst, stage[slot][:]).then_inc(s_put[slot], 16)

        def pool_step(pool, i, rope=False, n=0, last=False):
            pool_lo(pool, 2 * i + 2, 0, WC)
            pool_chunk(pool, 2 * i + 1, 1, n + 1, rope, 4 * n)
            if not last:
                pool_lo(pool, 2 * i + 3, 1, WC)
            pool_chunk(pool, 2 * i + 2, 0, n + 1, rope, 4 * n + 2)

        @block.gpsimd
        def _(pool):
            pool.wait_ge(s_xst, 16)
            norm["done"](pool)
            pool.memset(own[:], 1.0).then_inc(s_own, 1)
            for n, (m, b0, st_) in enumerate(((1, 0, -DEC_S), (-1, DEC_S - 1, DEC_S))):
                pool.wait_ge(s_own, n + 1)
                pool.affine_select(out=own[:], in_=own[:], compare_op=ALU.is_ge, fill=0.0, base=b0,
                                   pattern=[[st_, DEC_B]], channel_multiplier=m).then_inc(s_own, 1)
            pool_lo(pool, 0, 0, N_IDX)
            pool_lo(pool, 1, 1, WC)
            pool.wait_ge(s_tab, 32)
            with pool.Fori(0, 2) as i:
                pool_step(pool, i)
            pool_step(pool, 2)
            pool_step(pool, 3, True, 0)
            pool_step(pool, 4, True, 1)
            pool_step(pool, 5, last=True)
            for i in range(2):
                pool.wait_ge(s_put[i], 16 * NCHUNK // 2)

        def dve_expand_q(dve, t):
            n = tile_no[t]
            q = idx[:, t, 0:IH * ID].rearrange("p (h f) -> p h f", f=ID)
            if n:
                dve.wait_ge(s_pf, unit_of[("q", TILES[n - 1])] + 1)
            dve.tensor_copy(qi4[:, :, 0, :], q).then_inc(s_ich, 1)
            dve.tensor_copy(qi4[:, :, 1, :], q).then_inc(s_ich, 1)
            dve.wait_ge(s_ich, 20 + 4 * n + 1)
            hi = qi4[:, :, 0, :].bitcast(F32)
            dve.tensor_tensor(qi4[:, :, 2, :], q, hi, ALU.subtract).then_inc(s_ich, 1)
            dve.tensor_tensor(qi4[:, :, 3, :], q, hi, ALU.subtract).then_inc(s_ich, 1)
            dve.wait_ge(s_ich, 20 + 4 * n + 4)
            dve.sem_inc(s_q4, 1)

        n_acc = [0]

        def dve_scores(dve, a, t_idx, keys, n):
            for h in range(IH):
                r = relu_of[(keys, h)]
                w = idx[:, t_idx, IH * ID + ID + h:IH * ID + ID + h + 1]
                dve.wait_ge(s_pd, relu_unit[r] + 1)
                if h == 0:
                    i = dve.tensor_scalar(a[:, 0:n], relu[:, r % 2, 0:n], w, None, ALU.mult)
                else:
                    dve.wait_ge(s_acc, n_acc[0])
                    i = dve.scalar_tensor_tensor(a[:, 0:n], relu[:, r % 2, 0:n], w, a[:, 0:n], ALU.mult, ALU.add)
                i.then_inc(s_acc, 1)
                n_acc[0] += 1
                dve.wait_ge(s_acc, n_acc[0])
                dve.sem_inc(s_rlf, 1)

        relu_unit = {relu_of[k]: unit_of[k] for k in relu_of}

        n_sel = [0]

        def dve_select(dve, parts, rounds):
            n = len(parts)
            base = n_sel[0]
            for i in range(rounds):
                for q, (a, w) in enumerate(parts):
                    if i:
                        dve.wait_ge(s_sel, base + 2 * n * i - n + q + 1)
                    dve.max(m8[:, q, :], a[:, 0:w]).then_inc(s_sel, 1)
                for q, (a, w) in enumerate(parts):
                    dve.wait_ge(s_sel, base + 2 * n * i + q + 1)
                    dve.match_replace(out=a[:, 0:w], in_to_replace=m8[:, q, :], in_values=a[:, 0:w], imm_value=GONE).then_inc(s_sel, 1)
            n_sel[0] = base + 2 * n * rounds
            dve.wait_ge(s_sel, n_sel[0])

        @block.vector
        def _(dve):
            dve.wait_ge(s_rel, 16)
            rel_rows(dve, rb, ur, s_ur, 0)
            norm["dve"](dve)
            dve.wait_ge(s_rel, 32)
            dve.wait_ge(s_xst, 16)
            dve.wait_ge(s_tab, 32)
            dve.wait_ge(s_ev, NT)
            x = idx[:, :, 0:9 * ID].rearrange("p t (h f) -> p t h f", f=ID)
            rotate(dve, x, rx_i, cs_t[:, :, 0:HD // 2:2], sn_t[:, :, 0:HD // 2:2], s_ich, 0).then_inc(s_ich, 1)
            dve.wait_ge(s_ich, 3)
            dve.sem_inc(s_idx, 1)
            k = idx[:, 0:NP, IH * ID:IH * ID + ID]
            dve.tensor_copy(ki4[:, :, 0, :], k).then_inc(s_ich, 1)
            dve.tensor_copy(ki4[:, :, 2, :], k).then_inc(s_ich, 1)
            dve.wait_ge(s_ich, 5)
            for q in (1, 3):
                dve.tensor_tensor(ki4[:, :, q, :], k, ki4[:, :, 0, :].bitcast(F32), ALU.subtract).then_inc(s_ich, 1)
            dve.wait_ge(s_own, 3)
            q = idx[:, NP, 0:IH * ID].rearrange("p (h f) -> p h f", f=ID)
            dve.tensor_tensor(spread[:].rearrange("p h b f -> p h (b f)").rearrange("p h (b f) -> p h b f", b=DEC_B),
                              q.unsqueeze(2).broadcast_to([P, IH, DEC_B, ID]),
                              own[:].unsqueeze(1).unsqueeze(3).broadcast_to([P, IH, DEC_B, ID]), ALU.mult).then_inc(s_ich, 1)
            dve.tensor_tensor(kspread[:], idx[:, NP, IH * ID:IH * ID + ID].unsqueeze(1).broadcast_to([P, DEC_B, ID]),
                              own[:].unsqueeze(2).broadcast_to([P, DEC_B, ID]), ALU.mult).then_inc(s_ich, 1)
            few = SELB_AT[TOPK // P]
            dve.memset(selb[:, 0:few], 0.0).then_inc(s_ich, 1)
            dve.wait_ge(s_ich, 10)
            for t in range(TOPK // P):
                e = SELB_AT[t + 1]
                dve.memset(selb[0:CHUNK, e - CHUNK:e], NEG).then_inc(s_ich, 1)
            for _ in range(20 - 12):
                dve.sem_inc(s_ich, 1)
            dve.wait_ge(s_ich, 20)
            for t in PAIRS[0]:
                dve_expand_q(dve, t)
            for q, t in enumerate(PAIRS[0]):
                dve_scores(dve, acc[q], t, t, P * (t + 1))
                dve.wait_ge(s_acc, n_acc[0])
                dve.memset(acc[q][0:CHUNK, P * (t + 1) - CHUNK:P * (t + 1)], UNSEEN).then_inc(s_acc, 1)
                n_acc[0] += 1
            dve.wait_ge(s_pd, unit_of["kn"] + 1)
            for g in range(2):
                dve.tensor_reduce(out=kcT[g][:, PAST:KS], in_=ksum[:, g, :].rearrange("p (b q) -> p q b", b=DEC_B),
                                  axis=AX.X, op=ALU.add).then_inc(s_own, 1)
            dve_expand_q(dve, PAIRS[1][0])
            dve_scores(dve, acc_s, NP, "s", KS)
            dve.memset(acc_s[:, KS:KS + 4], FIRST).then_inc(s_acc, 1)
            n_acc[0] += 1
            dve.wait_ge(s_acc, n_acc[0])
            dve_select(dve, [(acc[q], P * (t + 1)) for q, t in enumerate(PAIRS[0])], TOPK // 8)
            dve_select(dve, [(acc_s, KS + 4)], (SEL_S + 4) // 8)
            for q, t in enumerate(PAIRS[0]):
                dve.tensor_scalar(selb[:, SELB_AT[t]:SELB_AT[t] + P * (t + 1)], acc[q][:, 0:P * (t + 1)], GONE, NEG,
                                  ALU.not_equal, ALU.mult).then_inc(s_acc, 1)
                n_acc[0] += 1
            dve.tensor_scalar(selb[:, SELB_AT[NP]:SELB_AT[NP] + KS], acc_s[:, 0:KS], GONE, NEG, ALU.not_equal, ALU.mult).then_inc(s_acc, 1)
            n_acc[0] += 1
            for pair in PAIRS[1:]:
                a_of = [late_acc[t] for t in pair] if pair is PAIRS[-1] else acc
                for q, t in enumerate(pair):
                    if q or pair is PAIRS[2]:
                        dve_expand_q(dve, t)
                    dve.wait_ge(s_acc, n_acc[0])
                    dve_scores(dve, a_of[q], t, t, P * (t + 1))
                    dve.wait_ge(s_acc, n_acc[0])
                    dve.memset(a_of[q][0:CHUNK, P * (t + 1) - CHUNK:P * (t + 1)], UNSEEN).then_inc(s_acc, 1)
                    n_acc[0] += 1
                dve.wait_ge(s_acc, n_acc[0])
                if pair is PAIRS[-1]:
                    break
                dve_select(dve, [(acc[q], P * (t + 1)) for q, t in enumerate(pair)], TOPK // 8)
                for q, t in enumerate(pair):
                    dve.tensor_scalar(selb[:, SELB_AT[t]:SELB_AT[t] + P * (t + 1)], acc[q][:, 0:P * (t + 1)], GONE, NEG,
                                      ALU.not_equal, ALU.mult).then_inc(s_acc, 1)
                    n_acc[0] += 1

        def pe_chunk(pe, c, slot, w):
            pe.wait_ge(s_wlo, c + 1)
            for t in range(NT):
                if not (isinstance(c, int) and c == 0 and t < 3):
                    pe.wait_ge(s_ev, NT * c + t - 2)
                ts = slice(t * P, (t + 1) * P)
                for kt in range(KT):
                    last = three_pass(pe, pw[t % 3][:, 0:w], (xT_hi[:, kt, ts], xT_lo[:, kt, ts]),
                                      (w_hi[slot][:, kt, 0:w], w_lo[slot][:, kt, 0:w]), kt == 0, kt == KT - 1)
                last.then_inc(s_grp, 1)

        def pe_pair(pe, key):
            u = unit_of[key]
            if u >= 2:
                pe.wait_ge(s_pd, u - 1)
            return ps[u % 2]

        def pe_tile(pe, t):
            n = tile_no[t]
            out = pe_pair(pe, ("q", t))
            pe.wait_ge(s_q4, n + 1)
            for h in range(IH):
                last = pe.transpose(out[:, h * P:(h + 1) * P], qi4[:, h, :, :].rearrange("p c f -> p (c f)").bitcast(F32), ident[:])
            last.then_inc(s_pf, 1)
            for h in range(IH):
                out = pe_pair(pe, (t, h))
                if h == 0:
                    pe.wait_ge(s_pd, unit_of[("q", t)] + 1)
                for k0 in range(0, P * (t + 1), 512):
                    k1 = min(k0 + 512, P * (t + 1))
                    last = pe.matmul(out[:, k0:k1], qiT[n % 2][:, h, :], kiT[:, k0:k1], start=True, stop=True)
                last.then_inc(s_pf, 1)

        def pe_step(pe, i):
            pe_chunk(pe, 2 * i + 1, 1, WC)
            pe_chunk(pe, 2 * i + 2, 0, WC)

        @block.tensor
        def _(pe):
            norm["pe"](pe)
            norm["done"](pe)
            pe_chunk(pe, 0, 0, N_IDX)
            pe.wait_ge(s_ich, 7)
            out = pe_pair(pe, "keys")
            for t in range(NP):
                last = pe.transpose(out[:, t * P:(t + 1) * P], ki4[:, t, :, :].rearrange("p c f -> p (c f)").bitcast(F32), ident[:])
            last.then_inc(s_pf, 1)
            for t in PAIRS[0]:
                pe_tile(pe, t)
            pe.wait_ge(s_ich, 9)
            for g in range(2):
                out = pe_pair(pe, f"bdq{g}")
                for h in range(IH):
                    last = pe.transpose(out[:, h * P:(h + 1) * P],
                                        spread[:, h, 4 * g:4 * g + 4, :].rearrange("p b f -> p (b f)"), ident[:])
                last.then_inc(s_pf, 1)
            out = pe_pair(pe, "kc")
            pe.wait_ge(s_kc, 16 * PAST // P)
            for g in range(2):
                for kt in range(PAST // P):
                    last = pe.transpose(out[:, g * PAST + kt * P:g * PAST + (kt + 1) * P],
                                        kc[:, kt, 4 * g:4 * g + 4, :].rearrange("p b f -> p (b f)"), ident[:])
            last.then_inc(s_pf, 1)
            out = pe_pair(pe, "kn")
            for g in range(2):
                last = pe.transpose(out[:, g * P:(g + 1) * P],
                                    kspread[:, 4 * g:4 * g + 4, :].rearrange("p b f -> p (b f)"), ident[:])
            last.then_inc(s_pf, 1)
            pe.wait_ge(s_own, 5)
            for h in range(IH):
                out = pe_pair(pe, ("s", h))
                for k0, k1 in ((0, PAST), (PAST, KS)):
                    for g in range(2):
                        last = pe.matmul(out[:, k0:k1], bdq[g][:, h, :], kcT[g][:, k0:k1], start=g == 0, stop=g == 1)
                last.then_inc(s_pf, 1)
            with pe.Fori(0, 2) as i:
                pe_step(pe, i)
            for t in PAIRS[1]:
                pe_tile(pe, t)
            with pe.Fori(2, 4) as i:
                pe_step(pe, i)
            for t in PAIRS[2]:
                pe_tile(pe, t)
            with pe.Fori(4, 6) as i:
                pe_step(pe, i)

FAR = BAND - 2 * MAXREL
NEAR = BAND - FAR


def attn_plan():
    heads = [(x, t, h) for x in range(2) for t in range(NP) for h in range(H)]
    tiles = [(x, t) for x in range(2) for t in range(NP)]
    plan = [("prep", 0, 0), ("score", 0)]
    for g, (x, t, h) in enumerate(heads):
        n = tiles.index((x, t))
        if h == 4 and n + 1 < len(tiles):
            plan.append(("prep",) + tiles[n + 1])
        if g + 1 < len(heads):
            plan.append(("score", g + 1))
        plan.append(("turn", g))
        if g >= 1:
            plan.append(("value", g - 1))
        if h == 2 and n >= 1:
            plan.append(("out",) + tiles[n - 1])
    plan += [("value", len(heads) - 1), ("out",) + tiles[-1]]
    return heads, plan


def sample_plan(n):
    plan = [("keys", 0), ("score", 0)]
    for s in range(n):
        if s + 1 < n:
            plan += [("keys", s + 1), ("score", s + 1)]
        plan.append(("turn", s))
        if s >= 1:
            plan.append(("value", s - 1))
        if s >= 2:
            plan.append(("out", s - 2))
    return plan + [("value", n - 1), ("out", n - 2), ("out", n - 1)]


def blocks_of(x, t):
    first = max(0, t - LEFT // 2) if x == 0 else 0
    return first, t + 1 - first


def attn_phase(nc, at, ident, selb, acc, proj, urel, caches, oT_hi, oT_lo, outs):
    tag = "t"
    proj_v = proj.rearrange("(t p) n -> p t n", p=P)
    FW = H * HD
    with ExitStack() as ctx:
        sem = lambda n: ctx.enter_context(nc.semaphore(f"{tag}_{n}"))
        keep = Plan(nc, tag, at)
        keep.at += 4 * SEQ
        sc = keep("sc", [P, 3 * D], F32)
        m8 = keep("m8", [P, 8], F32)
        at_bias = keep.at
        bias = keep("bias", [P, H, BAND], F32)
        pT = keep("pT", [P, 2, D], F32)
        osb = keep("osb", [P, 2, FW], F32)
        small = keep("small", [P, 2, 8], F32)
        sums = keep("sums", [P, 2, H], F32)
        rec = keep("rec", [P, 2, H], F32)
        flip_s = keep("flip_s", [P, H, DEC_S], F32)
        at_big = keep.at
        rows = keep("rows", [P, 2, FW], F32)
        qT = keep("qT", [P, 2, H, P], F32)
        kT, v = [None, None], [None, None]
        kT[0], v[0] = keep("kT0", [P, HT, SEQ], F32), keep("v0", [P, NP, FW], F32)
        rel = Plan(nc, tag, keep.at)
        kT[1], v[1] = keep("kT1", [P, HT, SEQ], F32), keep("v1", [P, NP, FW], F32)
        raw = rel("raw", [P, H, NEAR], F32)
        flip = rel("flip", [P, P], F32)
        assert rel.at <= keep.at
        assert keep.at <= SBUF_END - 2 * KT * ROWS * 4
        smp = Plan(nc, tag, at_big)
        kc = [smp(f"kc{i}", [P, PAST // P, FW], F32) for i in range(2)]
        vc = [smp(f"vc{i}", [P, PAST // P, FW], F32) for i in range(2)]
        vn = [smp(f"vn{i}", [DEC_S, FW], F32) for i in range(2)]
        kTs = [smp(f"kTs{i}", [P, HT, KS], F32) for i in range(2)]
        bd = [smp(f"bd{i}", [P, 5 * P], F32) for i in range(2)]
        snT = smp("snT", [P, 2, 2, HT, P], F32)
        late = Plan(nc, tag, at_bias)
        srow = late("srow", [P, 2, 2, FW], F32)
        raw_s = late("raw_s", [P, KS - FAR], F32)
        bias_s = late("bias_s", [P, KS], F32)
        rep = late("rep", [P, DEC_B, H, DEC_S], BF16)
        assert late.at <= at_bias + H * BAND * 4
        assert smp.at <= keep.at
        ps = [ctx.enter_context(nc.psum_tensor(f"{tag}_ps{i}", [P, D], F32)) for i in range(2)]
        pt = [ctx.enter_context(nc.psum_tensor(f"{tag}_pt{i}", [P, 512], F32)) for i in range(2)]
        po = ctx.enter_context(nc.psum_tensor(f"{tag}_po", [P, 512], F32))
        pm = ctx.enter_context(nc.psum_tensor(f"{tag}_pm", [P, 512], F32))

        s_bias, s_far, s_sel = sem("bias_loaded"), sem("far_bias_ready"), sem("selection_step")
        s_flip, s_flipped = sem("flip_ready"), sem("bias_flipped")
        s_be = [sem("bias_read_dve"), sem("bias_read_act")]
        s_mask, s_rep, s_zero = sem("bias_masked"), sem("rep_ready"), sem("zeroed")
        s_row = sem("rows_loaded")
        s_v = [sem(f"v_loaded{i}") for i in range(2)]
        s_out = sem("outputs_stored")
        s_mf, s_ma, s_ml = sem("misc_filled"), sem("misc_read_act"), sem("misc_read_dve")
        s_s, s_mx, s_sc, s_p = sem("scores_done"), sem("max_ready"), sem("scores_ready"), sem("exp_ready")
        s_t = sem("turned")
        s_pt = [sem("turned_read_act"), sem("turned_read_dve")]
        s_o, s_rc, s_os = sem("value_done"), sem("reciprocal"), sem("out_scaled")
        s_kt = sem("new_keys_placed")
        s_bd = sem("block_queries")
        s_kc, s_vc = [sem(f"kc_loaded{i}") for i in range(2)], [sem(f"vc_loaded{i}") for i in range(2)]
        s_sr = sem("sample_rows_loaded")

        heads, plan = attn_plan()
        NH = len(heads)
        NTT = 2 * NP
        units, u0 = {}, 0
        for g, (x, t, h) in enumerate(heads):
            n = blocks_of(x, t)[1]
            units[g] = [(u0 + j, 4 * j, min(4, n - 4 * j)) for j in range(-(-n // 4))]
            u0 += len(units[g])
        items = [(x, b) for x in range(2) for b in range(DEC_B)]
        kunits, punits = {}, {}
        splan = [(e, s, items[s][0], items[s][1]) for e, s in sample_plan(len(items))]
        for e, s, _, _ in splan:
            if e in ("keys", "turn"):
                (kunits if e == "keys" else punits)[s] = list(range(u0, u0 + (HT if e == "keys" else 2)))
                u0 += HT if e == "keys" else 2
        misc, m0, lo_n = {}, 0, {}
        nlo = 0
        free_at = {}
        def use(key, by_dve):
            nonlocal m0, nlo
            misc[key] = m0
            m0 += 1
            nlo += by_dve
            lo_n[key] = nlo
        order = []
        for e in plan:
            if e[0] == "prep":
                order += [(("k",) + e[1:], 0), (("q",) + e[1:], 0)]
            elif e[0] == "out":
                order += [(("o",) + e[1:], 1)]
        order += [((("sk", "sq")[j], x), 0) for x in range(2) for j in range(2)]
        order += [(("so", s), 1) for s in range(len(items))]
        for key, by in order:
            use(key, by)
        keys_in_order = [k for k, _ in order]

        def sc_of(g, a, b):
            at = g % 3 * (BAND if g < NH // 2 else D)
            return sc[:, at + a:at + b]

        def pe_misc(pe, key):
            m = misc[key]
            if m:
                prev = keys_in_order[m - 1]
                pe.wait_ge(s_ma, m)
                if lo_n[prev]:
                    pe.wait_ge(s_ml, lo_n[prev])
            return pm

        block = ctx.enter_context(nc.Block())

        @block.sync
        def _(sp):
            tiles = [(x, t) for x in range(2) for t in range(NP)]

            def rows_of(n):
                x, t = tiles[n]
                if n:
                    sp.wait_ge(s_mf, misc[("q",) + tiles[n - 1]] + 1)
                c = x * N_QKV
                sp.dma_start(rows[:, 0, :], proj_v[:, t, c + FW:c + 2 * FW]).then_inc(s_row, 16)
                sp.dma_start(rows[:, 1, :], proj_v[:, t, c:c + FW]).then_inc(s_row, 16)

            def values(x):
                sp.dma_start(v[x][:], proj_v[:, 0:NP, x * N_QKV + 2 * FW:x * N_QKV + 3 * FW]).then_inc(s_v[x], 16)

            rows_of(0)
            u = urel
            sp.dma_start(raw[:], bass.AP(u.tensor, FAR, [[1, P], [6 * P, H], [1, NEAR]])).then_inc(s_bias, 16)
            values(0)
            rows_of(1)
            sp.wait_ge(s_flipped, 2)
            values(1)
            for n in range(2, len(tiles)):
                rows_of(n)
            for dst, c, r0, r1 in outs:
                sp.dma_start(dst, proj[r0:r1, c:c + FW]).then_inc(s_out, 16)
            sp.wait_ge(s_t, units[NH - 1][-1][0] + 1)
            sp.wait_ge(s_o, NH)
            for h in range(H):
                sp.dma_start(raw_s[h * DEC_S:(h + 1) * DEC_S, :],
                             bass.AP(u.tensor, 6 * P * h + FAR + P - DEC_S, [[1, DEC_S], [1, KS - FAR]])).then_inc(s_bias, 16)
            for x in range(2):
                for j in range(2):
                    sp.dma_start(srow[:, x, j, :], proj_v[:, NP, x * N_QKV + (1 - j) * FW:x * N_QKV + (2 - j) * FW]).then_inc(s_sr, 16)

            def cached_keys(s):
                x, b = items[s]
                if s >= 2:
                    sp.wait_ge(s_t, kunits[s - 2][-1] + 1)
                sp.dma_start(kc[s % 2][:], caches[x][0][0, b].rearrange("(k p) h d -> p k (h d)", p=P)).then_inc(s_kc[s % 2], 16)

            def cached_values(s):
                x, b = items[s]
                if s >= 2:
                    sp.wait_ge(s_o, NH + s - 1)
                sp.dma_start(vc[s % 2][:], caches[x][1][0, b].rearrange("(k p) h d -> p k (h d)", p=P)).then_inc(s_vc[s % 2], 16)
                r = SEQ + b * DEC_S
                sp.dma_start(vn[s % 2][:], proj[r:r + DEC_S, x * N_QKV + 2 * FW:x * N_QKV + 3 * FW]).then_inc(s_vc[s % 2], 16)

            cached_keys(0)
            for s in range(len(items)):
                if s + 1 < len(items):
                    cached_keys(s + 1)
                cached_values(s)
            sp.wait_ge(s_out, 16 * len(outs))

        @block.gpsimd
        def _(pool):
            pool.memset(flip[:], 0.0).then_inc(s_flip, 1)
            pool.memset(flip_s[:], 0.0).then_inc(s_flip, 1)
            pool.wait_ge(s_flip, 2)
            pool.affine_select(out=flip[:], in_=flip[:], compare_op=ALU.not_equal, fill=1.0, base=1 - P,
                               pattern=[[1, P]], channel_multiplier=1).then_inc(s_flip, 1)
            pool.affine_select(out=flip_s[:], in_=flip_s[:], compare_op=ALU.not_equal, fill=1.0, base=1 - DEC_S,
                               pattern=[[-DEC_S, H], [1, DEC_S]], channel_multiplier=1).then_inc(s_flip, 1)
            pool.memset(qT[:], 0.0).then_inc(s_zero, 1)
            for i in range(2):
                pool.wait_ge(s_be[i], 1)
            pool.tensor_copy(bias[:, :, 0:FAR], bias[:, :, FAR:FAR + 1].broadcast_to([P, H, FAR])).then_inc(s_far, 1)
            pool.wait_ge(s_far, 1)
            pool.memset(bias[CHUNK:P, :, 0:CHUNK], NEG).then_inc(s_far, 1)
            pool.wait_ge(s_o, NH)
            pool.wait_ge(s_mf, misc[("o", 1, NP - 1)] + 1)
            for i in range(2):
                pool.memset(bd[i][:], 0.0).then_inc(s_zero, 1)
            pool.memset(rep[:], 0.0).then_inc(s_rep, 1)
            pool.wait_ge(s_rep, 1)
            pool.affine_select(out=rep[:], in_=rep[:], compare_op=ALU.not_equal, fill=1.0, base=0,
                               pattern=[[-DEC_S, DEC_B], [0, H], [-1, DEC_S]], channel_multiplier=1).then_inc(s_rep, 1)
            for s, (x, b) in enumerate(items):
                bs = slice(b * DEC_S, (b + 1) * DEC_S)
                pool.wait_ge(s_ma, misc[("sq", x)] + 1)
                if s >= 2:
                    pool.wait_ge(s_s, NH + s - 1)
                else:
                    pool.wait_ge(s_zero, 3)
                bv = bd[s % 2][:].rearrange("p (f c) -> p f c", c=5 * DEC_S * 2)
                for j, (dst, src) in enumerate(((kTs[s % 2][:, :, PAST:KS], snT[:, x, 0, :, bs]),
                                                (bv[0:HD, :, 0:DEC_S], snT[0:HD, x, 1, :, bs]),
                                                (bv[HD:P, :, DEC_S:2 * DEC_S], snT[HD:P, x, 1, :, bs]))):
                    pool.tensor_copy(dst, src).then_inc(s_bd, 1)
                    pool.wait_ge(s_bd, 3 * s + j + 1)

        def diag(r):
            a = pm[r * HD:(r + 1) * HD, 0:DEC_S]
            return bass.AP(a.tensor, a.offset + r * DEC_S, [list(a.ap[0]), [P + 2 * DEC_S, HT], [1, DEC_S]])

        def dve_out(dve, key, n):
            dve.reciprocal(rec[:, n % 2, :], sums[:, n % 2, :]).then_inc(s_rc, 1)
            dve.wait_ge(s_rc, n + 1)
            if n >= 2:
                dve.wait_ge(s_mf, misc[("o",) + tiles_of[n - 2]] + 1)
            dve.tensor_tensor(osb[:, n % 2, :].rearrange("p (h d) -> p h d", d=HD), po[:].rearrange("p (h d) -> p h d", d=HD),
                              rec[:, n % 2, :].unsqueeze(2).broadcast_to([P, H, HD]), ALU.mult).then_inc(s_os, 1)

        tiles_of = [(x, t) for x in range(2) for t in range(NP)]

        @block.vector
        def _(dve):
            dve.wait_ge(s_flipped, 1)
            dve.tensor_copy(bias[:, 0:H // 2, FAR:BAND], ps[0][:].rearrange("p (h c) -> p h c", c=NEAR)).then_inc(s_be[0], 1)
            dve.wait_ge(s_be[0], 1)
            dve.wait_ge(s_be[1], 1)
            dve.memset(bias[0:CHUNK, :, BAND - CHUNK:BAND], NEG).then_inc(s_mask, 1)
            dve.wait_ge(s_mask, 1)

            n_sel = [0]
            halves = [(t, i, j) for t in (NP - 2, NP - 1) for i in range(TOPK // 8) for j in range(2)]

            def select_half():
                t, i, j = halves.pop(0)
                a = acc[t][:, 0:P * (t + 1)]
                if i or j:
                    dve.wait_ge(s_sel, n_sel[0])
                if j == 0:
                    dve.max(m8[:], a).then_inc(s_sel, 1)
                else:
                    dve.match_replace(out=a, in_to_replace=m8[:], in_values=a, imm_value=GONE).then_inc(s_sel, 1)
                n_sel[0] += 1
                if (i, j) == (TOPK // 8 - 1, 1):
                    dve.wait_ge(s_sel, n_sel[0])
                    dve.tensor_scalar(selb[:, SELB_AT[t]:SELB_AT[t + 1]], a, GONE, NEG, ALU.not_equal, ALU.mult).then_inc(s_sel, 1)
                    n_sel[0] += 1

            todo = sum(blocks_of(x, t)[1] for x, t, h in heads[:heads.index((1, NP - 2, 0))])
            done, n_halves = 0, len(halves)
            for e in plan:
                if e[0] == "score":
                    g = e[1]
                    x, t, h = heads[g]
                    n = P * blocks_of(x, t)[1]
                    done += n // P
                    if halves and (n_halves - len(halves)) * todo <= n_halves * (done - n // P):
                        select_half()
                    if (x, t, h) == (1, 0, 0):
                        assert halves[0][0] == NP - 1
                        dve.wait_ge(s_sel, n_sel[0])
                    if (x, t, h) == (1, NP - 2, 0):
                        assert not halves
                        dve.wait_ge(s_sel, n_sel[0])
                    if (x, t, h) == (0, 2, 0):
                        dve.wait_ge(s_far, 2)
                    dve.wait_ge(s_s, g + 1)
                    if g >= 3:
                        dve.wait_ge(s_t, units[g - 2 if (x, t, h) == (1, 0, 0) else g - 3][-1][0] + 1)
                    if g >= 4:
                        dve.wait_ge(s_p, g - 3)
                    b = bias[:, h, BAND - n:BAND] if x == 0 else selb[:, SELB_AT[t]:SELB_AT[t] + n]
                    dve.tensor_tensor_reduce(out=sc_of(g, 0, n), in0=ps[g % 2][:, 0:n], in1=b, scale=1.0, scalar=GONE,
                                             op0=ALU.add, op1=ALU.max, accum_out=small[:, 0, g % 4:g % 4 + 1]).then_inc(s_mx, 1)
                    dve.wait_ge(s_mx, g + 1)
                    dve.tensor_scalar(small[:, 1, g % 4:g % 4 + 1], small[:, 0, g % 4:g % 4 + 1], -1.0, None, ALU.mult).then_inc(s_sc, 1)
                elif e[0] == "turn":
                    while halves and (n_halves - len(halves)) * todo <= n_halves * (done - 2):
                        select_half()
                    for u, b0, nb in units[e[1]]:
                        if u % 2:
                            dve.wait_ge(s_t, u + 1)
                            if e[1] >= 2:
                                dve.wait_ge(s_o, e[1] - 1)
                            dve.tensor_copy(pT[:, e[1] % 2, b0 * P:(b0 + nb) * P], pt[1][:, 0:nb * P]).then_inc(s_pt[1], 1)
                elif e[0] == "value" and heads[e[1]][2] == H - 1:
                    n = e[1] // H
                    dve.wait_ge(s_o, e[1] + 1)
                    dve_out(dve, None, n)
                elif e[0] == "out":
                    m = misc[("o",) + e[1:]]
                    ts = slice(e[2] * P, (e[2] + 1) * P)
                    dve.wait_ge(s_ma, m + 1)
                    fs = slice(e[1] * HT, (e[1] + 1) * HT)
                    dve.tensor_tensor(oT_lo[:, fs, ts], pm[:].rearrange("p (f c) -> p f c", c=P),
                                      oT_hi[:, fs, ts].bitcast(F32), ALU.subtract).then_inc(s_ml, 1)
            dve.wait_ge(s_flipped, 3)
            dve.tensor_copy(bias_s[:, FAR:KS], ps[0][:, 0:KS - FAR]).then_inc(s_be[0], 1)
            dve.wait_ge(s_be[0], 2)
            dve.tensor_copy(bias_s[:, 0:FAR], bias_s[:, FAR:FAR + 1].broadcast_to([P, FAR])).then_inc(s_mask, 1)
            dve.wait_ge(s_mask, 2)
            for e, s, x, b in splan:
                g, n = NH + s, NTT + s
                if e == "keys":
                    for f, u in enumerate(kunits[s]):
                        if u % 2:
                            dve.wait_ge(s_t, u + 1)
                            dve.tensor_copy(kTs[s % 2][:, f, 0:PAST], pt[1][:]).then_inc(s_pt[1], 1)
                elif e == "score":
                    dve.wait_ge(s_s, g + 1)
                    if x == 0:
                        dve.wait_ge(s_t, (units[NH - 3 + s][-1][0] if s < 3 else punits[s - 3][-1]) + 1)
                        dve.tensor_tensor_reduce(out=sc_of(g, 0, KS), in0=ps[g % 2][:, 0:KS], in1=bias_s[:], scale=1.0, scalar=GONE,
                                                 op0=ALU.add, op1=ALU.max, accum_out=small[:, 0, g % 4:g % 4 + 1]).then_inc(s_mx, 1)
                    else:
                        dve.tensor_reduce(out=small[:, 0, g % 4:g % 4 + 1], in_=ps[g % 2][:, 0:KS], axis=AX.X, op=ALU.max).then_inc(s_mx, 1)
                    dve.wait_ge(s_mx, g + 1)
                    dve.tensor_scalar(small[:, 1, g % 4:g % 4 + 1], small[:, 0, g % 4:g % 4 + 1], -1.0, None, ALU.mult).then_inc(s_sc, 1)
                elif e == "turn":
                    for j, u in enumerate(punits[s]):
                        if u % 2:
                            dve.wait_ge(s_t, u + 1)
                            dve.wait_ge(s_o, g - 1)
                            if j == 0:
                                dve.tensor_copy(pT[:, s % 2, 0:PAST], pt[1][:]).then_inc(s_pt[1], 1)
                            else:
                                dve.tensor_copy(pT[0:DEC_S, s % 2, PAST:PAST + P], pt[1][0:DEC_S, 0:P]).then_inc(s_pt[1], 1)
                elif e == "value":
                    dve.wait_ge(s_o, g + 1)
                    dve.reciprocal(rec[:, n % 2, 0:1], sums[:, 0, s % H:s % H + 1]).then_inc(s_rc, 1)
                    dve.wait_ge(s_rc, n + 1)
                    if s >= 2:
                        dve.wait_ge(s_mf, misc[("so", s - 2)] + 1)
                    dve.tensor_scalar(osb[:, n % 2, :], po[:], rec[:, n % 2, 0:1], None, ALU.mult).then_inc(s_os, 1)
                else:
                    m = misc[("so", s)]
                    dve.wait_ge(s_ma, m + 1)
                    cs = slice(SEQ + b * DEC_S, SEQ + (b + 1) * DEC_S)
                    fs = slice(x * HT, (x + 1) * HT)
                    for r in range(2):
                        i = dve.tensor_tensor(oT_lo[r * HD:(r + 1) * HD, fs, cs], diag(r),
                                              oT_hi[r * HD:(r + 1) * HD, fs, cs].bitcast(F32), ALU.subtract)
                    i.then_inc(s_ml, 1)

        def act_exp(act, g, n, src, total):
            act.wait_ge(s_sc, g + 1)
            act.activation(sc_of(g, 0, n), src, ACT.Exp, bias=small[:, 1, g % 4:g % 4 + 1], accum_out=total).then_inc(s_p, 1)

        @block.scalar
        def _(act):
            act.wait_ge(s_zero, 1)
            for e in plan:
                if e[0] == "prep":
                    x, t = e[1:]
                    n = x * NP + t
                    act.wait_ge(s_mf, misc[("k", x, t)] + 1)
                    act.activation(kT[x][:, :, t * P:(t + 1) * P], pm[:].rearrange("p (f c) -> p f c", c=P), ACT.Copy).then_inc(s_ma, 1)
                    act.wait_ge(s_mf, misc[("q", x, t)] + 1)
                    if n >= 2:
                        act.wait_ge(s_s, (n - 1) * H)
                    for r in range(2):
                        i = act.activation(qT[r * HD:(r + 1) * HD, n % 2, r::2, :],
                                           pm[r * HD:(r + 1) * HD, :].rearrange("p (f c) -> p f c", c=P), ACT.Copy, scale=HD ** -0.5)
                    i.then_inc(s_ma, 1)
                    if n == 0:
                        act.wait_ge(s_flipped, 2)
                        act.activation(bias[:, H // 2:H, FAR:BAND], ps[1][:].rearrange("p (h c) -> p h c", c=NEAR), ACT.Copy).then_inc(s_be[1], 1)
                elif e[0] == "score":
                    g = e[1]
                    x, t, h = heads[g]
                    n = P * blocks_of(x, t)[1]
                    if h == 0 and g >= 2 * H:
                        act.wait_ge(s_rc, g // H - 1)
                    act_exp(act, g, n, sc_of(g, 0, n), sums[:, (g // H) % 2, h:h + 1])
                elif e[0] == "turn":
                    for u, b0, nb in units[e[1]]:
                        if u % 2 == 0:
                            act.wait_ge(s_t, u + 1)
                            if e[1] >= 2:
                                act.wait_ge(s_o, e[1] - 1)
                            act.activation(pT[:, e[1] % 2, b0 * P:(b0 + nb) * P], pt[0][:, 0:nb * P], ACT.Copy).then_inc(s_pt[0], 1)
                elif e[0] == "out":
                    m = misc[("o",) + e[1:]]
                    act.wait_ge(s_mf, m + 1)
                    act.activation(oT_hi[:, e[1] * HT:(e[1] + 1) * HT, e[2] * P:(e[2] + 1) * P],
                                   pm[:].rearrange("p (f c) -> p f c", c=P), ACT.Copy).then_inc(s_ma, 1)
            for x in range(2):
                for j in range(2):
                    act.wait_ge(s_mf, misc[(("sk", "sq")[j], x)] + 1)
                    act.activation(snT[:, x, j, :, :], pm[:].rearrange("p (f c) -> p f c", c=P), ACT.Copy,
                                   scale=HD ** -0.5 if j else 1.0).then_inc(s_ma, 1)
            act.wait_ge(s_rc, NTT)
            for e, s, x, b in splan:
                g = NH + s
                if e == "keys":
                    for f, u in enumerate(kunits[s]):
                        if u % 2 == 0:
                            act.wait_ge(s_t, u + 1)
                            act.activation(kTs[s % 2][:, f, 0:PAST], pt[0][:], ACT.Copy).then_inc(s_pt[0], 1)
                elif e == "score":
                    if s >= H:
                        act.wait_ge(s_rc, NTT + s - H + 1)
                    if x == 1:
                        act.wait_ge(s_t, punits[s - 3][-1] + 1)
                    act_exp(act, g, KS, sc_of(g, 0, KS) if x == 0 else ps[g % 2][:, 0:KS], sums[:, 0, s % H:s % H + 1])
                elif e == "turn":
                    for j, u in enumerate(punits[s]):
                        if u % 2 == 0:
                            act.wait_ge(s_t, u + 1)
                            act.wait_ge(s_o, g - 1)
                            if j == 0:
                                act.activation(pT[:, s % 2, 0:PAST], pt[0][:], ACT.Copy).then_inc(s_pt[0], 1)
                            else:
                                act.activation(pT[0:DEC_S, s % 2, PAST:PAST + P], pt[0][0:DEC_S, 0:P], ACT.Copy).then_inc(s_pt[0], 1)
                elif e == "out":
                    act.wait_ge(s_mf, misc[("so", s)] + 1)
                    cs = slice(SEQ + b * DEC_S, SEQ + (b + 1) * DEC_S)
                    for r in range(2):
                        i = act.activation(oT_hi[r * HD:(r + 1) * HD, x * HT:(x + 1) * HT, cs], diag(r), ACT.Copy)
                    i.then_inc(s_ma, 1)

        def evacs(u):
            return u // 2 + 1

        def pe_turn(pe, u, blocks):
            if u >= 2:
                pe.wait_ge(s_pt[u % 2], evacs(u - 2))
            for dst, src in blocks:
                last = pe.transpose(dst, src, ident[:])
            last.then_inc(s_t, 1)

        def pe_rows(pe, key, src):
            out = pe_misc(pe, key)
            for f in range(HT):
                last = pe.transpose(out[:, f * P:(f + 1) * P], src[:, f * P:(f + 1) * P], ident[:])
            last.then_inc(s_mf, 1)

        @block.tensor
        def _(pe):
            for e in plan:
                if e[0] == "prep":
                    x, t = e[1:]
                    n = x * NP + t
                    pe.wait_ge(s_row, 32 * (n + 1))
                    pe_rows(pe, ("k", x, t), rows[:, 0, :])
                    pe_rows(pe, ("q", x, t), rows[:, 1, :])
                    if n == 0:
                        pe.wait_ge(s_bias, 16)
                        pe.wait_ge(s_flip, 4)
                        for i in range(2):
                            for j in range(2):
                                h2 = 4 * i + 2 * j
                                last = pe.matmul(ps[i][:, j * 512:(j + 1) * 512], flip[:],
                                                 raw[:, h2:h2 + 2, :].rearrange("p h c -> p (h c)"), start=True, stop=True)
                            last.then_inc(s_flipped, 1)
                        for i in range(2):
                            pe.wait_ge(s_be[i], 1)
                elif e[0] == "score":
                    g = e[1]
                    x, t, h = heads[g]
                    k0, nb = blocks_of(x, t)
                    if h == 0:
                        pe.wait_ge(s_ma, misc[("q", x, t)] + 1)
                    if g >= 2:
                        pe.wait_ge(s_mx, g - 1)
                    for c in range(0, nb, 4):
                        c1 = min(c + 4, nb)
                        last = pe.matmul(ps[g % 2][:, c * P:c1 * P], qT[:, (x * NP + t) % 2, h, :],
                                         kT[x][:, h // 2, (k0 + c) * P:(k0 + c1) * P], start=True, stop=True)
                    last.then_inc(s_s, 1)
                elif e[0] == "turn":
                    g = e[1]
                    pe.wait_ge(s_p, g + 1)
                    for u, b0, nb in units[g]:
                        pe_turn(pe, u, [(pt[u % 2][:, j * P:(j + 1) * P], sc_of(g, (b0 + j) * P, (b0 + j + 1) * P)) for j in range(nb)])
                elif e[0] == "value":
                    g = e[1]
                    x, t, h = heads[g]
                    k0, nb = blocks_of(x, t)
                    if t == 0 and h == 0:
                        pe.wait_ge(s_v[x], 16)
                    if h == 0 and g:
                        pe.wait_ge(s_os, g // H)
                    for u, _, _ in units[g]:
                        pe.wait_ge(s_pt[u % 2], evacs(u))
                    for j in range(nb):
                        last = pe.matmul(po[:, h * HD:(h + 1) * HD], pT[:, g % 2, j * P:(j + 1) * P],
                                         v[x][:, k0 + j, h * HD:(h + 1) * HD], start=j == 0, stop=j == nb - 1)
                    last.then_inc(s_o, 1)
                elif e[0] == "out":
                    n = e[1] * NP + e[2]
                    pe.wait_ge(s_os, n + 1)
                    pe_rows(pe, ("o",) + e[1:], osb[:, n % 2, :])
            pe.wait_ge(s_bias, 16 * (H + 1))
            pe.wait_ge(s_mx, NH)
            pe.matmul(ps[0][:, 0:KS - FAR], flip_s[:].rearrange("p h q -> p (h q)"), raw_s[:], start=True, stop=True).then_inc(s_flipped, 1)
            pe.wait_ge(s_be[0], 2)
            pe.wait_ge(s_sr, 64)
            for x in range(2):
                for j in range(2):
                    pe_rows(pe, (("sk", "sq")[j], x), srow[:, x, j, :])

            for e, s, x, b in splan:
                g = NH + s
                if e == "keys":
                    pe.wait_ge(s_kc[s % 2], 16 * (s // 2 + 1))
                    for f, u in enumerate(kunits[s]):
                        pe_turn(pe, u, [(pt[u % 2][:, k * P:(k + 1) * P], kc[s % 2][:, k, f * P:(f + 1) * P]) for k in range(PAST // P)])
                elif e == "score":
                    pe.wait_ge(s_bd, 3 * s + 3)
                    for u in kunits[s][-2:]:
                        pe.wait_ge(s_pt[u % 2], evacs(u))
                    pe.wait_ge(s_mx, g - 1)
                    if x == 1:
                        pe.wait_ge(s_p, g - 1)
                        if b == 0:
                            pe.wait_ge(s_rep, 2)
                    for c0, c1 in ((0, PAST), (PAST, KS)):
                        for f in range(HT):
                            last = pe.matmul(ps[g % 2][:, c0:c1], bd[s % 2][:, f * P:(f + 1) * P], kTs[s % 2][:, f, c0:c1],
                                             start=f == 0, stop=f == HT - 1 and x == 0)
                        if x == 1:
                            last = pe.matmul(ps[g % 2][:, c0:c1], rep[:, b, :, :].rearrange("p h q -> p (h q)"),
                                             selb[:, SELB_AT[NP] + c0:SELB_AT[NP] + c1], start=False, stop=True)
                    last.then_inc(s_s, 1)
                elif e == "turn":
                    pe.wait_ge(s_p, g + 1)
                    u = punits[s][0]
                    pe_turn(pe, u, [(pt[u % 2][:, k * P:(k + 1) * P], sc_of(g, k * P, (k + 1) * P)) for k in range(PAST // P)])
                    u = punits[s][1]
                    pe_turn(pe, u, [(pt[u % 2][0:DEC_S, 0:P], sc_of(g, PAST, KS))])
                elif e == "value":
                    pe.wait_ge(s_os, NTT + s)
                    pe.wait_ge(s_vc[s % 2], 32 * (s // 2 + 1))
                    for u in punits[s]:
                        pe.wait_ge(s_pt[u % 2], evacs(u))
                    for k in range(PAST // P):
                        pe.matmul(po[:], pT[:, s % 2, k * P:(k + 1) * P], vc[s % 2][:, k, :], start=k == 0, stop=False)
                    pe.matmul(po[:], pT[0:DEC_S, s % 2, PAST:PAST + P], vn[s % 2][:], start=False, stop=True).then_inc(s_o, 1)
                else:
                    pe.wait_ge(s_os, NTT + s + 1)
                    pe_rows(pe, ("so", s), osb[:, (NTT + s) % 2, :])

def wo_phase(nc, at, x_sb, x_mid, w_out, oT_hi, oT_lo):
    tag = "o"
    w_v = w_out.rearrange("a (k p) n -> p (a k) n", p=P)
    with ExitStack() as ctx:
        sem = lambda n: ctx.enter_context(nc.semaphore(f"{tag}_{n}"))
        keep = Plan(nc, tag, at)
        raw = keep("raw", [P, KT, 512], F32)
        w_hi = [keep(f"w_hi{i}", [P, KT, 512], F32R) for i in range(2)]
        w_lo = [keep(f"w_lo{i}", [P, KT, 512], F32R) for i in range(2)]
        assert keep.at <= SBUF_END - 2 * KT * ROWS * 4
        py = [ctx.enter_context(nc.psum_tensor(f"{tag}_py{i}", [P, 512], F32)) for i in range(4)]
        s_raw, s_hi, s_lo, s_y, s_acc = sem("w_loaded"), sem("w_hi"), sem("w_split"), sem("y_done"), sem("y_added")
        s_x = sem("x_loaded")
        block = ctx.enter_context(nc.Block())

        @block.sync
        def _(sp):
            for n in range(2):
                if n:
                    sp.wait_ge(s_lo, KT)
                for k in range(0, KT, 2):
                    sp.dma_start(raw[:, k:k + 2, :], w_v[:, k:k + 2, n * 512:(n + 1) * 512]).then_inc(s_raw, 16)
                    if k == 0 and n == 0:
                        sp.dma_start(x_sb[:], x_mid.rearrange("(t p) d -> p t d", p=P)).then_inc(s_x, 16)

        @block.scalar
        def _(act):
            for n in range(2):
                for k in range(KT):
                    act.wait_ge(s_raw, 16 * (4 * n + 4 if n == 0 else 8))
                    act.activation(w_hi[n][:, k, :], raw[:, k, :], ACT.Copy).then_inc(s_hi, 1)

        @block.vector
        def _(dve):
            def lo(n):
                for k in range(KT):
                    dve.wait_ge(s_hi, KT * n + k + 1)
                    dve.tensor_tensor(w_lo[n][:, k, :], raw[:, k, :], w_hi[n][:, k, :].bitcast(F32), ALU.subtract).then_inc(s_lo, 1)

            lo(0)
            dve.wait_ge(s_x, 16)
            for k in range(2 * NT):
                n, t = k // NT, k % NT
                if k == 2:
                    lo(1)
                xs = x_sb[:, t, n * 512:(n + 1) * 512]
                dve.wait_ge(s_y, k + 1)
                dve.tensor_tensor(xs, py[k % 4][:], xs, ALU.add).then_inc(s_acc, 1)

        @block.tensor
        def _(pe):
            for k in range(2 * NT):
                n, t = k // NT, k % NT
                if k >= 4:
                    pe.wait_ge(s_acc, k - 3)
                ts = slice(t * P, (t + 1) * P)
                for kt in range(KT):
                    if t == 0:
                        pe.wait_ge(s_lo, KT * n + kt + 1)
                    last = three_pass(pe, py[k % 4][:], (oT_hi[:, kt, ts], oT_lo[:, kt, ts]),
                                      (w_hi[n][:, kt, :], w_lo[n][:, kt, :]), kt == 0, kt == KT - 1)
                last.then_inc(s_y, 1)


def final_phase(nc, at, x_sb, g_dram, y_p, y_s):
    tag = "f"
    with ExitStack() as ctx:
        sem = lambda n: ctx.enter_context(nc.semaphore(f"{tag}_{n}"))
        keep = Plan(nc, tag, at)
        y = keep("y", [P, NT, D], F32)
        g_bc = keep("g", [P, D], F32)
        st = keep("st", [P, 6, NT], F32)
        SS, V, SD, R, A, B = range(6)
        junk = ctx.enter_context(nc.psum_tensor(f"{tag}_junk", [P, 2, D], F32))
        s_g, s_ss, s_v, s_sd, s_ch, s_y, s_out = (sem(n) for n in ("g_loaded", "squares_summed", "mean_ready", "root_ready",
                                                                 "newton_step", "row_normed", "stored"))
        cols = lambda k, g: st[:, k, g * CH:(g + 1) * CH]
        block = ctx.enter_context(nc.Block())

        @block.sync
        def _(sp):
            sp.dma_start(g_bc[:], g_dram.partition_broadcast(P)).then_inc(s_g, 16)
            for t in range(NT):
                sp.wait_ge(s_y, t + 1)
                dst = y_p[t * P:(t + 1) * P, :] if t < NP else y_s
                sp.dma_start(dst, y[:, t, :]).then_inc(s_out, 16)
            sp.wait_ge(s_out, 16 * NT)

        @block.scalar
        def _(act):
            for g in range(NCH):
                for t in range(g * CH, (g + 1) * CH):
                    if t >= 2:
                        act.wait_ge(s_ss, t - 1)
                    act.activation(junk[:, t % 2, :], x_sb[:, t, :], ACT.Square, accum_out=st[:, SS, t:t + 1]).then_inc(s_ss, 1)
                act.wait_ge(s_v, 2 * g + 1)
                act.activation(cols(SD, g), cols(V, g), ACT.Sqrt).then_inc(s_sd, 1)

        @block.vector
        def _(dve):
            dve.wait_ge(s_g, 16)
            for g in range(NCH):
                n = 4 * g
                dve.wait_ge(s_ss, CH * (g + 1))
                dve.tensor_scalar(cols(V, g), cols(SS, g), 1.0 / D, EPS, ALU.mult, ALU.add).then_inc(s_v, 1)
                dve.wait_ge(s_sd, g + 1)
                dve.reciprocal(cols(R, g), cols(SD, g)).then_inc(s_ch, 1)
                dve.wait_ge(s_ch, n + 1)
                dve.tensor_tensor(cols(A, g), cols(R, g), cols(R, g), ALU.mult).then_inc(s_ch, 1)
                dve.wait_ge(s_ch, n + 2)
                dve.tensor_tensor(cols(B, g), cols(A, g), cols(V, g), ALU.mult).then_inc(s_ch, 1)
                dve.wait_ge(s_ch, n + 3)
                dve.tensor_scalar(cols(A, g), cols(B, g), -0.5, 1.5, ALU.mult, ALU.add).then_inc(s_ch, 1)
                dve.wait_ge(s_ch, n + 4)
                dve.tensor_tensor(cols(SS, g), cols(R, g), cols(A, g), ALU.mult).then_inc(s_v, 1)
                dve.wait_ge(s_v, 2 * g + 2)
                for t in range(g * CH, (g + 1) * CH):
                    dve.scalar_tensor_tensor(y[:, t, :], x_sb[:, t, :], st[:, SS, t:t + 1], g_bc[:], ALU.mult, ALU.mult).then_inc(s_y, 1)


def program(nc, i, o):
    plan = Plan(nc, "r", SBUF_START)
    ident = plan("ident", [P, P], F32)
    at_selb = plan.at
    selb = plan("selb", [P, SELB_AT[NP] + KS], BF16)
    at_x = plan.at
    x_sb = plan("x", [P, NT, D], F32)
    at = plan.at
    late_acc = late_scores(nc, at_x)
    top = Plan(nc, "r", SBUF_END - 2 * KT * ROWS * 4)
    oT_hi = top("oT_hi", [P, KT, ROWS], F32R)
    oT_lo = top("oT_lo", [P, KT, ROWS], F32R)
    dram = lambda n, s: nc.dram_tensor(n, s, F32, kind="Internal").ap()
    x_mid, proj, urel = dram("x_mid", [ROWS, D]), dram("proj", [ROWS, 2 * N_QKV]), dram("urel", [H, 6 * P])
    xp_v = i["x_prompt"].rearrange("b (t p) d -> p (b t) d", p=P)
    xs_v = i["x_sample"].rearrange("b s d -> (b s) d")

    def load_rows(sp, s_x):
        for t in range(NP):
            sp.dma_start(x_sb[:, t, :], xp_v[:, t, :]).then_inc(s_x[t], 16)
        sp.dma_start(x_sb[:, NP, :], xs_v).then_inc(s_x[NP], 16)

    with ExitStack() as ctx:
        s_id = ctx.enter_context(nc.semaphore("ident_step"))
        block = ctx.enter_context(nc.Block())

        @block.gpsimd
        def _(pool):
            pool.memset(ident[:], 0.0).then_inc(s_id, 1)
            pool.wait_ge(s_id, 1)
            pool.affine_select(out=ident[:], in_=ident[:], compare_op=ALU.not_equal, fill=1.0, base=0,
                               pattern=[[-1, P]], channel_multiplier=1).then_inc(s_id, 1)
            pool.wait_ge(s_id, 2)

    ffn_phase(nc, "f1", at_selb, at, x_sb, ident, load_rows, i["ffn1_norm"][0], i["ffn1_w_gate"], i["ffn1_w_up"], i["ffn1_w_down"])
    wi_phase(nc, at_x, at, x_sb, ident, selb, late_acc, i["mix_norm"][0], i["w_in"], i["rel_bias"], urel, i["rope_cos"], i["rope_sin"], i["cache_idx_k"],
             x_mid, proj, o["idx_k_prompt"], o["idx_k_sample"])
    FW = H * HD
    flat = lambda a: a.rearrange("a b s h d -> (a b s) (h d)")
    keep0 = SEQ - min(LEFT * CHUNK, SEQ)
    outs = [(flat(o["a_k_prompt"]), FW, keep0, SEQ), (flat(o["a_v_prompt"]), 2 * FW, keep0, SEQ),
            (flat(o["b_k_prompt"]), N_QKV + FW, 0, SEQ), (flat(o["b_v_prompt"]), N_QKV + 2 * FW, 0, SEQ),
            (flat(o["a_k_sample"]), FW, SEQ, ROWS), (flat(o["a_v_sample"]), 2 * FW, SEQ, ROWS),
            (flat(o["b_k_sample"]), N_QKV + FW, SEQ, ROWS), (flat(o["b_v_sample"]), N_QKV + 2 * FW, SEQ, ROWS)]
    attn_phase(nc, at_x, ident, selb, late_acc, proj, urel,
               ((i["cache_a_k"], i["cache_a_v"]), (i["cache_b_k"], i["cache_b_v"])), oT_hi, oT_lo, outs)
    wo_phase(nc, at, x_sb, x_mid, i["w_out"], oT_hi, oT_lo)
    ffn_phase(nc, "f2", at_selb, at, x_sb, ident, None, i["ffn2_norm"][0], i["ffn2_w_gate"], i["ffn2_w_up"], i["ffn2_w_down"])
    final_phase(nc, at, x_sb, i["final_norm"], o["y_prompt"].rearrange("b s d -> (b s) d"), o["y_sample"].rearrange("b s d -> (b s) d"))


_INS = ["x_prompt", "x_sample", "cache_a_k", "cache_a_v", "cache_b_k", "cache_b_v", "cache_idx_k",
        "ffn1_norm", "ffn1_w_gate", "ffn1_w_up", "ffn1_w_down", "mix_norm", "w_in", "rel_bias", "w_out",
        "ffn2_norm", "ffn2_w_gate", "ffn2_w_up", "ffn2_w_down", "final_norm"]
_OUTS = [("y_prompt", (1, SEQ, D)), ("y_sample", (DEC_B, DEC_S, D)),
         ("a_k_prompt", (1, 1, min(LEFT * CHUNK, SEQ), H, HD)), ("a_v_prompt", (1, 1, min(LEFT * CHUNK, SEQ), H, HD)),
         ("b_k_prompt", (1, 1, SEQ, H, HD)), ("b_v_prompt", (1, 1, SEQ, H, HD)), ("idx_k_prompt", (1, 1, SEQ, ID)),
         ("a_k_sample", (1, DEC_B, DEC_S, H, HD)), ("a_v_sample", (1, DEC_B, DEC_S, H, HD)),
         ("b_k_sample", (1, DEC_B, DEC_S, H, HD)), ("b_v_sample", (1, DEC_B, DEC_S, H, HD)),
         ("idx_k_sample", (1, DEC_B, DEC_S, ID))]


def rope_tables():
    half = HD // 2
    inv = np.power(np.float32(10000.0), -np.arange(half, dtype=np.float32) / np.float32(half)).astype(np.float32)
    pos = np.concatenate([np.arange(SEQ), PAST + np.tile(np.arange(DEC_S), DEC_B)]).astype(np.float32)
    angle = (pos[:, None] * inv[None, :]).astype(np.float32)
    return np.cos(angle), np.sin(angle)


def kernel(**inputs):
    import concourse.bacc as _bacc
    from concourse.bass_utils import run_bass_kernel_spmd as _run

    nc = _bacc.Bacc("TRN2", target_bir_lowering=False, num_devices=1)
    arrays, ins, outs = {}, {}, {}
    for name in _INS:
        a = np.ascontiguousarray(inputs[name])
        arrays[f"in_{name}"] = a
        ins[name] = nc.dram_tensor(f"in_{name}", a.shape, mybir.dt.from_np(a.dtype), kind="ExternalInput").ap()
    for name, a in zip(("rope_cos", "rope_sin"), rope_tables()):
        arrays[f"in_{name}"] = a
        ins[name] = nc.dram_tensor(f"in_{name}", a.shape, F32, kind="ExternalInput").ap()
    for name, shape in _OUTS:
        outs[name] = nc.dram_tensor(f"out_{name}", shape, F32, kind="ExternalOutput").ap()
    program(nc, ins, outs)
    r = _run(nc, [arrays], core_ids=[0])
    return tuple(r.results[0][f"out_{name}"] for name, _ in _OUTS)
```

```python
from contextlib import ExitStack

import numpy as np

import concourse.bass as bass
from concourse import mybir

F32 = mybir.dt.float32
F32R = mybir.dt.float32r
BF16 = mybir.dt.bfloat16
ALU = mybir.AluOpType
ACT = mybir.ActivationFunctionType
AX = mybir.AxisListType

P = 128
D = 1024
KT = D // P
SEQ, DEC_B, DEC_S, PAST = 1024, 8, 16, 512
NP = SEQ // P
NT = NP + 1
ROWS = NT * P
FF = 2816
FB = 256
FSTEPS = FF // FB
CH = 3
NCH = NT // CH
CW = CH * P
H, HD = 8, 64
HT = H * HD // P
CHUNK, LEFT = 64, 8
IH, ID = 8, 32
TOPK = 256
SEL_S = min(TOPK, (PAST + DEC_S) // 4)
MAXREL = 128
BAND = LEFT * CHUNK + P
KS = PAST + DEC_S
N_QKV = 3 * H * HD
N_IDX = IH * ID + ID + IH
EPS = 1e-6
NEG = -1.0e30
GONE = -3.0e38
UNSEEN = -2.0e38
FIRST = 3.0e38


SBUF_START, SBUF_END = 16512, 229344


class Plan:

    def __init__(self, nc, tag, at):
        self.nc, self.tag, self.at = nc, tag, at

    def __call__(self, name, shape, dtype):
        size = int(np.prod(shape[1:])) * mybir.dt.size(dtype)
        t = self.nc.alloc_sbuf_tensor_at(f"{self.tag}_{name}", shape, dtype, offset=self.at)
        self.at += -(-size // 32) * 32
        assert self.at <= SBUF_END, (self.tag, name, self.at - SBUF_END)
        return t


def at_end(size):
    return SBUF_END - 2 * KT * ROWS * 4 - size


class TileNorm:
    SLOTS = NT + 5

    def __init__(self, nc, ctx, tag, at, st, x_sb, xT, ident, g_dram, y=None):
        self.x_sb, self.xT, self.ident, self.g_dram, self.st, self.y = x_sb, xT, ident, g_dram, st, y
        place = Plan(nc, tag, at)
        self.xn = place("xn", [P, 2, D], F32)
        self.g_bc = place("g", [P, D], F32)
        self.junk = place("junk", [P, D], F32)
        sem = lambda n: ctx.enter_context(nc.semaphore(f"{tag}_{n}"))
        self.s_g, self.s_ss, self.s_v = sem("g_loaded"), sem("squares_summed"), sem("mean_ready")
        self.s_sd, self.s_ch, self.s_xn = sem("root_ready"), sem("newton_step"), sem("row_normed")
        self.s_tr, self.s_hi, self.s_lo = sem("transposed"), sem("hi_ready"), sem("lo_ready")
        self.s_out = [sem(f"row_stored{i}") for i in range(len(y))] if y else None

    SS, V, SD, R, A, B = range(6)

    def xp_of(self, xp, t):
        return xp[:, 2 * (t % 2):2 * (t % 2) + 2, :].rearrange("p b c -> p (b c)")

    def load(self, sp):
        sp.dma_start(self.g_bc[:], self.g_dram.partition_broadcast(P)).then_inc(self.s_g, 16)

    def act(self, act, t, xp, x_ready):
        st, col = self.st, lambda k, t: self.st[:, k, t:t + 1]
        if not self.y and 0 <= t - 4 < NT:
            u = t - 4
            act.wait_ge(self.s_tr, u + 1)
            act.activation(self.xT[0][:, :, u * P:(u + 1) * P],
                           self.xp_of(xp, u).rearrange("p (k c) -> p k c", k=KT), ACT.Copy).then_inc(self.s_hi, 1)
        if t < NT:
            x_ready(act, t)
            if t:
                act.wait_ge(self.s_ss, t)
            act.activation(self.junk[:], self.x_sb[:, t, :], ACT.Square, accum_out=col(self.SS, t)).then_inc(self.s_ss, 1)
        if 0 <= t - 1 < NT:
            act.wait_ge(self.s_v, t)
            act.activation(col(self.SD, t - 1), col(self.V, t - 1), ACT.Sqrt).then_inc(self.s_sd, 1)

    def dve_lo(self, dve, t, xp):
        if not self.y and 0 <= t - 5 < NT:
            u = t - 5
            dve.wait_ge(self.s_hi, u + 1)
            cs = slice(u * P, (u + 1) * P)
            dve.tensor_tensor(self.xT[1][:, :, cs], self.xp_of(xp, u).rearrange("p (k c) -> p k c", k=KT),
                              self.xT[0][:, :, cs].bitcast(F32), ALU.subtract).then_inc(self.s_lo, 1)

    def dve(self, dve, t, x_ready):
        col = lambda k, t: self.st[:, k, t:t + 1]
        if 0 <= t - 1 < NT:
            dve.wait_ge(self.s_ss, t)
            dve.tensor_scalar(col(self.V, t - 1), col(self.SS, t - 1), 1.0 / D, EPS, ALU.mult, ALU.add).then_inc(self.s_v, 1)
        if not 0 <= t - 2 < NT:
            return
        u, n = t - 2, 5 * (t - 2)
        dve.wait_ge(self.s_sd, u + 1)
        dve.reciprocal(col(self.R, u), col(self.SD, u)).then_inc(self.s_ch, 1)
        dve.wait_ge(self.s_ch, n + 1)
        dve.tensor_tensor(col(self.A, u), col(self.R, u), col(self.R, u), ALU.mult).then_inc(self.s_ch, 1)
        dve.wait_ge(self.s_ch, n + 2)
        dve.tensor_tensor(col(self.B, u), col(self.A, u), col(self.V, u), ALU.mult).then_inc(self.s_ch, 1)
        dve.wait_ge(self.s_ch, n + 3)
        dve.tensor_scalar(col(self.A, u), col(self.B, u), -0.5, 1.5, ALU.mult, ALU.add).then_inc(self.s_ch, 1)
        dve.wait_ge(self.s_ch, n + 4)
        dve.tensor_tensor(col(self.SS, u), col(self.R, u), col(self.A, u), ALU.mult).then_inc(self.s_ch, 1)
        dve.wait_ge(self.s_ch, n + 5)
        x_ready(dve, u)
        if u == 0:
            dve.wait_ge(self.s_g, 16)
        if self.y:
            ring = len(self.y)
            if u >= ring:
                dve.wait_ge(self.s_out[u % ring], 16 * (u // ring))
            out = self.y[u % ring][:]
        else:
            if u >= 2:
                dve.wait_ge(self.s_tr, u - 1)
            out = self.xn[:, u % 2, :]
        dve.scalar_tensor_tensor(out, self.x_sb[:, u, :], col(self.SS, u), self.g_bc[:], ALU.mult, ALU.mult).then_inc(self.s_xn, 1)

    def pe(self, pe, t, xp):
        if not self.y and 0 <= t - 3 < NT:
            u = t - 3
            pe.wait_ge(self.s_xn, u + 1)
            if u >= 2:
                pe.wait_ge(self.s_lo, u - 1)
            for k in range(KT):
                last = pe.transpose(self.xp_of(xp, u)[:, k * P:(k + 1) * P], self.xn[:, u % 2, k * P:(k + 1) * P], self.ident[:])
            last.then_inc(self.s_tr, 1)

    def sp_stores(self, sp, dst_of):
        ring = len(self.y)
        for t in range(NT):
            sp.wait_ge(self.s_xn, t + 1)
            sp.dma_start(dst_of(t), self.y[t % ring][:]).then_inc(self.s_out[t % ring], 16)
        for i in range(ring):
            sp.wait_ge(self.s_out[i], 16 * len(range(i, NT, ring)))

    def done(self, eng):
        eng.wait_ge(self.s_lo, NT)


def three_pass(pe, out, a, b, first, last):
    pe.matmul(out, a[0], b[0], start=first, stop=False)
    pe.matmul(out, a[0], b[1], start=False, stop=False)
    return pe.matmul(out, a[1], b[0], start=False, stop=last)


def ffn_phase(nc, tag, at_selb, at, x_sb, xT, st, ident, load_x, g_dram, wg, wu, wd, g_next, prefetch, store):
    xT_hi, xT_lo = xT
    wg_v = wg.rearrange("a (k p) f -> p (a k) f", p=P)
    wu_v = wu.rearrange("a (k p) f -> p (a k) f", p=P)
    wd_v = wd.rearrange("a (n p) d -> p (a n) d", p=P)
    with ExitStack() as ctx:
        sem = lambda n: ctx.enter_context(nc.semaphore(f"{tag}_{n}"))
        keep = Plan(nc, tag, at)
        raw_d = Plan(nc, tag, at_selb)("raw_d", [P, 2, D], F32)
        sp_g = [[keep(f"g{'hl'[q]}{f}", [P, KT, P], F32R) for f in range(2)] for q in range(2)]
        sp_u = [[keep(f"u{'hl'[q]}{f}", [P, KT, P], F32R) for f in range(2)] for q in range(2)]
        sp_d = [keep(f"d{'hl'[q]}", [P, 2, D], F32R) for q in range(2)]
        s_x = [sem(f"x_loaded{t}") for t in range(NT)] if load_x else None
        first = TileNorm(nc, ctx, tag + "a", keep.at, st, x_sb, xT, ident, g_dram) if load_x else None
        x_loaded = lambda e, t: e.wait_ge(s_x[t], 16)
        h_hi = keep("h_hi", [P, 2, ROWS], F32R)
        h_lo = keep("h_lo", [P, 2, ROWS], F32R)
        silu = keep("silu", [P, 2, CW], F32)
        raws = Plan(nc, tag, at_end(2 * KT * FB * 4))
        assert keep.at <= raws.at
        y = [Plan(nc, tag, at + i * D * 4)(f"y{i}", [P, D], F32) for i in range(4)] if store else None
        after = TileNorm(nc, ctx, tag + "b", raws.at, st, x_sb, xT, ident, g_next, y)
        raw_g = raws("raw_g", [P, KT, FB], F32)
        raw_u = raws("raw_u", [P, KT, FB], F32)
        pgu = ctx.enter_context(nc.psum_tensor(f"{tag}_pgu", [P, 4, 512], F32))
        pg, pu = [pgu[:, i, :] for i in range(2)], [pgu[:, 2 + i, :] for i in range(2)]
        py = [ctx.enter_context(nc.psum_tensor(f"{tag}_py{i}", [P, 512], F32)) for i in range(3)]

        s_rg, s_ru, s_rd = sem("gate_loaded"), sem("up_loaded"), sem("down_loaded")
        s_whi = sem("weights_hi")
        s_gu = sem("gate_up_split")
        s_dn = sem("down_split")
        s_gud = sem("gate_up_done")
        s_silu = sem("silu_ready")
        s_free = sem("gate_up_read")
        s_hf = sem("hidden_ready")
        s_hh = sem("hidden_hi")
        s_h = sem("hidden_split")
        s_y = sem("down_done")
        s_acc = sem("y_added")
        NY = NT * 2

        def x_done(eng, t):
            eng.wait_ge(s_acc, 3 + NY * (FSTEPS - 1) + 2 * (t + 1))

        @(block := ctx.enter_context(nc.Block())).sync
        def _(sp):
            if load_x:
                load_x(sp, s_x)
                first.load(sp)
            for s, dst, src in ((s_rg, raw_g, wg_v[:, :, 0:FB]), (s_ru, raw_u, wu_v[:, :, 0:FB]),
                                (s_rd, raw_d, wd_v[:, 0:2, :])):
                sp.dma_start(dst[:], src).then_inc(s, 16)
            with sp.Fori(1, FSTEPS) as i:
                sp.wait_ge(s_gu, 2 * i)
                sp.dma_start(raw_g[:], wg_v[:, :, bass.ds(i * FB, FB)]).then_inc(s_rg, 16)
                sp.dma_start(raw_u[:], wu_v[:, :, bass.ds(i * FB, FB)]).then_inc(s_ru, 16)
                sp.wait_ge(s_dn, i)
                sp.dma_start(raw_d[:], wd_v[:, bass.ds(2 * i, 2), :]).then_inc(s_rd, 16)
            sp.wait_ge(s_gu, 2 * FSTEPS)
            after.load(sp)
            sp.wait_ge(s_gud, 2 * NCH * FSTEPS)
            if store:
                after.sp_stores(sp, store)
            else:
                prefetch(sp)

        def act_gate_up_hi(act, j, f):
            fs = slice(f * P, (f + 1) * P)
            act.wait_ge(s_rg, 16 * j + 16)
            act.activation(sp_g[0][f][:], raw_g[:, :, fs], ACT.Copy).then_inc(s_whi, 1)
            act.wait_ge(s_ru, 16 * j + 16)
            act.activation(sp_u[0][f][:], raw_u[:, :, fs], ACT.Copy).then_inc(s_whi, 1)

        def act_down_hi(act, j):
            act.wait_ge(s_rd, 16 * j + 16)
            act.activation(sp_d[0][:], raw_d[:], ACT.Copy).then_inc(s_whi, 1)

        def act_silu(act, i, f):
            for c in range(NCH):
                k = NCH * f + c
                act.wait_ge(s_gud, 2 * NCH * i + k + 1)
                act.wait_ge(s_h, 2 * NCH * i + k + 1)
                act.activation(silu[:, k % 2, :], pg[k % 2][:, 0:CW], ACT.Silu).then_inc(s_silu, 1)

        def act_step(act, i, more):
            act_silu(act, i, 0)
            if more:
                act.wait_ge(s_gud, 2 * NCH * i + NCH)
                act_gate_up_hi(act, i + 1, 0)
            act_silu(act, i, 1)
            if more:
                act.wait_ge(s_gud, 2 * NCH * i + 2 * NCH)
                act_gate_up_hi(act, i + 1, 1)
                act.wait_ge(s_y, NY * i + 2 * NY)
                act_down_hi(act, i + 1)

        @block.scalar
        def _(act):
            if load_x:
                for t in range(TileNorm.SLOTS):
                    first.act(act, t, pgu, x_loaded)
            act_gate_up_hi(act, 0, 0)
            act_gate_up_hi(act, 0, 1)
            act_down_hi(act, 0)
            with act.Fori(0, FSTEPS - 1) as i:
                act_step(act, i, True)
            act_step(act, FSTEPS - 1, False)
            for t in range(TileNorm.SLOTS):
                after.act(act, t, pgu, x_done)

        def dve_gate_up_lo(dve, j, f):
            fs = slice(f * P, (f + 1) * P)
            dve.wait_ge(s_whi, 5 * j + 2 * f + 1)
            dve.tensor_tensor(sp_g[1][f][:], raw_g[:, :, fs], sp_g[0][f][:].bitcast(F32), ALU.subtract)
            dve.wait_ge(s_whi, 5 * j + 2 * f + 2)
            dve.tensor_tensor(sp_u[1][f][:], raw_u[:, :, fs], sp_u[0][f][:].bitcast(F32), ALU.subtract).then_inc(s_gu, 1)

        def dve_down_lo(dve, j):
            dve.wait_ge(s_whi, 5 * j + 5)
            dve.tensor_tensor(sp_d[1][:], raw_d[:], sp_d[0][:].bitcast(F32), ALU.subtract).then_inc(s_dn, 1)

        def dve_hidden(dve, i, f):
            for c in range(NCH):
                k = NCH * f + c
                n = 2 * NCH * i + k + 1
                cs = slice(c * CW, (c + 1) * CW)
                dve.wait_ge(s_silu, n)
                dve.tensor_tensor(silu[:, k % 2, :], silu[:, k % 2, :], pu[k % 2][:, 0:CW], ALU.mult).then_inc(s_free, 1)
                dve.wait_ge(s_y, NY * i + 2 * CH * (c + 1))
                dve.wait_ge(s_free, n + 2)
                dve.tensor_copy(h_hi[:, f, cs], silu[:, k % 2, :]).then_inc(s_hh, 1)
                dve.wait_ge(s_hh, n)
                dve.tensor_tensor(h_lo[:, f, cs], silu[:, k % 2, :], h_hi[:, f, cs].bitcast(F32), ALU.subtract).then_inc(s_h, 1)

        def dve_step(dve, i, more):
            dve_hidden(dve, i, 0)
            if more:
                dve_gate_up_lo(dve, i + 1, 0)
            dve_hidden(dve, i, 1)
            if more:
                dve_gate_up_lo(dve, i + 1, 1)
            for t in range(NT if more else TileNorm.SLOTS):
                if not more:
                    after.dve_lo(dve, t, pgu)
                for k in range(2 * t, 2 * t + 2) if t < NT else ():
                    xs = x_sb[:, t, (k % 2) * 512:(k % 2 + 1) * 512]
                    dve.wait_ge(s_y, NY * i + NY + k + 1)
                    dve.scalar_tensor_tensor(xs, py[k % 3][:], 0.5, xs, ALU.mult, ALU.add).then_inc(s_acc, 1)
                if not more:
                    after.dve(dve, t, x_done)
            if more:
                dve_down_lo(dve, i + 1)

        @block.vector
        def _(dve):
            dve.sem_inc(s_free, 2)
            dve.sem_inc(s_h, 2)
            dve.sem_inc(s_acc, 3)
            if load_x:
                for t in range(TileNorm.SLOTS):
                    first.dve_lo(dve, t, pgu)
                    first.dve(dve, t, x_loaded)
            dve_gate_up_lo(dve, 0, 0)
            dve_gate_up_lo(dve, 0, 1)
            dve_down_lo(dve, 0)
            with dve.Fori(0, FSTEPS - 1) as i:
                dve_step(dve, i, True)
            dve_step(dve, FSTEPS - 1, False)

        def pe_step(pe, i, more=True):
            for f in range(2):
                pe.wait_ge(s_gu, 2 * i + f + 1)
                for c in range(NCH):
                    k = NCH * f + c
                    cs = slice(c * CW, (c + 1) * CW)
                    pe.wait_ge(s_free, 2 * NCH * i + k + 1)
                    for w, out in ((sp_g, pg), (sp_u, pu)):
                        for kt in range(KT):
                            last = three_pass(pe, out[k % 2][:, 0:CW], (w[0][f][:, kt, :], w[1][f][:, kt, :]),
                                              (xT_hi[:, kt, cs], xT_lo[:, kt, cs]), kt == 0, kt == KT - 1)
                    last.then_inc(s_gud, 1)
            pe.wait_ge(s_dn, i + 1)
            for k in range(NY):
                t, half = k // 2, k % 2
                ts, hs = slice(t * P, (t + 1) * P), slice(half * 512, (half + 1) * 512)
                if k % (2 * CH) == 0:
                    pe.wait_ge(s_h, 2 * NCH * i + NCH + t // CH + 3)
                pe.wait_ge(s_acc, NY * i + k + 1)
                for f in range(2):
                    last = three_pass(pe, py[k % 3][:], (h_hi[:, f, ts], h_lo[:, f, ts]),
                                      (sp_d[0][:, f, hs], sp_d[1][:, f, hs]), f == 0, f == 1)
                last.then_inc(s_y, 1)
                if not more and half:
                    if t == 3:
                        pe.wait_ge(s_free, 2 + 2 * NCH * FSTEPS)
                    after.pe(pe, t, pgu)
            if not more:
                for t in range(NT, TileNorm.SLOTS):
                    after.pe(pe, t, pgu)

        @block.tensor
        def _(pe):
            pe.sem_inc(s_y, NY)
            if load_x:
                for t in range(TileNorm.SLOTS):
                    first.pe(pe, t, pgu)
                first.done(pe)
            with pe.Fori(0, FSTEPS - 1) as i:
                pe_step(pe, i)
            pe_step(pe, FSTEPS - 1, False)


EARLY = 10
WC = 256
NCHUNK = 2 * N_QKV // WC
IDX_AT = 2 * N_QKV
IC = 4 * ID
SELB_AT = [P * t * (t + 1) // 2 for t in range(NP + 1)]


def rel_rows(dve, rb, ur, s, n0):
    dve.tensor_copy(ur[:, 0:4 * P], rb[:, 2 * MAXREL:2 * MAXREL + 1].broadcast_to([H, 4 * P])).then_inc(s, 1)
    dve.wait_ge(s, n0 + 1)
    dve.tensor_copy(ur[:, 4 * P - 1:6 * P - 1], rb[:, 2 * MAXREL:0:-1]).then_inc(s, 1)
    dve.tensor_copy(ur[:, 6 * P - 1:6 * P], rb[:, 0:1]).then_inc(s, 1)


def wi_phase(nc, at_x, at, x_sb, xT, ident, selb, late_acc, raw, s_raw, w_in, rel_bias, urel, cos, sin, cache_idx, x_mid, proj, idx_p, idx_s):
    tag = "w"
    xT_hi, xT_lo = xT
    w_v = w_in.rearrange("a (k p) n -> p (a k) n", p=P)
    proj_v = proj.rearrange("(t p) n -> p t n", p=P)
    with ExitStack() as ctx:
        sem = lambda n: ctx.enter_context(nc.semaphore(f"{tag}_{n}"))
        keep = Plan(nc, tag, at)
        keep.at += KT * N_IDX * 4
        w_hi = [keep(f"w_hi{i}", [P, KT, w], F32R) for i, w in enumerate((N_IDX, WC))]
        w_lo = [keep(f"w_lo{i}", [P, KT, w], F32R) for i, w in enumerate((N_IDX, WC))]
        beside = Plan(nc, tag, keep.at)
        rb = beside("rb", [H, 2 * MAXREL + 1], F32)
        ur = beside("ur", [H, 6 * P], F32)
        at_stage = keep.at
        stage = [keep(f"stage{i}", [P, NT, WC], F32) for i in range(2)]
        early = Plan(nc, tag, at_stage)
        rx_i = early("rx_i", [P, 2, NT * 9 * ID // 2], F32)
        early = Plan(nc, tag, at_stage)
        bdq = [early(f"bdq{g}", [P, IH, P], F32) for g in range(2)]
        early = Plan(nc, tag, at_stage + NT * WC * 4)
        spread = early("spread", [P, IH, DEC_B, ID], F32)
        kspread = early("kspread", [P, DEC_B, ID], F32)
        assert early.at <= keep.at
        idx = keep("idx", [P, NT, N_IDX], F32)
        cs_t = keep("cos", [P, NT, HD // 2], F32)
        sn_t = keep("sin", [P, NT, HD // 2], F32)
        rx = Plan(nc, tag, keep.at)("rx", [P, 2, NT * WC // 2], F32)
        kc = keep("kc", [P, PAST // P, DEC_B, ID], F32)
        kcT = [keep(f"kcT{g}", [P, KS], F32) for g in range(2)]
        ksum = keep("ksum", [P, 2, P], F32)
        ix = Plan(nc, tag, at_x)
        acc = [None, ix("acc1", [P, SEQ], F32)]
        acc[0] = ix("acc0", [P, SEQ], F32)
        qi4 = ix("qi4", [P, IH, 4, ID], F32R)
        own = ix("own", [P, DEC_B], F32)
        m8 = ix("m8", [P, 3, 8], F32)
        acc_s = ix("acc_s", [P, KS + 4], F32)
        kiT = ix("kiT", [P, SEQ], F32R)
        qiT = [ix(f"qiT{i}", [P, IH, P], F32R) for i in range(2)]
        ki4 = Plan(nc, tag, ix.at)("ki4", [P, NP, 4, ID], F32R)
        relu = ix("relu", [P, 2, SEQ], F32)
        assert ix.at <= at_x + NT * D * 4
        assert keep.at <= at_end(0)
        pw = [ctx.enter_context(nc.psum_tensor(f"{tag}_pw{i}", [P, 512], F32)) for i in range(3)]
        ps = [ctx.enter_context(nc.psum_tensor(f"{tag}_ps{i}", [P, D], F32)) for i in range(2)]

        s_whi, s_wlo = sem("w_hi"), sem("w_split")
        s_grp, s_ev = sem("group_done"), sem("group_read")
        s_rot = sem("rope_step")
        s_rdy = [sem(f"stage_ready{i}") for i in range(2)]
        s_put = [sem(f"stage_stored{i}") for i in range(2)]
        s_xst = sem("x_stored")
        s_tab = sem("tables_loaded")
        s_kc = sem("cached_keys_loaded")
        s_iout = sem("idx_keys_stored")
        s_ich = sem("idx_step")
        s_rel, s_ur = sem("rel_bias_moved"), sem("ur_step")
        s_own = sem("own_mask")
        s_idx = sem("idx_rows_ready")
        s_pf, s_pd = sem("pair_filled"), sem("pair_read")
        s_rlf = sem("relu_read")
        s_q4 = sem("queries_expanded")
        s_sel = sem("selection_step")
        s_acc = sem("scores_step")

        TILES = list(range(TOPK // P, NP))
        PAIRS = [TILES[i:i + 2] for i in range(0, len(TILES), 2)]
        unit_of, n_units = {}, 0
        def take(key):
            nonlocal n_units
            unit_of[key] = n_units
            n_units += 1
        take("keys")
        for t in PAIRS[0]:
            take(("q", t))
            for h in range(IH):
                take((t, h))
        for key in ("bdq0", "bdq1", "kc", "kn"):
            take(key)
        for h in range(IH):
            take(("s", h))
        for t in PAIRS[1] + PAIRS[2]:
            take(("q", t))
            for h in range(IH):
                take((t, h))
        relu_of = {k: n for n, k in enumerate(k for k in sorted(unit_of, key=unit_of.get) if isinstance(k, tuple) and k[0] != "q")}
        tile_no = {t: n for n, t in enumerate(TILES)}
        def col(c):
            return (c - 1) * WC

        block = ctx.enter_context(nc.Block())

        @block.sync
        def _(sp):
            sp.dma_start(rb[:], rel_bias[0]).then_inc(s_rel, 16)
            sp.dma_start(cs_t[:], cos.rearrange("(t p) f -> p t f", p=P)).then_inc(s_tab, 16)
            sp.dma_start(sn_t[:], sin.rearrange("(t p) f -> p t f", p=P)).then_inc(s_tab, 16)
            sp.dma_start(x_mid.rearrange("(t p) d -> p t d", p=P), x_sb[:]).then_inc(s_xst, 16)
            sp.wait_ge(s_ur, 3)
            sp.dma_start(urel, ur[:]).then_inc(s_rel, 16)
            for kt in range(PAST // P):
                sp.dma_start(kc[:, kt, :, :], cache_idx[0].rearrange("b (k p) d -> p k b d", p=P)[:, kt]).then_inc(s_kc, 16)
            sp.wait_ge(s_wlo, 1)
            sp.dma_start(raw[:, :, 0:WC], w_v[:, :, 0:WC]).then_inc(s_raw, 16)
            sp.wait_ge(s_idx, 1)
            sp.dma_start(idx_p.rearrange("a b (t p) d -> p (a b t) d", p=P), idx[:, 0:NP, IH * ID:IH * ID + ID]).then_inc(s_iout, 16)
            sp.dma_start(idx_s.rearrange("a b s d -> (a b s) d"), idx[:, NP, IH * ID:IH * ID + ID]).then_inc(s_iout, 16)
            with sp.Fori(1, NCHUNK) as c:
                sp.wait_ge(s_wlo, c + 1)
                sp.dma_start(raw[:, :, 0:WC], w_v[:, :, bass.ds(c * WC, WC)]).then_inc(s_raw, 16)
            sp.wait_ge(s_iout, 32)
            sp.wait_ge(s_xst, 16)

        def act_hi(act, c, slot, w):
            act.wait_ge(s_raw, 16 * c + 16)
            if not (isinstance(c, int) and c < 2):
                act.wait_ge(s_grp, NT * c - NT)
            act.activation(w_hi[slot][:, :, 0:w], raw[:, :, 0:w], ACT.Copy).then_inc(s_whi, 1)

        def act_unit(act, key, dst, src_cols, func, scale):
            u = unit_of[key]
            act.wait_ge(s_pf, u + 1)
            act.activation(dst, ps[u % 2][:, 0:src_cols] if len(dst.shape) == 2 else
                           ps[u % 2][:, 0:src_cols].rearrange("p (h c) -> p h c", c=P), func, scale=scale).then_inc(s_pd, 1)

        def act_tile(act, t):
            n = tile_no[t]
            if n >= 2:
                act.wait_ge(s_pf, unit_of[(TILES[n - 2], IH - 1)] + 1)
            act_unit(act, ("q", t), qiT[n % 2][:], D, ACT.Copy, 1.0)
            for h in range(IH):
                r = relu_of[(t, h)]
                if r >= 2:
                    act.wait_ge(s_rlf, r - 1)
                act_unit(act, (t, h), relu[:, r % 2, 0:P * (t + 1)], P * (t + 1), ACT.Relu, 1.0 / 16)

        def act_evac(act, c, slot, k):
            if not (isinstance(k, int) and k == 0):
                act.wait_ge(s_put[slot], 16 * k)
            for t in range(NT):
                act.wait_ge(s_grp, NT * c + t + 1)
                act.activation(stage[slot][:, t, :], pw[t % 3][:, 0:WC], ACT.Copy).then_inc(s_ev, 1)

        def act_step(act, i, last=False):
            act_hi(act, 2 * i + 2, 0, WC)
            act_evac(act, 2 * i + 1, 1, i)
            if not last:
                act_hi(act, 2 * i + 3, 1, WC)
            act_evac(act, 2 * i + 2, 0, i)

        @block.scalar
        def _(act):
            act_hi(act, 0, 0, N_IDX)
            for t in range(NT):
                act.wait_ge(s_grp, t + 1)
                act.activation(idx[:, t, :], pw[t % 3][:, 0:N_IDX], ACT.Copy).then_inc(s_ev, 1)
            act_hi(act, 1, 1, WC)
            act_unit(act, "keys", kiT[:], SEQ, ACT.Copy, 1.0)
            for t in PAIRS[0]:
                act_tile(act, t)
            act_unit(act, "bdq0", bdq[0][:], D, ACT.Copy, 1.0)
            act_unit(act, "bdq1", bdq[1][:], D, ACT.Copy, 1.0)
            u = unit_of["kc"]
            act.wait_ge(s_pf, u + 1)
            for g in range(2):
                i = act.activation(kcT[g][:, 0:PAST], ps[u % 2][:, g * PAST:(g + 1) * PAST], ACT.Copy)
            i.then_inc(s_pd, 1)
            act_unit(act, "kn", ksum[:], 2 * P, ACT.Copy, 1.0)
            for h in range(IH):
                r = relu_of[("s", h)]
                act.wait_ge(s_rlf, r - 1)
                act_unit(act, ("s", h), relu[:, r % 2, 0:KS], KS, ACT.Relu, 1.0 / 16)
            with act.Fori(0, 2) as i:
                act_step(act, i)
            for t in PAIRS[1]:
                act_tile(act, t)
            with act.Fori(2, 4) as i:
                act_step(act, i)
            for t in PAIRS[2]:
                act_tile(act, t)
            act_step(act, 4)
            act_step(act, 5, True)

        def pool_lo(pool, c, slot, w):
            pool.wait_ge(s_whi, c + 1)
            pool.tensor_tensor(w_lo[slot][:, :, 0:w], raw[:, :, 0:w], w_hi[slot][:, :, 0:w].bitcast(F32), ALU.subtract).then_inc(s_wlo, 1)

        def rotate(eng, x, tmp, cosv, sinv, s, n0):
            half = x.shape[3] // 2
            x1, x2 = x[:, :, :, 0:half], x[:, :, :, half:2 * half]
            a, b = (tmp[:, q, 0:x.shape[1] * x.shape[2] * half].rearrange("p (t h f) -> p t h f", t=x.shape[1], h=x.shape[2]) for q in range(2))
            cb = cosv.unsqueeze(2).broadcast_to([P, x.shape[1], x.shape[2], half])
            sb_ = sinv.unsqueeze(2).broadcast_to([P, x.shape[1], x.shape[2], half])
            eng.tensor_tensor(a, x1, sb_, ALU.mult)
            eng.tensor_tensor(b, x2, sb_, ALU.mult).then_inc(s, 1)
            eng.wait_ge(s, n0 + 1)
            eng.tensor_tensor(x1, x1, cb, ALU.mult)
            eng.tensor_tensor(x2, x2, cb, ALU.mult).then_inc(s, 1)
            eng.wait_ge(s, n0 + 2)
            eng.tensor_tensor(x1, x1, b, ALU.subtract)
            return eng.tensor_tensor(x2, x2, a, ALU.add)

        def pool_chunk(pool, c, slot, k, rope, n_rope):
            pool.wait_ge(s_ev, NT * (c + 1))
            if rope:
                x = stage[slot][:].rearrange("p t (h f) -> p t h f", f=HD)
                rotate(pool, x, rx, cs_t[:], sn_t[:], s_rot, n_rope).then_inc(s_rdy[slot], 1)
                pool.wait_ge(s_rdy[slot], k)
            dst = proj_v[:, :, bass.ds((c - 1) * WC, WC)] if not isinstance(c, int) else proj_v[:, :, (c - 1) * WC:c * WC]
            pool.dma_start(dst, stage[slot][:]).then_inc(s_put[slot], 16)

        def pool_step(pool, i, rope=False, n=0, last=False):
            pool_lo(pool, 2 * i + 2, 0, WC)
            pool_chunk(pool, 2 * i + 1, 1, n + 1, rope, 4 * n)
            if not last:
                pool_lo(pool, 2 * i + 3, 1, WC)
            pool_chunk(pool, 2 * i + 2, 0, n + 1, rope, 4 * n + 2)

        @block.gpsimd
        def _(pool):
            pool.wait_ge(s_xst, 16)
            pool.memset(own[:], 1.0).then_inc(s_own, 1)
            for n, (m, b0, st_) in enumerate(((1, 0, -DEC_S), (-1, DEC_S - 1, DEC_S))):
                pool.wait_ge(s_own, n + 1)
                pool.affine_select(out=own[:], in_=own[:], compare_op=ALU.is_ge, fill=0.0, base=b0,
                                   pattern=[[st_, DEC_B]], channel_multiplier=m).then_inc(s_own, 1)
            pool.wait_ge(s_wlo, 1)
            pool_lo(pool, 1, 1, WC)
            pool.wait_ge(s_tab, 32)
            with pool.Fori(0, 2) as i:
                pool_step(pool, i)
            pool_step(pool, 2)
            pool_step(pool, 3, True, 0)
            pool_step(pool, 4, True, 1)
            pool_step(pool, 5, last=True)
            for i in range(2):
                pool.wait_ge(s_put[i], 16 * NCHUNK // 2)

        def dve_expand_q(dve, t):
            n = tile_no[t]
            q = idx[:, t, 0:IH * ID].rearrange("p (h f) -> p h f", f=ID)
            if n:
                dve.wait_ge(s_pf, unit_of[("q", TILES[n - 1])] + 1)
            dve.tensor_copy(qi4[:, :, 0, :], q).then_inc(s_ich, 1)
            dve.tensor_copy(qi4[:, :, 1, :], q).then_inc(s_ich, 1)
            dve.wait_ge(s_ich, 20 + 4 * n + 1)
            hi = qi4[:, :, 0, :].bitcast(F32)
            dve.tensor_tensor(qi4[:, :, 2, :], q, hi, ALU.subtract).then_inc(s_ich, 1)
            dve.tensor_tensor(qi4[:, :, 3, :], q, hi, ALU.subtract).then_inc(s_ich, 1)
            dve.wait_ge(s_ich, 20 + 4 * n + 4)
            dve.sem_inc(s_q4, 1)

        n_acc = [0]

        def dve_scores(dve, a, t_idx, keys, n):
            for h in range(IH):
                r = relu_of[(keys, h)]
                w = idx[:, t_idx, IH * ID + ID + h:IH * ID + ID + h + 1]
                dve.wait_ge(s_pd, relu_unit[r] + 1)
                if h == 0:
                    i = dve.tensor_scalar(a[:, 0:n], relu[:, r % 2, 0:n], w, None, ALU.mult)
                else:
                    dve.wait_ge(s_acc, n_acc[0])
                    i = dve.scalar_tensor_tensor(a[:, 0:n], relu[:, r % 2, 0:n], w, a[:, 0:n], ALU.mult, ALU.add)
                i.then_inc(s_acc, 1)
                n_acc[0] += 1
                dve.wait_ge(s_acc, n_acc[0])
                dve.sem_inc(s_rlf, 1)

        relu_unit = {relu_of[k]: unit_of[k] for k in relu_of}

        n_sel = [0]

        def dve_select(dve, parts, rounds):
            n = len(parts)
            base = n_sel[0]
            for i in range(rounds):
                for q, (a, w) in enumerate(parts):
                    if i:
                        dve.wait_ge(s_sel, base + 2 * n * i - n + q + 1)
                    dve.max(m8[:, q, :], a[:, 0:w]).then_inc(s_sel, 1)
                for q, (a, w) in enumerate(parts):
                    dve.wait_ge(s_sel, base + 2 * n * i + q + 1)
                    dve.match_replace(out=a[:, 0:w], in_to_replace=m8[:, q, :], in_values=a[:, 0:w], imm_value=GONE).then_inc(s_sel, 1)
            n_sel[0] = base + 2 * n * rounds
            dve.wait_ge(s_sel, n_sel[0])

        @block.vector
        def _(dve):
            dve.wait_ge(s_rel, 16)
            rel_rows(dve, rb, ur, s_ur, 0)
            pool_lo(dve, 0, 0, N_IDX)
            dve.wait_ge(s_rel, 32)
            dve.wait_ge(s_xst, 16)
            dve.wait_ge(s_tab, 32)
            dve.wait_ge(s_ev, NT)
            x = idx[:, :, 0:9 * ID].rearrange("p t (h f) -> p t h f", f=ID)
            rotate(dve, x, rx_i, cs_t[:, :, 0:HD // 2:2], sn_t[:, :, 0:HD // 2:2], s_ich, 0).then_inc(s_ich, 1)
            dve.wait_ge(s_ich, 3)
            dve.sem_inc(s_idx, 1)
            k = idx[:, 0:NP, IH * ID:IH * ID + ID]
            dve.tensor_copy(ki4[:, :, 0, :], k).then_inc(s_ich, 1)
            dve.tensor_copy(ki4[:, :, 2, :], k).then_inc(s_ich, 1)
            dve.wait_ge(s_ich, 5)
            for q in (1, 3):
                dve.tensor_tensor(ki4[:, :, q, :], k, ki4[:, :, 0, :].bitcast(F32), ALU.subtract).then_inc(s_ich, 1)
            dve.wait_ge(s_own, 3)
            q = idx[:, NP, 0:IH * ID].rearrange("p (h f) -> p h f", f=ID)
            dve.tensor_tensor(spread[:].rearrange("p h b f -> p h (b f)").rearrange("p h (b f) -> p h b f", b=DEC_B),
                              q.unsqueeze(2).broadcast_to([P, IH, DEC_B, ID]),
                              own[:].unsqueeze(1).unsqueeze(3).broadcast_to([P, IH, DEC_B, ID]), ALU.mult).then_inc(s_ich, 1)
            dve.tensor_tensor(kspread[:], idx[:, NP, IH * ID:IH * ID + ID].unsqueeze(1).broadcast_to([P, DEC_B, ID]),
                              own[:].unsqueeze(2).broadcast_to([P, DEC_B, ID]), ALU.mult).then_inc(s_ich, 1)
            few = SELB_AT[TOPK // P]
            dve.memset(selb[:, 0:few], 0.0).then_inc(s_ich, 1)
            dve.wait_ge(s_ich, 10)
            for t in range(TOPK // P):
                e = SELB_AT[t + 1]
                dve.memset(selb[0:CHUNK, e - CHUNK:e], NEG).then_inc(s_ich, 1)
            for _ in range(20 - 12):
                dve.sem_inc(s_ich, 1)
            dve.wait_ge(s_ich, 20)
            for t in PAIRS[0]:
                dve_expand_q(dve, t)
            for q, t in enumerate(PAIRS[0]):
                dve_scores(dve, acc[q], t, t, P * (t + 1))
                dve.wait_ge(s_acc, n_acc[0])
                dve.memset(acc[q][0:CHUNK, P * (t + 1) - CHUNK:P * (t + 1)], UNSEEN).then_inc(s_acc, 1)
                n_acc[0] += 1
            dve.wait_ge(s_pd, unit_of["kn"] + 1)
            for g in range(2):
                dve.tensor_reduce(out=kcT[g][:, PAST:KS], in_=ksum[:, g, :].rearrange("p (b q) -> p q b", b=DEC_B),
                                  axis=AX.X, op=ALU.add).then_inc(s_own, 1)
            dve_expand_q(dve, PAIRS[1][0])
            dve_scores(dve, acc_s, NP, "s", KS)
            dve.memset(acc_s[:, KS:KS + 4], FIRST).then_inc(s_acc, 1)
            n_acc[0] += 1
            dve.wait_ge(s_acc, n_acc[0])
            dve_select(dve, [(acc[q], P * (t + 1)) for q, t in enumerate(PAIRS[0])], TOPK // 8)
            dve_select(dve, [(acc_s, KS + 4)], (SEL_S + 4) // 8)
            for q, t in enumerate(PAIRS[0]):
                dve.tensor_scalar(selb[:, SELB_AT[t]:SELB_AT[t] + P * (t + 1)], acc[q][:, 0:P * (t + 1)], GONE, NEG,
                                  ALU.not_equal, ALU.mult).then_inc(s_acc, 1)
                n_acc[0] += 1
            dve.tensor_scalar(selb[:, SELB_AT[NP]:SELB_AT[NP] + KS], acc_s[:, 0:KS], GONE, NEG, ALU.not_equal, ALU.mult).then_inc(s_acc, 1)
            n_acc[0] += 1
            for pair in PAIRS[1:]:
                a_of = [acc[0], late_acc] if pair is PAIRS[-1] else acc
                for q, t in enumerate(pair):
                    if q or pair is PAIRS[2]:
                        dve_expand_q(dve, t)
                    dve.wait_ge(s_acc, n_acc[0])
                    dve_scores(dve, a_of[q], t, t, P * (t + 1))
                    dve.wait_ge(s_acc, n_acc[0])
                    dve.memset(a_of[q][0:CHUNK, P * (t + 1) - CHUNK:P * (t + 1)], UNSEEN).then_inc(s_acc, 1)
                    n_acc[0] += 1
                dve.wait_ge(s_acc, n_acc[0])
                whole = list(enumerate(pair))
                if pair is PAIRS[-1]:
                    dve_select(dve, [(a_of[q], P * (t + 1)) for q, t in whole], EARLY)
                    whole = whole[:1]
                dve_select(dve, [(a_of[q], P * (t + 1)) for q, t in whole], TOPK // 8 - EARLY * (pair is PAIRS[-1]))
                for q, t in whole:
                    dve.tensor_scalar(selb[:, SELB_AT[t]:SELB_AT[t] + P * (t + 1)], acc[q][:, 0:P * (t + 1)], GONE, NEG,
                                      ALU.not_equal, ALU.mult).then_inc(s_acc, 1)
                    n_acc[0] += 1

        def pe_chunk(pe, c, slot, w):
            pe.wait_ge(s_wlo, c + 1)
            for t in range(NT):
                if not (isinstance(c, int) and c == 0 and t < 3):
                    pe.wait_ge(s_ev, NT * c + t - 2)
                ts = slice(t * P, (t + 1) * P)
                for kt in range(KT):
                    last = three_pass(pe, pw[t % 3][:, 0:w], (xT_hi[:, kt, ts], xT_lo[:, kt, ts]),
                                      (w_hi[slot][:, kt, 0:w], w_lo[slot][:, kt, 0:w]), kt == 0, kt == KT - 1)
                last.then_inc(s_grp, 1)

        def pe_pair(pe, key):
            u = unit_of[key]
            if u >= 2:
                pe.wait_ge(s_pd, u - 1)
            return ps[u % 2]

        def pe_tile(pe, t):
            n = tile_no[t]
            out = pe_pair(pe, ("q", t))
            pe.wait_ge(s_q4, n + 1)
            for h in range(IH):
                last = pe.transpose(out[:, h * P:(h + 1) * P], qi4[:, h, :, :].rearrange("p c f -> p (c f)").bitcast(F32), ident[:])
            last.then_inc(s_pf, 1)
            for h in range(IH):
                out = pe_pair(pe, (t, h))
                if h == 0:
                    pe.wait_ge(s_pd, unit_of[("q", t)] + 1)
                for k0 in range(0, P * (t + 1), 512):
                    k1 = min(k0 + 512, P * (t + 1))
                    last = pe.matmul(out[:, k0:k1], qiT[n % 2][:, h, :], kiT[:, k0:k1], start=True, stop=True)
                last.then_inc(s_pf, 1)

        def pe_step(pe, i):
            pe_chunk(pe, 2 * i + 1, 1, WC)
            pe_chunk(pe, 2 * i + 2, 0, WC)

        @block.tensor
        def _(pe):
            pe_chunk(pe, 0, 0, N_IDX)
            pe.wait_ge(s_ich, 7)
            out = pe_pair(pe, "keys")
            for t in range(NP):
                last = pe.transpose(out[:, t * P:(t + 1) * P], ki4[:, t, :, :].rearrange("p c f -> p (c f)").bitcast(F32), ident[:])
            last.then_inc(s_pf, 1)
            for t in PAIRS[0]:
                pe_tile(pe, t)
            pe.wait_ge(s_ich, 9)
            for g in range(2):
                out = pe_pair(pe, f"bdq{g}")
                for h in range(IH):
                    last = pe.transpose(out[:, h * P:(h + 1) * P],
                                        spread[:, h, 4 * g:4 * g + 4, :].rearrange("p b f -> p (b f)"), ident[:])
                last.then_inc(s_pf, 1)
            out = pe_pair(pe, "kc")
            pe.wait_ge(s_kc, 16 * PAST // P)
            for g in range(2):
                for kt in range(PAST // P):
                    last = pe.transpose(out[:, g * PAST + kt * P:g * PAST + (kt + 1) * P],
                                        kc[:, kt, 4 * g:4 * g + 4, :].rearrange("p b f -> p (b f)"), ident[:])
            last.then_inc(s_pf, 1)
            out = pe_pair(pe, "kn")
            for g in range(2):
                last = pe.transpose(out[:, g * P:(g + 1) * P],
                                    kspread[:, 4 * g:4 * g + 4, :].rearrange("p b f -> p (b f)"), ident[:])
            last.then_inc(s_pf, 1)
            pe.wait_ge(s_own, 5)
            for h in range(IH):
                out = pe_pair(pe, ("s", h))
                for k0, k1 in ((0, PAST), (PAST, KS)):
                    for g in range(2):
                        last = pe.matmul(out[:, k0:k1], bdq[g][:, h, :], kcT[g][:, k0:k1], start=g == 0, stop=g == 1)
                last.then_inc(s_pf, 1)
            with pe.Fori(0, 2) as i:
                pe_step(pe, i)
            for t in PAIRS[1]:
                pe_tile(pe, t)
            with pe.Fori(2, 4) as i:
                pe_step(pe, i)
            for t in PAIRS[2]:
                pe_tile(pe, t)
            with pe.Fori(4, 6) as i:
                pe_step(pe, i)

FAR = BAND - 2 * MAXREL
NEAR = BAND - FAR


def attn_plan():
    heads = [(x, t, h) for x in range(2) for t in range(NP) for h in range(H)]
    tiles = [(x, t) for x in range(2) for t in range(NP)]
    plan = [("prep", 0, 0), ("score", 0), ("score", 1)]
    for g, (x, t, h) in enumerate(heads):
        n = tiles.index((x, t))
        if h == 4 and n + 1 < len(tiles):
            plan.append(("prep",) + tiles[n + 1])
        plan.append(("turn", g))
        if g + 2 < len(heads):
            plan.append(("score", g + 2))
        if g >= 1:
            plan.append(("value", g - 1))
        if h == 2 and n >= 1:
            plan.append(("out",) + tiles[n - 1])
    plan += [("value", len(heads) - 1), ("out",) + tiles[-1]]
    return heads, plan


def sample_plan(n):
    plan = [("keys", 0), ("keys", 1), ("score", 0)]
    for s in range(n):
        plan.append(("turn", s))
        if s + 1 < n:
            plan.append(("score", s + 1))
        if s >= 1:
            plan.append(("value", s - 1))
        if s + 2 < n:
            plan.append(("keys", s + 2))
        if s >= 2:
            plan.append(("out", s - 2))
    return plan + [("value", n - 1), ("out", n - 2), ("out", n - 1)]


def blocks_of(x, t):
    first = max(0, t - LEFT // 2) if x == 0 else 0
    return first, t + 1 - first


def attn_phase(nc, at, ident, selb, acc, proj, urel, caches, oT_hi, oT_lo, outs):
    tag = "t"
    proj_v = proj.rearrange("(t p) n -> p t n", p=P)
    FW = H * HD
    with ExitStack() as ctx:
        sem = lambda n: ctx.enter_context(nc.semaphore(f"{tag}_{n}"))
        keep = Plan(nc, tag, at)
        keep.at += 4 * SEQ
        sc = keep("sc", [P, 3, D], F32)
        m8 = keep("m8", [P, 8], F32)
        at_bias = keep.at
        bias = keep("bias", [P, H, BAND], F32)
        pT = keep("pT", [P, 2, D], F32)
        osb = keep("osb", [P, 2, FW], F32)
        small = keep("small", [P, 2, 8], F32)
        sums = keep("sums", [P, 2, H], F32)
        rec = keep("rec", [P, 2, H], F32)
        flip_s = keep("flip_s", [P, H, DEC_S], F32)
        at_big = keep.at
        rows = keep("rows", [P, 2, FW], F32)
        qT = keep("qT", [P, 2, H, P], F32)
        kT, v = [None, None], [None, None]
        kT[0], v[0] = keep("kT0", [P, HT, SEQ], F32), keep("v0", [P, NP, FW], F32)
        rel = Plan(nc, tag, keep.at)
        kT[1], v[1] = keep("kT1", [P, HT, SEQ], F32), keep("v1", [P, NP, FW], F32)
        raw = rel("raw", [P, H, NEAR], F32)
        flip = rel("flip", [P, P], F32)
        assert rel.at <= keep.at
        assert keep.at <= SBUF_END - 2 * KT * ROWS * 4
        smp = Plan(nc, tag, at_big)
        kc = [smp(f"kc{i}", [P, PAST // P, FW], F32) for i in range(2)]
        vc = [smp(f"vc{i}", [P, PAST // P, FW], F32) for i in range(2)]
        vn = [smp(f"vn{i}", [DEC_S, FW], F32) for i in range(2)]
        kTs = [smp(f"kTs{i}", [P, HT, KS], F32) for i in range(2)]
        bd = [smp(f"bd{i}", [P, 5 * P], F32) for i in range(2)]
        snT = smp("snT", [P, 2, 2, HT, P], F32)
        late = Plan(nc, tag, at_bias)
        srow = late("srow", [P, 2, 2, FW], F32)
        raw_s = late("raw_s", [P, KS - FAR], F32)
        bias_s = late("bias_s", [P, KS], F32)
        rep = late("rep", [P, DEC_B, H, DEC_S], BF16)
        assert late.at <= at_bias + H * BAND * 4
        assert smp.at <= keep.at
        ps = [ctx.enter_context(nc.psum_tensor(f"{tag}_ps{i}", [P, D], F32)) for i in range(2)]
        pt = [ctx.enter_context(nc.psum_tensor(f"{tag}_pt{i}", [P, 512], F32)) for i in range(2)]
        po = ctx.enter_context(nc.psum_tensor(f"{tag}_po", [P, 512], F32))
        pm = ctx.enter_context(nc.psum_tensor(f"{tag}_pm", [P, 512], F32))

        s_bias, s_far, s_sel = sem("bias_loaded"), sem("far_bias_ready"), sem("selection_step")
        s_flip, s_flipped = sem("flip_ready"), sem("bias_flipped")
        s_be = [sem("bias_read_dve"), sem("bias_read_act")]
        s_mask, s_rep, s_zero = sem("bias_masked"), sem("rep_ready"), sem("zeroed")
        s_row = sem("rows_loaded")
        s_v = [sem(f"v_loaded{i}") for i in range(2)]
        s_out = sem("outputs_stored")
        s_mf, s_ma, s_ml = sem("misc_filled"), sem("misc_read_act"), sem("misc_read_dve")
        s_s, s_mx, s_sc, s_p = sem("scores_done"), sem("max_ready"), sem("scores_ready"), sem("exp_ready")
        s_t = sem("turned")
        s_pt = [sem("turned_read_act"), sem("turned_read_dve")]
        s_o, s_rc, s_os = sem("value_done"), sem("reciprocal"), sem("out_scaled")
        s_kt = sem("new_keys_placed")
        s_bd = sem("block_queries")
        s_kc, s_vc = [sem(f"kc_loaded{i}") for i in range(2)], [sem(f"vc_loaded{i}") for i in range(2)]
        s_sr = sem("sample_rows_loaded")

        heads, plan = attn_plan()
        NH = len(heads)
        NTT = 2 * NP
        units, u0 = {}, 0
        for g, (x, t, h) in enumerate(heads):
            n = blocks_of(x, t)[1]
            units[g] = [(u0 + j, 4 * j, min(4, n - 4 * j)) for j in range(-(-n // 4))]
            u0 += len(units[g])
        items = [(x, b) for x in range(2) for b in range(DEC_B)]
        kunits, punits = {}, {}
        splan = [(e, s, items[s][0], items[s][1]) for e, s in sample_plan(len(items))]
        for e, s, _, _ in splan:
            if e in ("keys", "turn"):
                (kunits if e == "keys" else punits)[s] = list(range(u0, u0 + (HT if e == "keys" else 2)))
                u0 += HT if e == "keys" else 2
        misc, m0, lo_n = {}, 0, {}
        nlo = 0
        free_at = {}
        def use(key, by_dve):
            nonlocal m0, nlo
            misc[key] = m0
            m0 += 1
            nlo += by_dve
            lo_n[key] = nlo
        order = []
        for e in plan:
            if e[0] == "prep":
                order += [(("k",) + e[1:], 0), (("q",) + e[1:], 0)]
            elif e[0] == "out":
                order += [(("o",) + e[1:], 1)]
        order += [((("sk", "sq")[j], x), 0) for x in range(2) for j in range(2)]
        order += [(("so", s), 1) for s in range(len(items))]
        for key, by in order:
            use(key, by)
        keys_in_order = [k for k, _ in order]

        def sc_of(g, a, b):
            return sc[:, g % 3, a:b]

        def in_halves(a):
            return a.rearrange("p (h c) -> p h c", h=2)

        def both_halves(g):
            return in_halves(ps[g % 2][:])[:, :, 0:KS // 2]

        def pe_misc(pe, key):
            m = misc[key]
            if m:
                prev = keys_in_order[m - 1]
                pe.wait_ge(s_ma, m)
                if lo_n[prev]:
                    pe.wait_ge(s_ml, lo_n[prev])
            return pm

        block = ctx.enter_context(nc.Block())

        @block.sync
        def _(sp):
            tiles = [(x, t) for x in range(2) for t in range(NP)]

            def rows_of(n):
                x, t = tiles[n]
                if n:
                    sp.wait_ge(s_mf, misc[("q",) + tiles[n - 1]] + 1)
                c = x * N_QKV
                sp.dma_start(rows[:, 0, :], proj_v[:, t, c + FW:c + 2 * FW]).then_inc(s_row, 16)
                sp.dma_start(rows[:, 1, :], proj_v[:, t, c:c + FW]).then_inc(s_row, 16)

            def values(x):
                sp.dma_start(v[x][:], proj_v[:, 0:NP, x * N_QKV + 2 * FW:x * N_QKV + 3 * FW]).then_inc(s_v[x], 16)

            rows_of(0)
            u = urel
            sp.dma_start(raw[:], bass.AP(u.tensor, FAR, [[1, P], [6 * P, H], [1, NEAR]])).then_inc(s_bias, 16)
            values(0)
            rows_of(1)
            sp.wait_ge(s_flipped, 2)
            values(1)
            for n in range(2, len(tiles)):
                rows_of(n)
            for dst, c, r0, r1 in outs:
                sp.dma_start(dst, proj[r0:r1, c:c + FW]).then_inc(s_out, 16)
            sp.wait_ge(s_t, units[NH - 1][-1][0] + 1)
            sp.wait_ge(s_o, NH)
            for h in range(H):
                sp.dma_start(raw_s[h * DEC_S:(h + 1) * DEC_S, :],
                             bass.AP(u.tensor, 6 * P * h + FAR + P - DEC_S, [[1, DEC_S], [1, KS - FAR]])).then_inc(s_bias, 16)
            for x in range(2):
                for j in range(2):
                    sp.dma_start(srow[:, x, j, :], proj_v[:, NP, x * N_QKV + (1 - j) * FW:x * N_QKV + (2 - j) * FW]).then_inc(s_sr, 16)

            def cached_keys(s):
                x, b = items[s]
                if s >= 2:
                    sp.wait_ge(s_t, kunits[s - 2][-1] + 1)
                sp.dma_start(kc[s % 2][:], caches[x][0][0, b].rearrange("(k p) h d -> p k (h d)", p=P)).then_inc(s_kc[s % 2], 16)

            def cached_values(s):
                x, b = items[s]
                if s >= 2:
                    sp.wait_ge(s_o, NH + s - 1)
                sp.dma_start(vc[s % 2][:], caches[x][1][0, b].rearrange("(k p) h d -> p k (h d)", p=P)).then_inc(s_vc[s % 2], 16)
                r = SEQ + b * DEC_S
                sp.dma_start(vn[s % 2][:], proj[r:r + DEC_S, x * N_QKV + 2 * FW:x * N_QKV + 3 * FW]).then_inc(s_vc[s % 2], 16)

            cached_keys(0)
            for s in range(len(items)):
                if s + 1 < len(items):
                    cached_keys(s + 1)
                cached_values(s)
            sp.wait_ge(s_out, 16 * len(outs))

        @block.gpsimd
        def _(pool):
            pool.memset(flip[:], 0.0).then_inc(s_flip, 1)
            pool.memset(flip_s[:], 0.0).then_inc(s_flip, 1)
            pool.wait_ge(s_flip, 2)
            pool.affine_select(out=flip[:], in_=flip[:], compare_op=ALU.not_equal, fill=1.0, base=1 - P,
                               pattern=[[1, P]], channel_multiplier=1).then_inc(s_flip, 1)
            pool.affine_select(out=flip_s[:], in_=flip_s[:], compare_op=ALU.not_equal, fill=1.0, base=1 - DEC_S,
                               pattern=[[-DEC_S, H], [1, DEC_S]], channel_multiplier=1).then_inc(s_flip, 1)
            pool.memset(qT[:], 0.0).then_inc(s_zero, 1)
            for i in range(2):
                pool.wait_ge(s_be[i], 1)
            pool.tensor_copy(bias[:, :, 0:FAR], bias[:, :, FAR:FAR + 1].broadcast_to([P, H, FAR])).then_inc(s_far, 1)
            pool.wait_ge(s_far, 1)
            pool.memset(bias[CHUNK:P, :, 0:CHUNK], NEG).then_inc(s_far, 1)
            pool.wait_ge(s_o, NH)
            pool.wait_ge(s_mf, misc[("o", 1, NP - 1)] + 1)
            for i in range(2):
                pool.memset(bd[i][:], 0.0).then_inc(s_zero, 1)
            pool.memset(rep[:], 0.0).then_inc(s_rep, 1)
            pool.wait_ge(s_rep, 1)
            pool.affine_select(out=rep[:], in_=rep[:], compare_op=ALU.not_equal, fill=1.0, base=0,
                               pattern=[[-DEC_S, DEC_B], [0, H], [-1, DEC_S]], channel_multiplier=1).then_inc(s_rep, 1)
            for s, (x, b) in enumerate(items):
                bs = slice(b * DEC_S, (b + 1) * DEC_S)
                pool.wait_ge(s_ma, misc[("sq", x)] + 1)
                if s >= 2:
                    pool.wait_ge(s_s, NH + s - 1)
                else:
                    pool.wait_ge(s_zero, 3)
                bv = bd[s % 2][:].rearrange("p (f c) -> p f c", c=5 * DEC_S * 2)
                for j, (dst, src) in enumerate(((kTs[s % 2][:, :, PAST:KS], snT[:, x, 0, :, bs]),
                                                (bv[0:HD, :, 0:DEC_S], snT[0:HD, x, 1, :, bs]),
                                                (bv[HD:P, :, DEC_S:2 * DEC_S], snT[HD:P, x, 1, :, bs]))):
                    pool.tensor_copy(dst, src).then_inc(s_bd, 1)
                    pool.wait_ge(s_bd, 3 * s + j + 1)

        def diag(r):
            a = pm[r * HD:(r + 1) * HD, 0:DEC_S]
            return bass.AP(a.tensor, a.offset + r * DEC_S, [list(a.ap[0]), [P + 2 * DEC_S, HT], [1, DEC_S]])

        def dve_out(dve, key, n):
            dve.reciprocal(rec[:, n % 2, :], sums[:, n % 2, :]).then_inc(s_rc, 1)
            dve.wait_ge(s_rc, n + 1)
            if n >= 2:
                dve.wait_ge(s_mf, misc[("o",) + tiles_of[n - 2]] + 1)
            dve.tensor_tensor(osb[:, n % 2, :].rearrange("p (h d) -> p h d", d=HD), po[:].rearrange("p (h d) -> p h d", d=HD),
                              rec[:, n % 2, :].unsqueeze(2).broadcast_to([P, H, HD]), ALU.mult).then_inc(s_os, 1)

        tiles_of = [(x, t) for x in range(2) for t in range(NP)]

        @block.vector
        def _(dve):
            dve.wait_ge(s_flipped, 1)
            dve.tensor_copy(bias[:, 0:H // 2, FAR:BAND], ps[0][:].rearrange("p (h c) -> p h c", c=NEAR)).then_inc(s_be[0], 1)
            dve.wait_ge(s_be[0], 1)
            dve.wait_ge(s_be[1], 1)
            dve.memset(bias[0:CHUNK, :, BAND - CHUNK:BAND], NEG).then_inc(s_mask, 1)
            dve.wait_ge(s_mask, 1)

            n_sel = [0]
            halves = [(i, j) for i in range(EARLY, TOPK // 8) for j in range(2)]

            def select_half():
                i, j = halves.pop(0)
                a = acc[:]
                if n_sel[0]:
                    dve.wait_ge(s_sel, n_sel[0])
                if j == 0:
                    dve.max(m8[:], a).then_inc(s_sel, 1)
                else:
                    dve.match_replace(out=a, in_to_replace=m8[:], in_values=a, imm_value=GONE).then_inc(s_sel, 1)
                n_sel[0] += 1
                if (i, j) == (TOPK // 8 - 1, 1):
                    dve.wait_ge(s_sel, n_sel[0])
                    dve.tensor_scalar(selb[:, SELB_AT[NP - 1]:SELB_AT[NP]], a, GONE, NEG, ALU.not_equal, ALU.mult).then_inc(s_sel, 1)
                    n_sel[0] += 1

            todo = sum(blocks_of(x, t)[1] for x, t, h in heads[:heads.index((1, NP - 1, 0))])
            done, n_halves = 0, len(halves)
            for e in plan:
                if e[0] == "score":
                    g = e[1]
                    x, t, h = heads[g]
                    n = P * blocks_of(x, t)[1]
                    if (x, t, h) == (1, NP - 1, 0):
                        assert not halves
                        dve.wait_ge(s_sel, n_sel[0])
                    if (x, t, h) == (0, 2, 0):
                        dve.wait_ge(s_far, 2)
                    dve.wait_ge(s_s, g + 1)
                    if g >= 3:
                        dve.wait_ge(s_t, units[g - 3][-1][0] + 1)
                    if g >= 4:
                        dve.wait_ge(s_p, g - 3)
                    b = bias[:, h, BAND - n:BAND] if x == 0 else selb[:, SELB_AT[t]:SELB_AT[t] + n]
                    dve.tensor_tensor_reduce(out=sc_of(g, 0, n), in0=ps[g % 2][:, 0:n], in1=b, scale=1.0, scalar=GONE,
                                             op0=ALU.add, op1=ALU.max, accum_out=small[:, 0, g % 4:g % 4 + 1]).then_inc(s_mx, 1)
                    dve.wait_ge(s_mx, g + 1)
                    dve.tensor_scalar(small[:, 1, g % 4:g % 4 + 1], small[:, 0, g % 4:g % 4 + 1], -1.0, None, ALU.mult).then_inc(s_sc, 1)
                    done += n // P
                    while halves and (n_halves - len(halves) + 1) * todo <= n_halves * done:
                        select_half()
                elif e[0] == "turn":
                    for u, b0, nb in units[e[1]]:
                        if u % 2:
                            dve.wait_ge(s_t, u + 1)
                            if e[1] >= 2:
                                dve.wait_ge(s_o, e[1] - 1)
                            dve.tensor_copy(pT[:, e[1] % 2, b0 * P:(b0 + nb) * P], pt[1][:, 0:nb * P]).then_inc(s_pt[1], 1)
                elif e[0] == "value" and heads[e[1]][2] == H - 1:
                    n = e[1] // H
                    dve.wait_ge(s_o, e[1] + 1)
                    dve_out(dve, None, n)
                elif e[0] == "out":
                    m = misc[("o",) + e[1:]]
                    ts = slice(e[2] * P, (e[2] + 1) * P)
                    dve.wait_ge(s_ma, m + 1)
                    fs = slice(e[1] * HT, (e[1] + 1) * HT)
                    dve.tensor_tensor(oT_lo[:, fs, ts], pm[:].rearrange("p (f c) -> p f c", c=P),
                                      oT_hi[:, fs, ts].bitcast(F32), ALU.subtract).then_inc(s_ml, 1)
            dve.wait_ge(s_flipped, 3)
            dve.tensor_copy(bias_s[:, FAR:KS], ps[0][:, 0:KS - FAR]).then_inc(s_be[0], 1)
            dve.wait_ge(s_be[0], 2)
            dve.tensor_copy(bias_s[:, 0:FAR], bias_s[:, FAR:FAR + 1].broadcast_to([P, FAR])).then_inc(s_mask, 1)
            dve.wait_ge(s_mask, 2)
            for e, s, x, b in splan:
                g, n = NH + s, NTT + s
                if e == "keys":
                    for f, u in enumerate(kunits[s]):
                        if u % 2:
                            dve.wait_ge(s_t, u + 1)
                            dve.tensor_copy(kTs[s % 2][:, f, 0:PAST], pt[1][:]).then_inc(s_pt[1], 1)
                elif e == "score":
                    dve.wait_ge(s_s, g + 1)
                    if x == 0:
                        dve.wait_ge(s_t, (units[NH - 3 + s][-1][0] if s < 3 else punits[s - 3][-1]) + 1)
                        dve.tensor_tensor_reduce(out=in_halves(sc_of(g, 0, KS)), in0=both_halves(g), in1=in_halves(bias_s[:]), scale=1.0, scalar=GONE,
                                                 op0=ALU.add, op1=ALU.max, accum_out=small[:, 0, g % 4:g % 4 + 1]).then_inc(s_mx, 1)
                    else:
                        dve.tensor_reduce(out=small[:, 0, g % 4:g % 4 + 1], in_=both_halves(g), axis=AX.XY, op=ALU.max).then_inc(s_mx, 1)
                    dve.wait_ge(s_mx, g + 1)
                    dve.tensor_scalar(small[:, 1, g % 4:g % 4 + 1], small[:, 0, g % 4:g % 4 + 1], -1.0, None, ALU.mult).then_inc(s_sc, 1)
                elif e == "turn":
                    for j, u in enumerate(punits[s]):
                        if u % 2:
                            dve.wait_ge(s_t, u + 1)
                            dve.wait_ge(s_o, g - 1)
                            if j == 0:
                                dve.tensor_copy(pT[:, s % 2, 0:PAST], pt[1][:]).then_inc(s_pt[1], 1)
                            else:
                                dve.tensor_copy(pT[0:DEC_S, s % 2, PAST:PAST + P], pt[1][0:DEC_S, 0:P]).then_inc(s_pt[1], 1)
                elif e == "value":
                    dve.wait_ge(s_o, g + 1)
                    dve.reciprocal(rec[:, n % 2, 0:1], sums[:, 0, s % H:s % H + 1]).then_inc(s_rc, 1)
                    dve.wait_ge(s_rc, n + 1)
                    if s >= 2:
                        dve.wait_ge(s_mf, misc[("so", s - 2)] + 1)
                    dve.tensor_scalar(osb[:, n % 2, :], po[:], rec[:, n % 2, 0:1], None, ALU.mult).then_inc(s_os, 1)
                else:
                    m = misc[("so", s)]
                    dve.wait_ge(s_ma, m + 1)
                    cs = slice(SEQ + b * DEC_S, SEQ + (b + 1) * DEC_S)
                    fs = slice(x * HT, (x + 1) * HT)
                    for r in range(2):
                        i = dve.tensor_tensor(oT_lo[r * HD:(r + 1) * HD, fs, cs], diag(r),
                                              oT_hi[r * HD:(r + 1) * HD, fs, cs].bitcast(F32), ALU.subtract)
                    i.then_inc(s_ml, 1)

        def act_exp(act, g, n, src, total):
            act.wait_ge(s_sc, g + 1)
            act.activation(sc_of(g, 0, n) if len(src.shape) == 2 else in_halves(sc_of(g, 0, n)), src, ACT.Exp, bias=small[:, 1, g % 4:g % 4 + 1], accum_out=total).then_inc(s_p, 1)

        @block.scalar
        def _(act):
            act.wait_ge(s_zero, 1)
            for e in plan:
                if e[0] == "prep":
                    x, t = e[1:]
                    n = x * NP + t
                    act.wait_ge(s_mf, misc[("k", x, t)] + 1)
                    act.activation(kT[x][:, :, t * P:(t + 1) * P], pm[:].rearrange("p (f c) -> p f c", c=P), ACT.Copy).then_inc(s_ma, 1)
                    act.wait_ge(s_mf, misc[("q", x, t)] + 1)
                    if n >= 2:
                        act.wait_ge(s_s, (n - 1) * H)
                    for r in range(2):
                        i = act.activation(qT[r * HD:(r + 1) * HD, n % 2, r::2, :],
                                           pm[r * HD:(r + 1) * HD, :].rearrange("p (f c) -> p f c", c=P), ACT.Copy, scale=HD ** -0.5)
                    i.then_inc(s_ma, 1)
                    if n == 0:
                        act.wait_ge(s_flipped, 2)
                        act.activation(bias[:, H // 2:H, FAR:BAND], ps[1][:].rearrange("p (h c) -> p h c", c=NEAR), ACT.Copy).then_inc(s_be[1], 1)
                elif e[0] == "score":
                    g = e[1]
                    x, t, h = heads[g]
                    n = P * blocks_of(x, t)[1]
                    if h == 0 and g >= 2 * H:
                        act.wait_ge(s_rc, g // H - 1)
                    act_exp(act, g, n, sc_of(g, 0, n), sums[:, (g // H) % 2, h:h + 1])
                elif e[0] == "turn":
                    for u, b0, nb in units[e[1]]:
                        if u % 2 == 0:
                            act.wait_ge(s_t, u + 1)
                            if e[1] >= 2:
                                act.wait_ge(s_o, e[1] - 1)
                            act.activation(pT[:, e[1] % 2, b0 * P:(b0 + nb) * P], pt[0][:, 0:nb * P], ACT.Copy).then_inc(s_pt[0], 1)
                elif e[0] == "out":
                    m = misc[("o",) + e[1:]]
                    act.wait_ge(s_mf, m + 1)
                    act.activation(oT_hi[:, e[1] * HT:(e[1] + 1) * HT, e[2] * P:(e[2] + 1) * P],
                                   pm[:].rearrange("p (f c) -> p f c", c=P), ACT.Copy).then_inc(s_ma, 1)
            for x in range(2):
                for j in range(2):
                    act.wait_ge(s_mf, misc[(("sk", "sq")[j], x)] + 1)
                    act.activation(snT[:, x, j, :, :], pm[:].rearrange("p (f c) -> p f c", c=P), ACT.Copy,
                                   scale=HD ** -0.5 if j else 1.0).then_inc(s_ma, 1)
            act.wait_ge(s_rc, NTT)
            for e, s, x, b in splan:
                g = NH + s
                if e == "keys":
                    for f, u in enumerate(kunits[s]):
                        if u % 2 == 0:
                            act.wait_ge(s_t, u + 1)
                            act.activation(kTs[s % 2][:, f, 0:PAST], pt[0][:], ACT.Copy).then_inc(s_pt[0], 1)
                elif e == "score":
                    if s >= H:
                        act.wait_ge(s_rc, NTT + s - H + 1)
                    if x == 1:
                        act.wait_ge(s_t, punits[s - 3][-1] + 1)
                    act_exp(act, g, KS, sc_of(g, 0, KS) if x == 0 else both_halves(g), sums[:, 0, s % H:s % H + 1])
                elif e == "turn":
                    for j, u in enumerate(punits[s]):
                        if u % 2 == 0:
                            act.wait_ge(s_t, u + 1)
                            act.wait_ge(s_o, g - 1)
                            if j == 0:
                                act.activation(pT[:, s % 2, 0:PAST], pt[0][:], ACT.Copy).then_inc(s_pt[0], 1)
                            else:
                                act.activation(pT[0:DEC_S, s % 2, PAST:PAST + P], pt[0][0:DEC_S, 0:P], ACT.Copy).then_inc(s_pt[0], 1)
                elif e == "out":
                    act.wait_ge(s_mf, misc[("so", s)] + 1)
                    cs = slice(SEQ + b * DEC_S, SEQ + (b + 1) * DEC_S)
                    for r in range(2):
                        i = act.activation(oT_hi[r * HD:(r + 1) * HD, x * HT:(x + 1) * HT, cs], diag(r), ACT.Copy)
                    i.then_inc(s_ma, 1)

        def evacs(u):
            return u // 2 + 1

        def pe_turn(pe, u, blocks):
            if u >= 2:
                pe.wait_ge(s_pt[u % 2], evacs(u - 2))
            for dst, src in blocks:
                last = pe.transpose(dst, src, ident[:])
            last.then_inc(s_t, 1)

        def pe_rows(pe, key, src):
            out = pe_misc(pe, key)
            for f in range(HT):
                last = pe.transpose(out[:, f * P:(f + 1) * P], src[:, f * P:(f + 1) * P], ident[:])
            last.then_inc(s_mf, 1)

        @block.tensor
        def _(pe):
            for e in plan:
                if e[0] == "prep":
                    x, t = e[1:]
                    n = x * NP + t
                    pe.wait_ge(s_row, 32 * (n + 1))
                    pe_rows(pe, ("k", x, t), rows[:, 0, :])
                    pe_rows(pe, ("q", x, t), rows[:, 1, :])
                    if n == 0:
                        pe.wait_ge(s_bias, 16)
                        pe.wait_ge(s_flip, 4)
                        for i in range(2):
                            for j in range(2):
                                h2 = 4 * i + 2 * j
                                last = pe.matmul(ps[i][:, j * 512:(j + 1) * 512], flip[:],
                                                 raw[:, h2:h2 + 2, :].rearrange("p h c -> p (h c)"), start=True, stop=True)
                            last.then_inc(s_flipped, 1)
                        for i in range(2):
                            pe.wait_ge(s_be[i], 1)
                elif e[0] == "score":
                    g = e[1]
                    x, t, h = heads[g]
                    k0, nb = blocks_of(x, t)
                    if h == 0:
                        pe.wait_ge(s_ma, misc[("q", x, t)] + 1)
                    if g >= 2:
                        pe.wait_ge(s_mx, g - 1)
                    for c in range(0, nb, 4):
                        c1 = min(c + 4, nb)
                        last = pe.matmul(ps[g % 2][:, c * P:c1 * P], qT[:, (x * NP + t) % 2, h, :],
                                         kT[x][:, h // 2, (k0 + c) * P:(k0 + c1) * P], start=True, stop=True)
                    last.then_inc(s_s, 1)
                elif e[0] == "turn":
                    g = e[1]
                    pe.wait_ge(s_p, g + 1)
                    for u, b0, nb in units[g]:
                        pe_turn(pe, u, [(pt[u % 2][:, j * P:(j + 1) * P], sc_of(g, (b0 + j) * P, (b0 + j + 1) * P)) for j in range(nb)])
                elif e[0] == "value":
                    g = e[1]
                    x, t, h = heads[g]
                    k0, nb = blocks_of(x, t)
                    if t == 0 and h == 0:
                        pe.wait_ge(s_v[x], 16)
                    if h == 0 and g:
                        pe.wait_ge(s_os, g // H)
                    for u, _, _ in units[g]:
                        pe.wait_ge(s_pt[u % 2], evacs(u))
                    for j in range(nb):
                        last = pe.matmul(po[:, h * HD:(h + 1) * HD], pT[:, g % 2, j * P:(j + 1) * P],
                                         v[x][:, k0 + j, h * HD:(h + 1) * HD], start=j == 0, stop=j == nb - 1)
                    last.then_inc(s_o, 1)
                elif e[0] == "out":
                    n = e[1] * NP + e[2]
                    pe.wait_ge(s_os, n + 1)
                    pe_rows(pe, ("o",) + e[1:], osb[:, n % 2, :])
            pe.wait_ge(s_bias, 16 * (H + 1))
            pe.wait_ge(s_mx, NH)
            pe.matmul(ps[0][:, 0:KS - FAR], flip_s[:].rearrange("p h q -> p (h q)"), raw_s[:], start=True, stop=True).then_inc(s_flipped, 1)
            pe.wait_ge(s_be[0], 2)
            pe.wait_ge(s_sr, 64)
            for x in range(2):
                for j in range(2):
                    pe_rows(pe, (("sk", "sq")[j], x), srow[:, x, j, :])

            for e, s, x, b in splan:
                g = NH + s
                if e == "keys":
                    pe.wait_ge(s_kc[s % 2], 16 * (s // 2 + 1))
                    for f, u in enumerate(kunits[s]):
                        pe_turn(pe, u, [(pt[u % 2][:, k * P:(k + 1) * P], kc[s % 2][:, k, f * P:(f + 1) * P]) for k in range(PAST // P)])
                elif e == "score":
                    pe.wait_ge(s_bd, 3 * s + 3)
                    for u in kunits[s][-2:]:
                        pe.wait_ge(s_pt[u % 2], evacs(u))
                    pe.wait_ge(s_mx, g - 1)
                    if x == 1:
                        pe.wait_ge(s_p, g - 1)
                        if b == 0:
                            pe.wait_ge(s_rep, 2)
                    for c0, c1 in ((0, KS // 2), (KS // 2, KS)):
                        out = ps[g % 2][:, c0 // (KS // 2) * 512:c0 // (KS // 2) * 512 + KS // 2]
                        for f in range(HT):
                            last = pe.matmul(out, bd[s % 2][:, f * P:(f + 1) * P], kTs[s % 2][:, f, c0:c1],
                                             start=f == 0, stop=f == HT - 1 and x == 0)
                        if x == 1:
                            last = pe.matmul(out, rep[:, b, :, :].rearrange("p h q -> p (h q)"),
                                             selb[:, SELB_AT[NP] + c0:SELB_AT[NP] + c1], start=False, stop=True)
                    last.then_inc(s_s, 1)
                elif e == "turn":
                    pe.wait_ge(s_p, g + 1)
                    u = punits[s][0]
                    pe_turn(pe, u, [(pt[u % 2][:, k * P:(k + 1) * P], sc_of(g, k * P, (k + 1) * P)) for k in range(PAST // P)])
                    u = punits[s][1]
                    pe_turn(pe, u, [(pt[u % 2][0:DEC_S, 0:P], sc_of(g, PAST, KS))])
                elif e == "value":
                    pe.wait_ge(s_os, NTT + s)
                    pe.wait_ge(s_vc[s % 2], 32 * (s // 2 + 1))
                    for u in punits[s]:
                        pe.wait_ge(s_pt[u % 2], evacs(u))
                    for k in range(PAST // P):
                        pe.matmul(po[:], pT[:, s % 2, k * P:(k + 1) * P], vc[s % 2][:, k, :], start=k == 0, stop=False)
                    pe.matmul(po[:], pT[0:DEC_S, s % 2, PAST:PAST + P], vn[s % 2][:], start=False, stop=True).then_inc(s_o, 1)
                else:
                    pe.wait_ge(s_os, NTT + s + 1)
                    pe_rows(pe, ("so", s), osb[:, (NTT + s) % 2, :])

def wo_phase(nc, at, x_sb, x_mid, w_out, T, st, ident, g_next):
    tag = "o"
    w_v = w_out.rearrange("a (k p) n -> p (a k) n", p=P)
    with ExitStack() as ctx:
        sem = lambda n: ctx.enter_context(nc.semaphore(f"{tag}_{n}"))
        keep = Plan(nc, tag, at)
        w_hi = [keep(f"w_hi{k}", [P, D], F32R) for k in range(KT)]
        w_lo = [keep(f"w_lo{k}", [P, D], F32R) for k in range(KT)]
        raw = [keep(f"raw{i}", [P, D], F32) for i in range(2)]
        after = TileNorm(nc, ctx, tag + "b", at_end(4 * D * 4), st, x_sb, T, ident, g_next)
        assert keep.at <= at_end(4 * D * 4)
        py = [ctx.enter_context(nc.psum_tensor(f"{tag}_py{i}", [P, 512], F32)) for i in range(4)]
        xp = ctx.enter_context(nc.psum_tensor(f"{tag}_xp", [P, 4, 512], F32))
        s_raw = [sem(f"w_loaded{i}") for i in range(2)]
        s_x = [sem(f"x_loaded{t}") for t in range(NT)]
        s_hi, s_lo, s_y, s_acc = sem("w_hi"), sem("w_split"), sem("y_done"), sem("y_added")
        block = ctx.enter_context(nc.Block())

        def x_done(eng, t):
            eng.wait_ge(s_acc, 2 * (t + 1))

        @block.sync
        def _(sp):
            x_v = x_mid.rearrange("(t p) d -> p t d", p=P)
            for k in range(KT):
                if k >= 2:
                    sp.wait_ge(s_lo, k - 1)
                sp.dma_start(raw[k % 2][:], w_v[:, k, :]).then_inc(s_raw[k % 2], 16)
                if k % 2:
                    for t in range(k - 1, min(k + 1 + (k == KT - 1), NT)):
                        sp.dma_start(x_sb[:, t, :], x_v[:, t, :]).then_inc(s_x[t], 16)
            after.load(sp)

        @block.scalar
        def _(act):
            for k in range(KT):
                act.wait_ge(s_raw[k % 2], 16 * (k // 2 + 1))
                act.activation(w_hi[k][:], raw[k % 2][:], ACT.Copy).then_inc(s_hi, 1)
            for t in range(TileNorm.SLOTS):
                after.act(act, t, xp, x_done)

        @block.vector
        def _(dve):
            for k in range(KT):
                dve.wait_ge(s_hi, k + 1)
                dve.tensor_tensor(w_lo[k][:], raw[k % 2][:], w_hi[k][:].bitcast(F32), ALU.subtract).then_inc(s_lo, 1)
            for t in range(TileNorm.SLOTS):
                after.dve_lo(dve, t, xp)
                if t < NT:
                    dve.wait_ge(s_x[t], 16)
                for k in range(2 * t, 2 * t + 2) if t < NT else ():
                    xs = x_sb[:, t, k % 2 * 512:(k % 2 + 1) * 512]
                    dve.wait_ge(s_y, k + 1)
                    dve.tensor_tensor(xs, py[k % 4][:], xs, ALU.add).then_inc(s_acc, 1)
                after.dve(dve, t, x_done)

        @block.tensor
        def _(pe):
            def piece(k, kt):
                t, ns = k // 2, slice(k % 2 * 512, (k % 2 + 1) * 512)
                ts = slice(t * P, (t + 1) * P)
                return three_pass(pe, py[k % 4][:], (T[0][:, kt, ts], T[1][:, kt, ts]),
                                  (w_hi[kt][:, ns], w_lo[kt][:, ns]), kt == 0, kt == KT - 1)

            for kt in range(KT):
                pe.wait_ge(s_lo, kt + 1)
                for k in range(4):
                    last = piece(k, kt)
                    if kt == KT - 1:
                        last.then_inc(s_y, 1)
            after.pe(pe, 0, xp)
            after.pe(pe, 1, xp)
            for t in range(2, TileNorm.SLOTS):
                for k in range(2 * t, 2 * t + 2) if t < NT else ():
                    pe.wait_ge(s_acc, k - 3)
                    for kt in range(KT):
                        last = piece(k, kt)
                    last.then_inc(s_y, 1)
                after.pe(pe, t, xp)


def program(nc, i, o):
    with ExitStack() as outer:
        run_phases(nc, outer, i, o)


def run_phases(nc, outer, i, o):
    plan = Plan(nc, "r", SBUF_START)
    ident = plan("ident", [P, P], F32)
    st = plan("stats", [P, 6, NT], F32)
    at_selb = plan.at
    selb = plan("selb", [P, SELB_AT[NP] + KS], BF16)
    at_x = plan.at
    x_sb = plan("x", [P, NT, D], F32)
    at = plan.at
    late_acc = Plan(nc, "r", at_x)("late_acc", [P, SEQ], F32)
    wi_raw = Plan(nc, "r", at)("wi_raw", [P, KT, N_IDX], F32)
    top = Plan(nc, "r", at_end(0))
    T = top("T_hi", [P, KT, ROWS], F32R), top("T_lo", [P, KT, ROWS], F32R)
    dram = lambda n, s: nc.dram_tensor(n, s, F32, kind="Internal").ap()
    x_mid, proj, urel = dram("x_mid", [ROWS, D]), dram("proj", [ROWS, 2 * N_QKV]), dram("urel", [H, 6 * P])
    xp_v = i["x_prompt"].rearrange("b (t p) d -> p (b t) d", p=P)
    xs_v = i["x_sample"].rearrange("b s d -> (b s) d")

    def load_rows(sp, s_x):
        for t in range(NP):
            sp.dma_start(x_sb[:, t, :], xp_v[:, t, :]).then_inc(s_x[t], 16)
        sp.dma_start(x_sb[:, NP, :], xs_v).then_inc(s_x[NP], 16)

    with ExitStack() as ctx:
        s_id = ctx.enter_context(nc.semaphore("ident_step"))
        block = ctx.enter_context(nc.Block())

        @block.gpsimd
        def _(pool):
            pool.memset(ident[:], 0.0).then_inc(s_id, 1)
            pool.wait_ge(s_id, 1)
            pool.affine_select(out=ident[:], in_=ident[:], compare_op=ALU.not_equal, fill=1.0, base=0,
                               pattern=[[-1, P]], channel_multiplier=1).then_inc(s_id, 1)
            pool.wait_ge(s_id, 2)

    s_raw = outer.enter_context(nc.semaphore("wi_w_loaded"))

    def load_wi(sp):
        sp.dma_start(wi_raw[:], i["w_in"].rearrange("a (k p) n -> p (a k) n", p=P)[:, :, IDX_AT:IDX_AT + N_IDX]).then_inc(s_raw, 16)

    ffn_phase(nc, "f1", at_selb, at, x_sb, T, st, ident, load_rows, i["ffn1_norm"][0], i["ffn1_w_gate"], i["ffn1_w_up"],
              i["ffn1_w_down"], i["mix_norm"][0], load_wi, None)
    wi_phase(nc, at_x, at, x_sb, T, ident, selb, late_acc, wi_raw, s_raw, i["w_in"], i["rel_bias"], urel, i["rope_cos"], i["rope_sin"], i["cache_idx_k"],
             x_mid, proj, o["idx_k_prompt"], o["idx_k_sample"])
    FW = H * HD
    flat = lambda a: a.rearrange("a b s h d -> (a b s) (h d)")
    keep0 = SEQ - min(LEFT * CHUNK, SEQ)
    outs = [(flat(o["a_k_prompt"]), FW, keep0, SEQ), (flat(o["a_v_prompt"]), 2 * FW, keep0, SEQ),
            (flat(o["b_k_prompt"]), N_QKV + FW, 0, SEQ), (flat(o["b_v_prompt"]), N_QKV + 2 * FW, 0, SEQ),
            (flat(o["a_k_sample"]), FW, SEQ, ROWS), (flat(o["a_v_sample"]), 2 * FW, SEQ, ROWS),
            (flat(o["b_k_sample"]), N_QKV + FW, SEQ, ROWS), (flat(o["b_v_sample"]), N_QKV + 2 * FW, SEQ, ROWS)]
    attn_phase(nc, at_x, ident, selb, late_acc, proj, urel,
               ((i["cache_a_k"], i["cache_a_v"]), (i["cache_b_k"], i["cache_b_v"])), *T, outs)
    wo_phase(nc, at, x_sb, x_mid, i["w_out"], T, st, ident, i["ffn2_norm"][0])
    y_p, y_s = o["y_prompt"].rearrange("b s d -> (b s) d"), o["y_sample"].rearrange("b s d -> (b s) d")
    ffn_phase(nc, "f2", at_selb, at, x_sb, T, st, ident, None, None, i["ffn2_w_gate"], i["ffn2_w_up"], i["ffn2_w_down"],
              i["final_norm"], None, lambda t: y_p[t * P:(t + 1) * P, :] if t < NP else y_s)


_INS = ["x_prompt", "x_sample", "cache_a_k", "cache_a_v", "cache_b_k", "cache_b_v", "cache_idx_k",
        "ffn1_norm", "ffn1_w_gate", "ffn1_w_up", "ffn1_w_down", "mix_norm", "w_in", "rel_bias", "w_out",
        "ffn2_norm", "ffn2_w_gate", "ffn2_w_up", "ffn2_w_down", "final_norm"]
_OUTS = [("y_prompt", (1, SEQ, D)), ("y_sample", (DEC_B, DEC_S, D)),
         ("a_k_prompt", (1, 1, min(LEFT * CHUNK, SEQ), H, HD)), ("a_v_prompt", (1, 1, min(LEFT * CHUNK, SEQ), H, HD)),
         ("b_k_prompt", (1, 1, SEQ, H, HD)), ("b_v_prompt", (1, 1, SEQ, H, HD)), ("idx_k_prompt", (1, 1, SEQ, ID)),
         ("a_k_sample", (1, DEC_B, DEC_S, H, HD)), ("a_v_sample", (1, DEC_B, DEC_S, H, HD)),
         ("b_k_sample", (1, DEC_B, DEC_S, H, HD)), ("b_v_sample", (1, DEC_B, DEC_S, H, HD)),
         ("idx_k_sample", (1, DEC_B, DEC_S, ID))]


def rope_tables():
    half = HD // 2
    inv = np.power(np.float32(10000.0), -np.arange(half, dtype=np.float32) / np.float32(half)).astype(np.float32)
    pos = np.concatenate([np.arange(SEQ), PAST + np.tile(np.arange(DEC_S), DEC_B)]).astype(np.float32)
    angle = (pos[:, None] * inv[None, :]).astype(np.float32)
    return np.cos(angle), np.sin(angle)


def kernel(**inputs):
    import concourse.bacc as _bacc
    from concourse.bass_utils import run_bass_kernel_spmd as _run

    nc = _bacc.Bacc("TRN2", target_bir_lowering=False, num_devices=1)
    arrays, ins, outs = {}, {}, {}
    for name in _INS:
        a = np.ascontiguousarray(inputs[name])
        arrays[f"in_{name}"] = a
        ins[name] = nc.dram_tensor(f"in_{name}", a.shape, mybir.dt.from_np(a.dtype), kind="ExternalInput").ap()
    for name, a in zip(("rope_cos", "rope_sin"), rope_tables()):
        arrays[f"in_{name}"] = a
        ins[name] = nc.dram_tensor(f"in_{name}", a.shape, F32, kind="ExternalInput").ap()
    for name, shape in _OUTS:
        outs[name] = nc.dram_tensor(f"out_{name}", shape, F32, kind="ExternalOutput").ap()
    program(nc, ins, outs)
    r = _run(nc, [arrays], core_ids=[0])
    return tuple(r.results[0][f"out_{name}"] for name, _ in _OUTS)
```

```python
from contextlib import ExitStack

import numpy as np

import concourse.bass as bass
from concourse import mybir

F32 = mybir.dt.float32
F32R = mybir.dt.float32r
BF16 = mybir.dt.bfloat16
ALU = mybir.AluOpType
ACT = mybir.ActivationFunctionType
AX = mybir.AxisListType

P = 128
D = 1024
KT = D // P
SEQ, DEC_B, DEC_S, PAST = 1024, 8, 16, 512
NP = SEQ // P
NT = NP + 1
ROWS = NT * P
FF = 2816
FB = 256
FSTEPS = FF // FB
CH = 3
NCH = NT // CH
CW = CH * P
H, HD = 8, 64
HT = H * HD // P
CHUNK, LEFT = 64, 8
IH, ID = 8, 32
TOPK = 256
SEL_S = min(TOPK, (PAST + DEC_S) // 4)
MAXREL = 128
BAND = LEFT * CHUNK + P
KS = PAST + DEC_S
N_QKV = 3 * H * HD
N_IDX = IH * ID + ID + IH
EPS = 1e-6
NEG = -1.0e30
GONE = -3.0e38
UNSEEN = -2.0e38
FIRST = 3.0e38


SBUF_START, SBUF_END = 16512, 229344


class Plan:

    def __init__(self, nc, tag, at):
        self.nc, self.tag, self.at = nc, tag, at

    def __call__(self, name, shape, dtype):
        size = int(np.prod(shape[1:])) * mybir.dt.size(dtype)
        t = self.nc.alloc_sbuf_tensor_at(f"{self.tag}_{name}", shape, dtype, offset=self.at)
        self.at += -(-size // 32) * 32
        assert self.at <= SBUF_END, (self.tag, name, self.at - SBUF_END)
        return t


def at_end(size):
    return SBUF_END - 2 * KT * ROWS * 4 - size


class TileNorm:
    SLOTS = NT + 5

    def __init__(self, nc, ctx, tag, at, st, x_sb, xT, ident, g_dram, y=None):
        self.x_sb, self.xT, self.ident, self.g_dram, self.st, self.y = x_sb, xT, ident, g_dram, st, y
        place = Plan(nc, tag, at)
        self.xn = place("xn", [P, 2, D], F32)
        self.g_bc = place("g", [P, D], F32)
        self.junk = place("junk", [P, D], F32)
        sem = lambda n: ctx.enter_context(nc.semaphore(f"{tag}_{n}"))
        self.s_g, self.s_ss, self.s_v = sem("g_loaded"), sem("squares_summed"), sem("mean_ready")
        self.s_sd, self.s_ch, self.s_xn = sem("root_ready"), sem("newton_step"), sem("row_normed")
        if not y:
            self.s_tr, self.s_hi, self.s_lo = sem("transposed"), sem("hi_ready"), sem("lo_ready")
        self.s_out = [sem(f"row_stored{i}") for i in range(len(y))] if y else None

    SS, V, SD, R, A, B = range(6)

    def xp_of(self, xp, t):
        return xp[:, 2 * (t % 2):2 * (t % 2) + 2, :].rearrange("p b c -> p (b c)")

    def load(self, sp):
        sp.dma_start(self.g_bc[:], self.g_dram.partition_broadcast(P)).then_inc(self.s_g, 16)

    def act(self, act, t, xp, x_ready):
        st, col = self.st, lambda k, t: self.st[:, k, t:t + 1]
        if not self.y and 0 <= t - 4 < NT:
            u = t - 4
            act.wait_ge(self.s_tr, u + 1)
            act.activation(self.xT[0][:, :, u * P:(u + 1) * P],
                           self.xp_of(xp, u).rearrange("p (k c) -> p k c", k=KT), ACT.Copy).then_inc(self.s_hi, 1)
        if t < NT:
            x_ready(act, t)
            if t:
                act.wait_ge(self.s_ss, t)
            act.activation(self.junk[:], self.x_sb[:, t, :], ACT.Square, accum_out=col(self.SS, t)).then_inc(self.s_ss, 1)
        if 0 <= t - 1 < NT:
            act.wait_ge(self.s_v, t)
            act.activation(col(self.SD, t - 1), col(self.V, t - 1), ACT.Sqrt).then_inc(self.s_sd, 1)

    def dve_lo(self, dve, t, xp):
        if not self.y and 0 <= t - 5 < NT:
            u = t - 5
            dve.wait_ge(self.s_hi, u + 1)
            cs = slice(u * P, (u + 1) * P)
            dve.tensor_tensor(self.xT[1][:, :, cs], self.xp_of(xp, u).rearrange("p (k c) -> p k c", k=KT),
                              self.xT[0][:, :, cs].bitcast(F32), ALU.subtract).then_inc(self.s_lo, 1)

    def dve(self, dve, t, x_ready):
        col = lambda k, t: self.st[:, k, t:t + 1]
        if 0 <= t - 1 < NT:
            dve.wait_ge(self.s_ss, t)
            dve.tensor_scalar(col(self.V, t - 1), col(self.SS, t - 1), 1.0 / D, EPS, ALU.mult, ALU.add).then_inc(self.s_v, 1)
        if not 0 <= t - 2 < NT:
            return
        u, n = t - 2, 5 * (t - 2)
        dve.wait_ge(self.s_sd, u + 1)
        dve.reciprocal(col(self.R, u), col(self.SD, u)).then_inc(self.s_ch, 1)
        dve.wait_ge(self.s_ch, n + 1)
        dve.tensor_tensor(col(self.A, u), col(self.R, u), col(self.R, u), ALU.mult).then_inc(self.s_ch, 1)
        dve.wait_ge(self.s_ch, n + 2)
        dve.tensor_tensor(col(self.B, u), col(self.A, u), col(self.V, u), ALU.mult).then_inc(self.s_ch, 1)
        dve.wait_ge(self.s_ch, n + 3)
        dve.tensor_scalar(col(self.A, u), col(self.B, u), -0.5, 1.5, ALU.mult, ALU.add).then_inc(self.s_ch, 1)
        dve.wait_ge(self.s_ch, n + 4)
        dve.tensor_tensor(col(self.SS, u), col(self.R, u), col(self.A, u), ALU.mult).then_inc(self.s_ch, 1)
        dve.wait_ge(self.s_ch, n + 5)
        x_ready(dve, u)
        if u == 0:
            dve.wait_ge(self.s_g, 16)
        if self.y:
            ring = len(self.y)
            if u >= ring:
                dve.wait_ge(self.s_out[u % ring], 16 * (u // ring))
            out = self.y[u % ring][:]
        else:
            if u >= 2:
                dve.wait_ge(self.s_tr, u - 1)
            out = self.xn[:, u % 2, :]
        dve.scalar_tensor_tensor(out, self.x_sb[:, u, :], col(self.SS, u), self.g_bc[:], ALU.mult, ALU.mult).then_inc(self.s_xn, 1)

    def pe(self, pe, t, xp):
        if not self.y and 0 <= t - 3 < NT:
            u = t - 3
            pe.wait_ge(self.s_xn, u + 1)
            if u >= 2:
                pe.wait_ge(self.s_lo, u - 1)
            for k in range(KT):
                last = pe.transpose(self.xp_of(xp, u)[:, k * P:(k + 1) * P], self.xn[:, u % 2, k * P:(k + 1) * P], self.ident[:])
            last.then_inc(self.s_tr, 1)

    def sp_stores(self, sp, dst_of):
        ring = len(self.y)
        for t in range(NT):
            sp.wait_ge(self.s_xn, t + 1)
            sp.dma_start(dst_of(t), self.y[t % ring][:]).then_inc(self.s_out[t % ring], 16)
        for i in range(ring):
            sp.wait_ge(self.s_out[i], 16 * len(range(i, NT, ring)))


def three_pass(pe, out, a, b, first, last):
    pe.matmul(out, a[0], b[0], start=first, stop=False)
    pe.matmul(out, a[0], b[1], start=False, stop=False)
    return pe.matmul(out, a[1], b[0], start=False, stop=last)


def ffn_phase(nc, tag, at_selb, at, x_sb, xT, st, ident, load_x, g_dram, wg, wu, wd, g_next, early, store):
    xT_hi, xT_lo = xT
    wg_v = wg.rearrange("a (k p) f -> p (a k) f", p=P)
    wu_v = wu.rearrange("a (k p) f -> p (a k) f", p=P)
    wd_v = wd.rearrange("a (n p) d -> p (a n) d", p=P)
    with ExitStack() as ctx:
        sem = lambda n: ctx.enter_context(nc.semaphore(f"{tag}_{n}"))
        keep = Plan(nc, tag, at)
        raw_d = Plan(nc, tag, at_selb)("raw_d", [P, 2, D], F32)
        sp_g = [[keep(f"g{'hl'[q]}{f}", [P, KT, P], F32R) for f in range(2)] for q in range(2)]
        sp_u = [[keep(f"u{'hl'[q]}{f}", [P, KT, P], F32R) for f in range(2)] for q in range(2)]
        sp_d = [keep(f"d{'hl'[q]}", [P, 2, D], F32R) for q in range(2)]
        s_x = [sem(f"x_loaded{t}") for t in range(NT)] if load_x else None
        first = TileNorm(nc, ctx, tag + "a", keep.at - 4 * D * 4, st, x_sb, xT, ident, g_dram) if load_x else None
        x_loaded = lambda e, t: e.wait_ge(s_x[t], 16)
        h_hi = keep("h_hi", [P, 2, ROWS], F32R)
        h_lo = keep("h_lo", [P, 2, ROWS], F32R)
        silu = keep("silu", [P, 2, CW], F32)
        raws = Plan(nc, tag, at_end(2 * KT * FB * 4))
        assert keep.at <= raws.at
        y = [Plan(nc, tag, at + i * D * 4)(f"y{i}", [P, D], F32) for i in range(4)] if store else None
        after = TileNorm(nc, ctx, tag + "b", raws.at, st, x_sb, xT, ident, g_next, y)
        raw_g = raws("raw_g", [P, KT, FB], F32)
        raw_u = raws("raw_u", [P, KT, FB], F32)
        pgu = ctx.enter_context(nc.psum_tensor(f"{tag}_pgu", [P, 4, 512], F32))
        pg, pu = [pgu[:, i, :] for i in range(2)], [pgu[:, 2 + i, :] for i in range(2)]
        pyx = ctx.enter_context(nc.psum_tensor(f"{tag}_pyx", [P, 4, 512], F32))
        py = [pyx[:, i, :] for i in range(4)]

        s_rg, s_ru, s_rd = sem("gate_loaded"), sem("up_loaded"), sem("down_loaded")
        s_g0, s_u0, s_glo = sem("first_gate_loaded"), sem("first_up_loaded"), sem("first_gate_split")
        s_whi = sem("weights_hi")
        s_gu = sem("gate_up_split")
        s_dn = sem("down_split")
        s_gud = sem("gate_up_done")
        s_silu = sem("silu_ready")
        s_free = sem("gate_up_read")
        s_hh = sem("hidden_hi")
        s_h = sem("hidden_split")
        s_y = sem("down_done")
        s_acc = sem("y_added")
        NY = NT * 2

        def x_done(eng, t):
            eng.wait_ge(s_acc, 4 + NY * (FSTEPS - 1) + 2 * (t + 1))

        @(block := ctx.enter_context(nc.Block())).sync
        def _(sp):
            if load_x:
                load_x(sp, s_x, 0, CH + 2)
                first.load(sp)
            for dst, src, s in ((raw_g, wg_v, s_g0), (raw_u, wu_v, s_u0)):
                sp.dma_start(dst[:, :, 0:P], src[:, :, 0:P]).then_inc(s, 16)
            for dst, src, s in ((raw_g, wg_v, s_rg), (raw_u, wu_v, s_ru)):
                sp.dma_start(dst[:, :, P:FB], src[:, :, P:FB]).then_inc(s, 16)
            if load_x:
                load_x(sp, s_x, CH + 2, NT)
            sp.dma_start(raw_d[:], wd_v[:, 0:2, :]).then_inc(s_rd, 16)
            with sp.Fori(1, FSTEPS) as i:
                sp.wait_ge(s_gu, 2 * i)
                sp.dma_start(raw_g[:], wg_v[:, :, bass.ds(i * FB, FB)]).then_inc(s_rg, 16)
                sp.dma_start(raw_u[:], wu_v[:, :, bass.ds(i * FB, FB)]).then_inc(s_ru, 16)
                sp.wait_ge(s_dn, i)
                sp.dma_start(raw_d[:], wd_v[:, bass.ds(2 * i, 2), :]).then_inc(s_rd, 16)
            sp.wait_ge(s_gu, 2 * FSTEPS)
            after.load(sp)
            sp.wait_ge(s_gud, 2 * NCH * FSTEPS)
            if store:
                after.sp_stores(sp, store)
            else:
                early["sp"](sp)

        def act_gate_up_hi(act, j, f):
            fs = slice(f * P, (f + 1) * P)
            first_slice = isinstance(j, int) and (j, f) == (0, 0)
            act.wait_ge(s_g0, 16) if first_slice else act.wait_ge(s_rg, 16 * j + 16)
            act.activation(sp_g[0][f][:], raw_g[:, :, fs], ACT.Copy).then_inc(s_whi, 1)
            act.wait_ge(s_u0, 16) if first_slice else act.wait_ge(s_ru, 16 * j + 16)
            act.activation(sp_u[0][f][:], raw_u[:, :, fs], ACT.Copy).then_inc(s_whi, 1)

        def act_down_hi(act, j):
            act.wait_ge(s_rd, 16 * j + 16)
            act.activation(sp_d[0][:], raw_d[:], ACT.Copy).then_inc(s_whi, 1)

        def act_silu(act, i, f, chunks=range(NCH)):
            for c in chunks:
                k = NCH * f + c
                act.wait_ge(s_gud, 2 * NCH * i + k + 1)
                act.wait_ge(s_h, 2 * NCH * i + k + 1)
                act.activation(silu[:, k % 2, :], pg[k % 2][:, 0:CW], ACT.Silu).then_inc(s_silu, 1)

        def act_step(act, i, more, begun=False):
            if not begun:
                act_silu(act, i, 0)
            if more:
                act.wait_ge(s_gud, 2 * NCH * i + NCH)
                act_gate_up_hi(act, i + 1, 0)
            act_silu(act, i, 1)
            if more:
                act.wait_ge(s_gud, 2 * NCH * i + 2 * NCH)
                act_gate_up_hi(act, i + 1, 1)
                act.wait_ge(s_y, NY * i + 2 * NY)
                act_down_hi(act, i + 1)

        @block.scalar
        def _(act):
            if load_x:
                norm = lambda a, b: [first.act(act, t, pyx, x_loaded) for t in range(a, b)]
                norm(0, 5)
                act_gate_up_hi(act, 0, 0)
                norm(5, 10)
                act_silu(act, 0, 0, (0,))
                norm(10, TileNorm.SLOTS)
                act_gate_up_hi(act, 0, 1)
                act_silu(act, 0, 0, (1, 2))
                act_down_hi(act, 0)
                act_step(act, 0, True, True)
            else:
                act_gate_up_hi(act, 0, 0)
                act_gate_up_hi(act, 0, 1)
                act_down_hi(act, 0)
            with act.Fori(1 if load_x else 0, FSTEPS - 1) as i:
                act_step(act, i, True)
            act_step(act, FSTEPS - 1, False)
            for t in range(TileNorm.SLOTS):
                after.act(act, t, pgu, x_done)
                if early and t == 4:
                    early["act"](act)

        def dve_gate_up_lo(dve, j, f):
            fs = slice(f * P, (f + 1) * P)
            dve.wait_ge(s_whi, 5 * j + 2 * f + 1)
            i = dve.tensor_tensor(sp_g[1][f][:], raw_g[:, :, fs], sp_g[0][f][:].bitcast(F32), ALU.subtract)
            if isinstance(j, int) and (j, f) == (0, 0):
                i.then_inc(s_glo, 1)
            dve.wait_ge(s_whi, 5 * j + 2 * f + 2)
            dve.tensor_tensor(sp_u[1][f][:], raw_u[:, :, fs], sp_u[0][f][:].bitcast(F32), ALU.subtract).then_inc(s_gu, 1)

        def dve_down_lo(dve, j):
            dve.wait_ge(s_whi, 5 * j + 5)
            dve.tensor_tensor(sp_d[1][:], raw_d[:], sp_d[0][:].bitcast(F32), ALU.subtract).then_inc(s_dn, 1)

        def dve_hidden(dve, i, f, chunks=range(NCH)):
            for c in chunks:
                k = NCH * f + c
                n = 2 * NCH * i + k + 1
                cs = slice(c * CW, (c + 1) * CW)
                dve.wait_ge(s_silu, n)
                dve.tensor_tensor(silu[:, k % 2, :], silu[:, k % 2, :], pu[k % 2][:, 0:CW], ALU.mult).then_inc(s_free, 1)
                dve.wait_ge(s_y, NY * i + 2 * CH * (c + 1))
                dve.wait_ge(s_free, n + 2)
                dve.tensor_copy(h_hi[:, f, cs], silu[:, k % 2, :]).then_inc(s_hh, 1)
                dve.wait_ge(s_hh, n)
                dve.tensor_tensor(h_lo[:, f, cs], silu[:, k % 2, :], h_hi[:, f, cs].bitcast(F32), ALU.subtract).then_inc(s_h, 1)

        def dve_step(dve, i, more, begun=False):
            if not begun:
                dve_hidden(dve, i, 0)
            if more:
                dve_gate_up_lo(dve, i + 1, 0)
            dve_hidden(dve, i, 1)
            if more:
                dve_gate_up_lo(dve, i + 1, 1)
            for t in range(NT if more else TileNorm.SLOTS):
                if not more:
                    after.dve_lo(dve, t, pgu)
                for k in range(2 * t, 2 * t + 2) if t < NT else ():
                    xs = x_sb[:, t, (k % 2) * 512:(k % 2 + 1) * 512]
                    dve.wait_ge(s_y, NY * i + NY + k + 1)
                    dve.scalar_tensor_tensor(xs, py[k % 4][:], 0.5, xs, ALU.mult, ALU.add).then_inc(s_acc, 1)
                if not more:
                    after.dve(dve, t, x_done)
                    if early and t == 5:
                        early["dve"](dve)
            if more:
                dve_down_lo(dve, i + 1)

        @block.vector
        def _(dve):
            dve.sem_inc(s_free, 2)
            dve.sem_inc(s_h, 2)
            dve.sem_inc(s_acc, 4)
            if load_x:
                def norm(a, b):
                    for t in range(a, b):
                        first.dve_lo(dve, t, pyx)
                        first.dve(dve, t, x_loaded)

                norm(0, 5)
                dve_gate_up_lo(dve, 0, 0)
                norm(5, 11)
                dve_hidden(dve, 0, 0, (0,))
                norm(11, TileNorm.SLOTS)
                dve_gate_up_lo(dve, 0, 1)
                dve_hidden(dve, 0, 0, (1, 2))
                dve_down_lo(dve, 0)
                dve_step(dve, 0, True, True)
            else:
                dve_gate_up_lo(dve, 0, 0)
                dve_gate_up_lo(dve, 0, 1)
                dve_down_lo(dve, 0)
            with dve.Fori(1 if load_x else 0, FSTEPS - 1) as i:
                dve_step(dve, i, True)
            dve_step(dve, FSTEPS - 1, False)

        def pe_step(pe, i, more=True, norm=False, begin=False):
            for f in range(2):
                if not (begin and f == 0):
                    pe.wait_ge(s_gu, 2 * i + f + 1)
                for c in range(NCH):
                    if norm and (f, c) == (0, 0):
                        for t in range(2 * CH):
                            first.pe(pe, t, pyx)
                    if norm and f == 0:
                        pe.wait_ge(first.s_lo, CH * (c + 1))
                    k = NCH * f + c
                    cs = slice(c * CW, (c + 1) * CW)
                    pe.wait_ge(s_free, 2 * NCH * i + k + 1)
                    for n, (w, out) in enumerate(((sp_g, pg), (sp_u, pu))):
                        if begin and k == 0:
                            pe.wait_ge((s_glo, s_gu)[n], 1)
                        for kt in range(KT):
                            last = three_pass(pe, out[k % 2][:, 0:CW], (w[0][f][:, kt, :], w[1][f][:, kt, :]),
                                              (xT_hi[:, kt, cs], xT_lo[:, kt, cs]), kt == 0, kt == KT - 1)
                            if norm and k < NCH - 1 and kt % 4 == 3 and (n, kt) != (1, KT - 1):
                                first.pe(pe, 2 * CH + CH * c + 2 * n + kt // 4, pyx)
                    last.then_inc(s_gud, 1)
            pe.wait_ge(s_dn, i + 1)
            for k in range(NY):
                t, half = k // 2, k % 2
                ts, hs = slice(t * P, (t + 1) * P), slice(half * 512, (half + 1) * 512)
                if k % (2 * CH) == 0:
                    pe.wait_ge(s_h, 2 * NCH * i + NCH + t // CH + 3)
                pe.wait_ge(s_acc, NY * i + k + 1)
                for f in range(2):
                    last = three_pass(pe, py[k % 4][:], (h_hi[:, f, ts], h_lo[:, f, ts]),
                                      (sp_d[0][:, f, hs], sp_d[1][:, f, hs]), f == 0, f == 1)
                last.then_inc(s_y, 1)
                if not more and half:
                    if t == 3:
                        pe.wait_ge(s_free, 2 + 2 * NCH * FSTEPS)
                    after.pe(pe, t, pgu)
            if not more:
                for t in range(NT, TileNorm.SLOTS):
                    after.pe(pe, t, pgu)

        @block.tensor
        def _(pe):
            pe.sem_inc(s_y, NY)
            if load_x:
                pe_step(pe, 0, norm=True, begin=True)
            else:
                pe_step(pe, 0, begin=True)
            with pe.Fori(1, FSTEPS - 1) as i:
                pe_step(pe, i)
            pe_step(pe, FSTEPS - 1, False)


EARLY = 16
KEYS_AT, PAIRS_AT = 5, (8, 48, 91)
WC = 256
NCHUNK = 2 * N_QKV // WC
IDX_AT = 2 * N_QKV
IC = 4 * ID
SELB_AT = [P * t * (t + 1) // 2 for t in range(NP + 1)]


class EarlyWeights:

    def __init__(self, nc, ctx, at, w_in):
        place = Plan(nc, "i", at)
        self.raw = place("raw", [P, KT, N_IDX], F32)
        self.hi, self.lo = place("hi", [P, KT, N_IDX], F32R), place("lo", [P, KT, N_IDX], F32R)
        self.end, self.w_in = place.at, w_in
        self.s_raw, self.s_hi, self.s_lo = (ctx.enter_context(nc.semaphore(f"w_{n}")) for n in ("loaded", "hi", "split"))

    def sp(self, sp):
        sp.dma_start(self.raw[:], self.w_in.rearrange("a (k p) n -> p (a k) n", p=P)[:, :, IDX_AT:IDX_AT + N_IDX]).then_inc(self.s_raw, 16)

    def act(self, act):
        act.wait_ge(self.s_raw, 16)
        act.activation(self.hi[:], self.raw[:], ACT.Copy).then_inc(self.s_hi, 1)

    def dve(self, dve):
        dve.wait_ge(self.s_hi, 1)
        dve.tensor_tensor(self.lo[:], self.raw[:], self.hi[:].bitcast(F32), ALU.subtract).then_inc(self.s_lo, 1)


def rel_rows(dve, rb, ur, s, n0):
    dve.tensor_copy(ur[:, 0:4 * P], rb[:, 2 * MAXREL:2 * MAXREL + 1].broadcast_to([H, 4 * P])).then_inc(s, 1)
    dve.wait_ge(s, n0 + 1)
    dve.tensor_copy(ur[:, 4 * P - 1:6 * P - 1], rb[:, 2 * MAXREL:0:-1]).then_inc(s, 1)
    dve.tensor_copy(ur[:, 6 * P - 1:6 * P], rb[:, 0:1]).then_inc(s, 1)


def wi_phase(nc, at_x, at, x_sb, xT, ident, selb, late_acc, pre, w_in, rel_bias, urel, cos, sin, cache_idx, x_mid, proj, idx_p, idx_s):
    tag = "w"
    xT_hi, xT_lo = xT
    raw, s_raw, s_whi, s_wlo = pre.raw, pre.s_raw, pre.s_hi, pre.s_lo
    w_v = w_in.rearrange("a (k p) n -> p (a k) n", p=P)
    proj_v = proj.rearrange("(t p) n -> p t n", p=P)
    with ExitStack() as ctx:
        sem = lambda n: ctx.enter_context(nc.semaphore(f"{tag}_{n}"))
        keep = Plan(nc, tag, at)
        keep.at = pre.end
        w_hi, w_lo = [pre.hi, keep("w_hi1", [P, KT, WC], F32R)], [pre.lo, keep("w_lo1", [P, KT, WC], F32R)]
        stage = [keep(f"stage{i}", [P, NT, WC], F32) for i in range(2)]
        idx = keep("idx", [P, NT, N_IDX], F32)
        cs_t = keep("cos", [P, NT, HD // 2], F32)
        sn_t = keep("sin", [P, NT, HD // 2], F32)
        rx = Plan(nc, tag, keep.at)("rx", [P, 2, NT * WC // 2], F32)
        kc = keep("kc", [P, PAST // P, DEC_B, ID], F32)
        kcT = [keep(f"kcT{g}", [P, KS], F32) for g in range(2)]
        ksum = keep("ksum", [P, 2, P], F32)
        rb = keep("rb", [H, 2 * MAXREL + 1], F32)
        ur = keep("ur", [H, 6 * P], F32)
        kspread = keep("kspread", [P, DEC_B, ID], F32)
        ix = Plan(nc, tag, at_x)
        acc = [None, ix("acc1", [P, SEQ], F32)]
        acc[0] = ix("acc0", [P, SEQ - 2 * P], F32)
        ix.at = at_x + 8 * SEQ
        qi4 = ix("qi4", [P, IH, 4, ID], F32R)
        own = ix("own", [P, DEC_B], F32)
        m8 = ix("m8", [P, 3, 8], F32)
        acc_s = ix("acc_s", [P, KS + 4], F32)
        kiT = ix("kiT", [P, SEQ], F32R)
        rx_i = Plan(nc, tag, at_x)("rx_i", [P, 2, NT * 9 * ID // 2], F32)
        spread = Plan(nc, tag, at_x)("spread", [P, IH, DEC_B, ID], F32)
        bdq = [Plan(nc, tag, ix.at + 4 * g * IH * P)(f"bdq{g}", [P, IH, P], F32) for g in range(2)]
        qiT = [ix(f"qiT{i}", [P, IH, P], F32R) for i in range(2)]
        ki4 = Plan(nc, tag, ix.at + 4 * SEQ)("ki4", [P, NP, 4, ID], F32R)
        relu = ix("relu", [P, 2, SEQ], F32)
        assert ix.at <= at_x + NT * D * 4
        assert keep.at <= at_end(0)
        pw = [ctx.enter_context(nc.psum_tensor(f"{tag}_pw{i}", [P, 512], F32)) for i in range(3)]
        ps = [ctx.enter_context(nc.psum_tensor(f"{tag}_ps{i}", [P, D], F32)) for i in range(2)]

        s_grp, s_ev = sem("group_done"), sem("group_read")
        s_rot = sem("rope_step")
        s_rdy = [sem(f"stage_ready{i}") for i in range(2)]
        s_put = [sem(f"stage_stored{i}") for i in range(2)]
        s_xst = sem("x_stored")
        s_tab = sem("tables_loaded")
        s_kc = sem("cached_keys_loaded")
        s_iout = sem("idx_keys_stored")
        s_ich = sem("idx_step")
        s_rel, s_ur = sem("rel_bias_moved"), sem("ur_step")
        s_own = sem("own_mask")
        s_idx = sem("idx_rows_ready")
        s_pf, s_pd = sem("pair_filled"), sem("pair_read")
        s_rlf = sem("relu_read")
        s_q4 = sem("queries_expanded")
        s_sel = sem("selection_step")
        s_acc = sem("scores_step")

        TILES = list(range(TOPK // P, NP))
        PAIRS = [TILES[i:i + 2] for i in range(0, len(TILES), 2)]
        unit_of, n_units = {}, 0
        def take(key):
            nonlocal n_units
            unit_of[key] = n_units
            n_units += 1
        for key in ["keys", "bdq0", "bdq1", "kc", "kn"] + [("s", h) for h in range(IH)]:
            take(key)
        for t in TILES:
            take(("q", t))
            for h in range(IH):
                take((t, h))
        after_group = {}
        def place(n, keys, each):
            for j, key in enumerate(keys):
                after_group.setdefault(n + j // each, []).append(key)
        place(KEYS_AT, ["keys", "bdq0", "bdq1", "kc", "kn"], 5)
        place(KEYS_AT + 1, [("s", h) for h in range(IH)], 4)
        for at_group, pair in zip(PAIRS_AT, PAIRS):
            place(at_group, [k for t in pair for k in [("q", t)] + [(t, h) for h in range(IH)]], 4)
        relu_of = {k: n for n, k in enumerate(k for k in sorted(unit_of, key=unit_of.get) if isinstance(k, tuple) and k[0] != "q")}
        tile_no = {t: n for n, t in enumerate(TILES)}
        def col(c):
            return (c - 1) * WC

        block = ctx.enter_context(nc.Block())

        @block.sync
        def _(sp):
            sp.dma_start(rb[:], rel_bias[0]).then_inc(s_rel, 16)
            sp.dma_start(raw[:, :, 0:WC], w_v[:, :, 0:WC]).then_inc(s_raw, 16)
            sp.dma_start(cs_t[:], cos.rearrange("(t p) f -> p t f", p=P)).then_inc(s_tab, 16)
            sp.dma_start(sn_t[:], sin.rearrange("(t p) f -> p t f", p=P)).then_inc(s_tab, 16)
            sp.dma_start(x_mid.rearrange("(t p) d -> p t d", p=P), x_sb[:]).then_inc(s_xst, 16)
            sp.wait_ge(s_ur, 3)
            sp.dma_start(urel, ur[:]).then_inc(s_rel, 16)
            for kt in range(PAST // P):
                sp.dma_start(kc[:, kt, :, :], cache_idx[0].rearrange("b (k p) d -> p k b d", p=P)[:, kt]).then_inc(s_kc, 16)
            sp.wait_ge(s_wlo, 2)
            sp.dma_start(raw[:, :, 0:WC], w_v[:, :, WC:2 * WC]).then_inc(s_raw, 16)
            sp.wait_ge(s_idx, 1)
            sp.dma_start(idx_p.rearrange("a b (t p) d -> p (a b t) d", p=P), idx[:, 0:NP, IH * ID:IH * ID + ID]).then_inc(s_iout, 16)
            sp.dma_start(idx_s.rearrange("a b s d -> (a b s) d"), idx[:, NP, IH * ID:IH * ID + ID]).then_inc(s_iout, 16)
            with sp.Fori(2, NCHUNK) as c:
                sp.wait_ge(s_wlo, c + 1)
                sp.dma_start(raw[:, :, 0:WC], w_v[:, :, bass.ds(c * WC, WC)]).then_inc(s_raw, 16)
            sp.wait_ge(s_iout, 32)
            sp.wait_ge(s_xst, 16)

        def act_hi(act, c, slot, w):
            act.wait_ge(s_raw, 16 * c + 16)
            if not (isinstance(c, int) and c < 2):
                act.wait_ge(s_grp, NT * c - NT)
            act.activation(w_hi[slot][:, :, 0:w], raw[:, :, 0:w], ACT.Copy).then_inc(s_whi, 1)

        def act_unit(act, key, dst, src_cols, func, scale):
            u = unit_of[key]
            act.wait_ge(s_pf, u + 1)
            act.activation(dst, ps[u % 2][:, 0:src_cols] if len(dst.shape) == 2 else
                           ps[u % 2][:, 0:src_cols].rearrange("p (h c) -> p h c", c=P), func, scale=scale).then_inc(s_pd, 1)

        def act_index(act, key):
            if key == "keys":
                act_unit(act, key, kiT[:], SEQ, ACT.Copy, 1.0)
            elif key in ("bdq0", "bdq1"):
                act_unit(act, key, bdq[int(key[3])][:], D, ACT.Copy, 1.0)
            elif key == "kc":
                u = unit_of[key]
                act.wait_ge(s_pf, u + 1)
                for g in range(2):
                    i = act.activation(kcT[g][:, 0:PAST], ps[u % 2][:, g * PAST:(g + 1) * PAST], ACT.Copy)
                i.then_inc(s_pd, 1)
            elif key == "kn":
                act_unit(act, key, ksum[:], 2 * P, ACT.Copy, 1.0)
            elif key[0] == "q":
                n = tile_no[key[1]]
                if n >= 2:
                    act.wait_ge(s_pf, unit_of[(TILES[n - 2], IH - 1)] + 1)
                act_unit(act, key, qiT[n % 2][:], D, ACT.Copy, 1.0)
            else:
                r = relu_of[key]
                w = KS if key[0] == "s" else P * (key[0] + 1)
                if r >= 2:
                    act.wait_ge(s_rlf, r - 1)
                act_unit(act, key, relu[:, r % 2, 0:w], w, ACT.Relu, 1.0 / 16)

        def act_evac(act, c, slot, k):
            if not (isinstance(k, int) and k == 0):
                act.wait_ge(s_put[slot], 16 * k)
            for t in range(NT):
                act.wait_ge(s_grp, NT * c + t + 1)
                act.activation(stage[slot][:, t, :], pw[t % 3][:, 0:WC], ACT.Copy).then_inc(s_ev, 1)
                for key in after_group.get(NT * c - NT + t, ()) if isinstance(c, int) else ():
                    act_index(act, key)

        def act_step(act, i, last=False):
            act_hi(act, 2 * i + 2, 0, WC)
            act_evac(act, 2 * i + 1, 1, i)
            if not last:
                act_hi(act, 2 * i + 3, 1, WC)
            act_evac(act, 2 * i + 2, 0, i)

        @block.scalar
        def _(act):
            for t in range(NT):
                act.wait_ge(s_grp, t + 1)
                act.activation(idx[:, t, :], pw[t % 3][:, 0:N_IDX], ACT.Copy).then_inc(s_ev, 1)
                if t == 2:
                    act_hi(act, 1, 1, WC)
            for i in range(6):
                act_step(act, i, i == 5)

        def pool_lo(pool, c, slot, w):
            pool.wait_ge(s_whi, c + 1)
            pool.tensor_tensor(w_lo[slot][:, :, 0:w], raw[:, :, 0:w], w_hi[slot][:, :, 0:w].bitcast(F32), ALU.subtract).then_inc(s_wlo, 1)

        def rotate(eng, x, tmp, cosv, sinv, s, n0):
            half = x.shape[3] // 2
            x1, x2 = x[:, :, :, 0:half], x[:, :, :, half:2 * half]
            a, b = (tmp[:, q, 0:x.shape[1] * x.shape[2] * half].rearrange("p (t h f) -> p t h f", t=x.shape[1], h=x.shape[2]) for q in range(2))
            cb = cosv.unsqueeze(2).broadcast_to([P, x.shape[1], x.shape[2], half])
            sb_ = sinv.unsqueeze(2).broadcast_to([P, x.shape[1], x.shape[2], half])
            eng.tensor_tensor(a, x1, sb_, ALU.mult)
            eng.tensor_tensor(b, x2, sb_, ALU.mult).then_inc(s, 1)
            eng.wait_ge(s, n0 + 1)
            eng.tensor_tensor(x1, x1, cb, ALU.mult)
            eng.tensor_tensor(x2, x2, cb, ALU.mult).then_inc(s, 1)
            eng.wait_ge(s, n0 + 2)
            eng.tensor_tensor(x1, x1, b, ALU.subtract)
            return eng.tensor_tensor(x2, x2, a, ALU.add)

        def pool_chunk(pool, c, slot, k, rope, n_rope):
            pool.wait_ge(s_ev, NT * (c + 1))
            if rope:
                x = stage[slot][:].rearrange("p t (h f) -> p t h f", f=HD)
                rotate(pool, x, rx, cs_t[:], sn_t[:], s_rot, n_rope).then_inc(s_rdy[slot], 1)
                pool.wait_ge(s_rdy[slot], k)
            dst = proj_v[:, :, bass.ds((c - 1) * WC, WC)] if not isinstance(c, int) else proj_v[:, :, (c - 1) * WC:c * WC]
            pool.dma_start(dst, stage[slot][:]).then_inc(s_put[slot], 16)

        def pool_step(pool, i, rope=False, n=0, last=False):
            pool_lo(pool, 2 * i + 2, 0, WC)
            pool_chunk(pool, 2 * i + 1, 1, n + 1, rope, 4 * n)
            if not last:
                pool_lo(pool, 2 * i + 3, 1, WC)
            pool_chunk(pool, 2 * i + 2, 0, n + 1, rope, 4 * n + 2)

        @block.gpsimd
        def _(pool):
            pool_lo(pool, 1, 1, WC)
            pool.wait_ge(s_xst, 16)
            pool.memset(own[:], 1.0).then_inc(s_own, 1)
            for n, (m, b0, st_) in enumerate(((1, 0, -DEC_S), (-1, DEC_S - 1, DEC_S))):
                pool.wait_ge(s_own, n + 1)
                pool.affine_select(out=own[:], in_=own[:], compare_op=ALU.is_ge, fill=0.0, base=b0,
                                   pattern=[[st_, DEC_B]], channel_multiplier=m).then_inc(s_own, 1)
            pool.wait_ge(s_tab, 32)
            with pool.Fori(0, 2) as i:
                pool_step(pool, i)
            pool_step(pool, 2)
            pool_step(pool, 3, True, 0)
            pool_step(pool, 4, True, 1)
            pool_step(pool, 5, last=True)
            for i in range(2):
                pool.wait_ge(s_put[i], 16 * NCHUNK // 2)

        def dve_expand_q(dve, t):
            n = tile_no[t]
            q = idx[:, t, 0:IH * ID].rearrange("p (h f) -> p h f", f=ID)
            if n:
                dve.wait_ge(s_pf, unit_of[("q", TILES[n - 1])] + 1)
            dve.tensor_copy(qi4[:, :, 0, :], q).then_inc(s_ich, 1)
            dve.tensor_copy(qi4[:, :, 1, :], q).then_inc(s_ich, 1)
            dve.wait_ge(s_ich, 20 + 4 * n + 1)
            hi = qi4[:, :, 0, :].bitcast(F32)
            dve.tensor_tensor(qi4[:, :, 2, :], q, hi, ALU.subtract).then_inc(s_ich, 1)
            dve.tensor_tensor(qi4[:, :, 3, :], q, hi, ALU.subtract).then_inc(s_ich, 1)
            dve.wait_ge(s_ich, 20 + 4 * n + 4)
            dve.sem_inc(s_q4, 1)

        n_acc = [0]

        def dve_scores(dve, a, t_idx, keys, n):
            for h in range(IH):
                r = relu_of[(keys, h)]
                w = idx[:, t_idx, IH * ID + ID + h:IH * ID + ID + h + 1]
                dve.wait_ge(s_pd, relu_unit[r] + 1)
                if h == 0:
                    i = dve.tensor_scalar(a[:, 0:n], relu[:, r % 2, 0:n], w, None, ALU.mult)
                else:
                    dve.wait_ge(s_acc, n_acc[0])
                    i = dve.scalar_tensor_tensor(a[:, 0:n], relu[:, r % 2, 0:n], w, a[:, 0:n], ALU.mult, ALU.add)
                i.then_inc(s_acc, 1)
                n_acc[0] += 1
                dve.wait_ge(s_acc, n_acc[0])
                dve.sem_inc(s_rlf, 1)

        relu_unit = {relu_of[k]: unit_of[k] for k in relu_of}

        n_sel = [0]

        def dve_select(dve, parts, rounds):
            n = len(parts)
            base = n_sel[0]
            for i in range(rounds):
                for q, (a, w) in enumerate(parts):
                    if i:
                        dve.wait_ge(s_sel, base + 2 * n * i - n + q + 1)
                    dve.max(m8[:, q, :], a[:, 0:w]).then_inc(s_sel, 1)
                for q, (a, w) in enumerate(parts):
                    dve.wait_ge(s_sel, base + 2 * n * i + q + 1)
                    dve.match_replace(out=a[:, 0:w], in_to_replace=m8[:, q, :], in_values=a[:, 0:w], imm_value=GONE).then_inc(s_sel, 1)
            n_sel[0] = base + 2 * n * rounds
            dve.wait_ge(s_sel, n_sel[0])

        @block.vector
        def _(dve):
            dve.wait_ge(s_rel, 16)
            rel_rows(dve, rb, ur, s_ur, 0)
            dve.wait_ge(s_rel, 32)
            dve.wait_ge(s_xst, 16)
            dve.wait_ge(s_tab, 32)
            dve.wait_ge(s_ev, NT)
            x = idx[:, :, 0:9 * ID].rearrange("p t (h f) -> p t h f", f=ID)
            rotate(dve, x, rx_i, cs_t[:, :, 0:HD // 2:2], sn_t[:, :, 0:HD // 2:2], s_ich, 0).then_inc(s_ich, 1)
            dve.wait_ge(s_ich, 3)
            dve.sem_inc(s_idx, 1)
            k = idx[:, 0:NP, IH * ID:IH * ID + ID]
            dve.tensor_copy(ki4[:, :, 0, :], k).then_inc(s_ich, 1)
            dve.tensor_copy(ki4[:, :, 2, :], k).then_inc(s_ich, 1)
            dve.wait_ge(s_ich, 5)
            for q in (1, 3):
                dve.tensor_tensor(ki4[:, :, q, :], k, ki4[:, :, 0, :].bitcast(F32), ALU.subtract).then_inc(s_ich, 1)
            dve.wait_ge(s_own, 3)
            q = idx[:, NP, 0:IH * ID].rearrange("p (h f) -> p h f", f=ID)
            dve.tensor_tensor(spread[:].rearrange("p h b f -> p h (b f)").rearrange("p h (b f) -> p h b f", b=DEC_B),
                              q.unsqueeze(2).broadcast_to([P, IH, DEC_B, ID]),
                              own[:].unsqueeze(1).unsqueeze(3).broadcast_to([P, IH, DEC_B, ID]), ALU.mult).then_inc(s_ich, 1)
            dve.tensor_tensor(kspread[:], idx[:, NP, IH * ID:IH * ID + ID].unsqueeze(1).broadcast_to([P, DEC_B, ID]),
                              own[:].unsqueeze(2).broadcast_to([P, DEC_B, ID]), ALU.mult).then_inc(s_ich, 1)
            few = SELB_AT[TOPK // P]
            dve.memset(selb[:, 0:few], 0.0).then_inc(s_ich, 1)
            dve.wait_ge(s_ich, 10)
            for t in range(TOPK // P):
                e = SELB_AT[t + 1]
                dve.memset(selb[0:CHUNK, e - CHUNK:e], NEG).then_inc(s_ich, 1)
            for _ in range(20 - 12):
                dve.sem_inc(s_ich, 1)
            dve.wait_ge(s_ich, 20)
            dve_expand_q(dve, TILES[0])
            dve.wait_ge(s_pd, unit_of["kn"] + 1)
            for g in range(2):
                dve.tensor_reduce(out=kcT[g][:, PAST:KS], in_=ksum[:, g, :].rearrange("p (b q) -> p q b", b=DEC_B),
                                  axis=AX.X, op=ALU.add).then_inc(s_own, 1)
            dve_scores(dve, acc_s, NP, "s", KS)
            dve.memset(acc_s[:, KS:KS + 4], FIRST).then_inc(s_acc, 1)
            n_acc[0] += 1

            def selected(t, a, w):
                dve.tensor_scalar(selb[:, SELB_AT[t]:SELB_AT[t] + w], a[:, 0:w], GONE, NEG, ALU.not_equal, ALU.mult).then_inc(s_acc, 1)
                n_acc[0] += 1

            for pair in PAIRS:
                a_of = late_acc if pair is PAIRS[-1] else acc
                for q, t in enumerate(pair):
                    if t + 1 in tile_no:
                        dve_expand_q(dve, t + 1)
                    dve.wait_ge(s_acc, n_acc[0])
                    dve_scores(dve, a_of[q], t, t, P * (t + 1))
                    dve.wait_ge(s_acc, n_acc[0])
                    dve.memset(a_of[q][0:CHUNK, P * (t + 1) - CHUNK:P * (t + 1)], UNSEEN).then_inc(s_acc, 1)
                    n_acc[0] += 1
                dve.wait_ge(s_acc, n_acc[0])
                if pair is PAIRS[-1]:
                    dve_select(dve, [(a_of[0], P * (pair[0] + 1))], EARLY)
                    break
                whole = list(enumerate(pair))
                dve_select(dve, [(a_of[q], P * (t + 1)) for q, t in whole], TOPK // 8)
                for q, t in whole:
                    selected(t, a_of[q], P * (t + 1))
                if pair is PAIRS[0]:
                    dve_select(dve, [(acc_s, KS + 4)], (SEL_S + 4) // 8)
                    selected(NP, acc_s, KS)

        def pe_chunk(pe, c, slot, w):
            pe.wait_ge(s_wlo, c + 1)
            for t in range(NT):
                if not (isinstance(c, int) and c == 0 and t < 3):
                    pe.wait_ge(s_ev, NT * c + t - 2)
                ts = slice(t * P, (t + 1) * P)
                for kt in range(KT):
                    last = three_pass(pe, pw[t % 3][:, 0:w], (xT_hi[:, kt, ts], xT_lo[:, kt, ts]),
                                      (w_hi[slot][:, kt, 0:w], w_lo[slot][:, kt, 0:w]), kt == 0, kt == KT - 1)
                last.then_inc(s_grp, 1)
                for key in after_group.get(NT * c - NT + t, ()) if isinstance(c, int) else ():
                    pe_index(pe, key)

        def pe_index(pe, key):
            u = unit_of[key]
            out = ps[u % 2]
            if u >= 2:
                pe.wait_ge(s_pd, u - 1)
            turn = lambda at, src: pe.transpose(out[:, at:at + P], src, ident[:])
            if key == "keys":
                pe.wait_ge(s_ich, 7)
                for t in range(NP):
                    last = turn(t * P, ki4[:, t, :, :].rearrange("p c f -> p (c f)").bitcast(F32))
            elif key in ("bdq0", "bdq1"):
                pe.wait_ge(s_ich, 9)
                g = int(key[3])
                for h in range(IH):
                    last = turn(h * P, spread[:, h, 4 * g:4 * g + 4, :].rearrange("p b f -> p (b f)"))
            elif key == "kc":
                pe.wait_ge(s_kc, 16 * PAST // P)
                for g in range(2):
                    for kt in range(PAST // P):
                        last = turn(g * PAST + kt * P, kc[:, kt, 4 * g:4 * g + 4, :].rearrange("p b f -> p (b f)"))
            elif key == "kn":
                for g in range(2):
                    last = turn(g * P, kspread[:, 4 * g:4 * g + 4, :].rearrange("p b f -> p (b f)"))
            elif key[0] == "q":
                pe.wait_ge(s_q4, tile_no[key[1]] + 1)
                for h in range(IH):
                    last = turn(h * P, qi4[:, h, :, :].rearrange("p c f -> p (c f)").bitcast(F32))
            elif key[0] == "s":
                if key[1] == 0:
                    pe.wait_ge(s_own, 5)
                for k0, k1 in ((0, PAST), (PAST, KS)):
                    for g in range(2):
                        last = pe.matmul(out[:, k0:k1], bdq[g][:, key[1], :], kcT[g][:, k0:k1], start=g == 0, stop=g == 1)
            else:
                t, h = key
                if h == 0:
                    pe.wait_ge(s_pd, unit_of[("q", t)] + 1)
                for k0 in range(0, P * (t + 1), 512):
                    k1 = min(k0 + 512, P * (t + 1))
                    last = pe.matmul(out[:, k0:k1], qiT[tile_no[t] % 2][:, h, :], kiT[:, k0:k1], start=True, stop=True)
            last.then_inc(s_pf, 1)

        def pe_step(pe, i):
            pe_chunk(pe, 2 * i + 1, 1, WC)
            pe_chunk(pe, 2 * i + 2, 0, WC)

        @block.tensor
        def _(pe):
            pe_chunk(pe, 0, 0, N_IDX)
            for i in range(6):
                pe_step(pe, i)

FAR = BAND - 2 * MAXREL
NEAR = BAND - FAR
SHARE = 2.6


def attn_plan():
    heads = [(x, t, h) for x in range(2) for t in range(NP) for h in range(H)]
    tiles = [(x, t) for x in range(2) for t in range(NP)]
    plan = [("prep", 0, 0), ("score", 0), ("score", 1)]
    for g, (x, t, h) in enumerate(heads):
        n = tiles.index((x, t))
        if h == 4 and n + 1 < len(tiles):
            plan.append(("prep",) + tiles[n + 1])
        plan.append(("turn", g))
        if g + 2 < len(heads):
            plan.append(("score", g + 2))
        if g >= 1:
            plan.append(("value", g - 1))
        if h == 2 and n >= 1:
            plan.append(("out",) + tiles[n - 1])
    plan += [("value", len(heads) - 1), ("out",) + tiles[-1]]
    return heads, plan


def sample_plan(n):
    plan = [("keys", 0), ("keys", 1), ("score", 0)]
    for s in range(n):
        plan.append(("turn", s))
        if s + 1 < n:
            plan.append(("score", s + 1))
        if s >= 1:
            plan.append(("value", s - 1))
        if s + 2 < n:
            plan.append(("keys", s + 2))
        if s >= 2:
            plan.append(("out", s - 2))
    return plan + [("value", n - 1), ("out", n - 2), ("out", n - 1)]


def blocks_of(x, t):
    first = max(0, t - LEFT // 2) if x == 0 else 0
    return first, t + 1 - first


def attn_phase(nc, at, ident, selb, acc, proj, urel, caches, oT_hi, oT_lo, outs):
    tag = "t"
    proj_v = proj.rearrange("(t p) n -> p t n", p=P)
    FW = H * HD
    with ExitStack() as ctx:
        sem = lambda n: ctx.enter_context(nc.semaphore(f"{tag}_{n}"))
        keep = Plan(nc, tag, at)
        keep.at += 4 * SEQ
        acc6 = Plan(nc, tag, SBUF_END - 4 * ROWS)("acc6", [P, SEQ - P], F32)
        sc = keep("sc", [P, 3, D], F32)
        m8 = keep("m8", [P, 8], F32)
        at_bias = keep.at
        bias = keep("bias", [P, H, BAND], F32)
        pT = keep("pT", [P, 2, D], F32)
        osb = keep("osb", [P, 2, FW], F32)
        small = keep("small", [P, 2, 8], F32)
        sums = keep("sums", [P, 2, H], F32)
        rec = keep("rec", [P, 2, H], F32)
        flip_s = keep("flip_s", [P, H, DEC_S], F32)
        at_big = keep.at
        rows = keep("rows", [P, 2, FW], F32)
        qT = keep("qT", [P, 2, H, P], F32)
        kT, v = [None, None], [None, None]
        kT[0], v[0] = keep("kT0", [P, HT, SEQ], F32), keep("v0", [P, NP, FW], F32)
        rel = Plan(nc, tag, keep.at)
        kT[1], v[1] = keep("kT1", [P, HT, SEQ], F32), keep("v1", [P, NP, FW], F32)
        raw = rel("raw", [P, H, NEAR], F32)
        flip = rel("flip", [P, P], F32)
        assert rel.at <= keep.at
        assert keep.at <= SBUF_END - 2 * KT * ROWS * 4
        smp = Plan(nc, tag, at_big)
        kc = [smp(f"kc{i}", [P, PAST // P, FW], F32) for i in range(2)]
        vc = [smp(f"vc{i}", [P, PAST // P, FW], F32) for i in range(2)]
        vn = [smp(f"vn{i}", [DEC_S, FW], F32) for i in range(2)]
        kTs = [smp(f"kTs{i}", [P, HT, KS], F32) for i in range(2)]
        bd = [smp(f"bd{i}", [P, 5 * P], F32) for i in range(2)]
        snT = smp("snT", [P, 2, 2, HT, P], F32)
        late = Plan(nc, tag, at_bias)
        srow = late("srow", [P, 2, 2, FW], F32)
        raw_s = late("raw_s", [P, KS - FAR], F32)
        bias_s = late("bias_s", [P, KS], F32)
        rep = late("rep", [P, DEC_B, H, DEC_S], BF16)
        assert late.at <= at_bias + H * BAND * 4
        assert smp.at <= keep.at
        ps = [ctx.enter_context(nc.psum_tensor(f"{tag}_ps{i}", [P, D], F32)) for i in range(2)]
        pt = [ctx.enter_context(nc.psum_tensor(f"{tag}_pt{i}", [P, 512], F32)) for i in range(2)]
        po = ctx.enter_context(nc.psum_tensor(f"{tag}_po", [P, 512], F32))
        pm = ctx.enter_context(nc.psum_tensor(f"{tag}_pm", [P, 512], F32))

        s_bias, s_far, s_sel = sem("bias_loaded"), sem("far_bias_ready"), sem("selection_step")
        s_flip, s_flipped = sem("flip_ready"), sem("bias_flipped")
        s_be = [sem("bias_read_dve"), sem("bias_read_act")]
        s_mask, s_rep, s_zero = sem("bias_masked"), sem("rep_ready"), sem("zeroed")
        s_row = sem("rows_loaded")
        s_v = [sem(f"v_loaded{i}") for i in range(2)]
        s_out = sem("outputs_stored")
        s_mf, s_ma, s_ml = sem("misc_filled"), sem("misc_read_act"), sem("misc_read_dve")
        s_s, s_mx, s_sc, s_p = sem("scores_done"), sem("max_ready"), sem("scores_ready"), sem("exp_ready")
        s_t = sem("turned")
        s_pt = [sem("turned_read_act"), sem("turned_read_dve")]
        s_o, s_rc, s_os = sem("value_done"), sem("reciprocal"), sem("out_scaled")
        s_kt = sem("new_keys_placed")
        s_bd = sem("block_queries")
        s_kc, s_vc = [sem(f"kc_loaded{i}") for i in range(2)], [sem(f"vc_loaded{i}") for i in range(2)]
        s_sr = sem("sample_rows_loaded")

        heads, plan = attn_plan()
        NH = len(heads)
        NTT = 2 * NP
        units, u0 = {}, 0
        for g, (x, t, h) in enumerate(heads):
            n = blocks_of(x, t)[1]
            units[g] = [(u0 + j, 4 * j, min(4, n - 4 * j)) for j in range(-(-n // 4))]
            u0 += len(units[g])
        items = [(x, b) for x in range(2) for b in range(DEC_B)]
        kunits, punits = {}, {}
        splan = [(e, s, items[s][0], items[s][1]) for e, s in sample_plan(len(items))]
        for e, s, _, _ in splan:
            if e in ("keys", "turn"):
                (kunits if e == "keys" else punits)[s] = list(range(u0, u0 + (HT if e == "keys" else 2)))
                u0 += HT if e == "keys" else 2
        by_dve, todo_act, todo_dve = [], 0.0, 0.0
        for g, (x, t, h) in enumerate(heads):
            n = blocks_of(x, t)[1]
            todo_act, todo_dve = todo_act + n + 2, todo_dve + SHARE * n + 2
            for _, _, nb in units[g]:
                by_dve.append(int(todo_dve < todo_act))
                if by_dve[-1]:
                    todo_dve += nb + 1
                else:
                    todo_act += nb + 1
        by_dve += [u % 2 for u in range(len(by_dve), u0)]
        misc, m0, lo_n = {}, 0, {}
        nlo = 0
        free_at = {}
        def use(key, by_dve):
            nonlocal m0, nlo
            misc[key] = m0
            m0 += 1
            nlo += by_dve
            lo_n[key] = nlo
        order = []
        for e in plan:
            if e[0] == "prep":
                order += [(("k",) + e[1:], 0), (("q",) + e[1:], 0)]
            elif e[0] == "out":
                order += [(("o",) + e[1:], 1)]
        order += [((("sk", "sq")[j], x), 0) for x in range(2) for j in range(2)]
        order += [(("so", s), 1) for s in range(len(items))]
        for key, by in order:
            use(key, by)
        keys_in_order = [k for k, _ in order]

        def sc_of(g, a, b):
            return sc[:, g % 3, a:b]

        def in_halves(a):
            return a.rearrange("p (h c) -> p h c", h=2)

        def both_halves(g):
            return in_halves(ps[g % 2][:])[:, :, 0:KS // 2]

        def pe_misc(pe, key):
            m = misc[key]
            if m:
                prev = keys_in_order[m - 1]
                pe.wait_ge(s_ma, m)
                if lo_n[prev]:
                    pe.wait_ge(s_ml, lo_n[prev])
            return pm

        block = ctx.enter_context(nc.Block())

        @block.sync
        def _(sp):
            tiles = [(x, t) for x in range(2) for t in range(NP)]

            def rows_of(n):
                x, t = tiles[n]
                if n:
                    sp.wait_ge(s_mf, misc[("q",) + tiles[n - 1]] + 1)
                c = x * N_QKV
                sp.dma_start(rows[:, 0, :], proj_v[:, t, c + FW:c + 2 * FW]).then_inc(s_row, 16)
                sp.dma_start(rows[:, 1, :], proj_v[:, t, c:c + FW]).then_inc(s_row, 16)

            def values(x):
                sp.dma_start(v[x][:], proj_v[:, 0:NP, x * N_QKV + 2 * FW:x * N_QKV + 3 * FW]).then_inc(s_v[x], 16)

            rows_of(0)
            u = urel
            sp.dma_start(raw[:], bass.AP(u.tensor, FAR, [[1, P], [6 * P, H], [1, NEAR]])).then_inc(s_bias, 16)
            values(0)
            rows_of(1)
            sp.wait_ge(s_flipped, 2)
            values(1)
            for n in range(2, len(tiles)):
                rows_of(n)
            for dst, c, r0, r1 in outs:
                sp.dma_start(dst, proj[r0:r1, c:c + FW]).then_inc(s_out, 16)
            sp.wait_ge(s_t, units[NH - 1][-1][0] + 1)
            sp.wait_ge(s_o, NH)
            for h in range(H):
                sp.dma_start(raw_s[h * DEC_S:(h + 1) * DEC_S, :],
                             bass.AP(u.tensor, 6 * P * h + FAR + P - DEC_S, [[1, DEC_S], [1, KS - FAR]])).then_inc(s_bias, 16)
            for x in range(2):
                for j in range(2):
                    sp.dma_start(srow[:, x, j, :], proj_v[:, NP, x * N_QKV + (1 - j) * FW:x * N_QKV + (2 - j) * FW]).then_inc(s_sr, 16)

            def cached_keys(s):
                x, b = items[s]
                if s >= 2:
                    sp.wait_ge(s_t, kunits[s - 2][-1] + 1)
                sp.dma_start(kc[s % 2][:], caches[x][0][0, b].rearrange("(k p) h d -> p k (h d)", p=P)).then_inc(s_kc[s % 2], 16)

            def cached_values(s):
                x, b = items[s]
                if s >= 2:
                    sp.wait_ge(s_o, NH + s - 1)
                sp.dma_start(vc[s % 2][:], caches[x][1][0, b].rearrange("(k p) h d -> p k (h d)", p=P)).then_inc(s_vc[s % 2], 16)
                r = SEQ + b * DEC_S
                sp.dma_start(vn[s % 2][:], proj[r:r + DEC_S, x * N_QKV + 2 * FW:x * N_QKV + 3 * FW]).then_inc(s_vc[s % 2], 16)

            cached_keys(0)
            for s in range(len(items)):
                if s + 1 < len(items):
                    cached_keys(s + 1)
                cached_values(s)
            sp.wait_ge(s_out, 16 * len(outs))

        @block.gpsimd
        def _(pool):
            pool.memset(flip[:], 0.0).then_inc(s_flip, 1)
            pool.memset(flip_s[:], 0.0).then_inc(s_flip, 1)
            pool.wait_ge(s_flip, 2)
            pool.affine_select(out=flip[:], in_=flip[:], compare_op=ALU.not_equal, fill=1.0, base=1 - P,
                               pattern=[[1, P]], channel_multiplier=1).then_inc(s_flip, 1)
            pool.affine_select(out=flip_s[:], in_=flip_s[:], compare_op=ALU.not_equal, fill=1.0, base=1 - DEC_S,
                               pattern=[[-DEC_S, H], [1, DEC_S]], channel_multiplier=1).then_inc(s_flip, 1)
            pool.memset(qT[:], 0.0).then_inc(s_zero, 1)
            for i in range(2):
                pool.wait_ge(s_be[i], 1)
            pool.tensor_copy(bias[:, :, 0:FAR], bias[:, :, FAR:FAR + 1].broadcast_to([P, H, FAR])).then_inc(s_far, 1)
            pool.wait_ge(s_far, 1)
            pool.memset(bias[CHUNK:P, :, 0:CHUNK], NEG).then_inc(s_far, 1)
            pool.wait_ge(s_o, NH)
            pool.wait_ge(s_mf, misc[("o", 1, NP - 1)] + 1)
            for i in range(2):
                pool.memset(bd[i][:], 0.0).then_inc(s_zero, 1)
            pool.memset(rep[:], 0.0).then_inc(s_rep, 1)
            pool.wait_ge(s_rep, 1)
            pool.affine_select(out=rep[:], in_=rep[:], compare_op=ALU.not_equal, fill=1.0, base=0,
                               pattern=[[-DEC_S, DEC_B], [0, H], [-1, DEC_S]], channel_multiplier=1).then_inc(s_rep, 1)
            for s, (x, b) in enumerate(items):
                bs = slice(b * DEC_S, (b + 1) * DEC_S)
                pool.wait_ge(s_ma, misc[("sq", x)] + 1)
                if s >= 2:
                    pool.wait_ge(s_s, NH + s - 1)
                else:
                    pool.wait_ge(s_zero, 3)
                bv = bd[s % 2][:].rearrange("p (f c) -> p f c", c=5 * DEC_S * 2)
                for j, (dst, src) in enumerate(((kTs[s % 2][:, :, PAST:KS], snT[:, x, 0, :, bs]),
                                                (bv[0:HD, :, 0:DEC_S], snT[0:HD, x, 1, :, bs]),
                                                (bv[HD:P, :, DEC_S:2 * DEC_S], snT[HD:P, x, 1, :, bs]))):
                    pool.tensor_copy(dst, src).then_inc(s_bd, 1)
                    pool.wait_ge(s_bd, 3 * s + j + 1)

        def diag(r):
            a = pm[r * HD:(r + 1) * HD, 0:DEC_S]
            return bass.AP(a.tensor, a.offset + r * DEC_S, [list(a.ap[0]), [P + 2 * DEC_S, HT], [1, DEC_S]])

        def dve_out(dve, key, n):
            dve.reciprocal(rec[:, n % 2, :], sums[:, n % 2, :]).then_inc(s_rc, 1)
            dve.wait_ge(s_rc, n + 1)
            if n >= 2:
                dve.wait_ge(s_mf, misc[("o",) + tiles_of[n - 2]] + 1)
            dve.tensor_tensor(osb[:, n % 2, :].rearrange("p (h d) -> p h d", d=HD), po[:].rearrange("p (h d) -> p h d", d=HD),
                              rec[:, n % 2, :].unsqueeze(2).broadcast_to([P, H, HD]), ALU.mult).then_inc(s_os, 1)

        tiles_of = [(x, t) for x in range(2) for t in range(NP)]

        @block.vector
        def _(dve):
            dve.wait_ge(s_flipped, 1)
            dve.tensor_copy(bias[:, 0:H // 2, FAR:BAND], ps[0][:].rearrange("p (h c) -> p h c", c=NEAR)).then_inc(s_be[0], 1)
            dve.wait_ge(s_be[0], 1)
            dve.wait_ge(s_be[1], 1)
            dve.memset(bias[0:CHUNK, :, BAND - CHUNK:BAND], NEG).then_inc(s_mask, 1)
            dve.wait_ge(s_mask, 1)

            n_sel = [0]
            halves = [(t, i, j) for t, i0 in ((NP - 2, EARLY), (NP - 1, 0)) for i in range(i0, TOPK // 8) for j in range(2)]
            dve.tensor_copy(acc6[:], acc[0][:]).then_inc(s_sel, 1)
            n_sel[0] = 1
            dve.wait_ge(s_sel, 1)

            def select_half():
                t, i, j = halves.pop(0)
                a = (acc6 if t == NP - 2 else acc[1])[:]
                dve.wait_ge(s_sel, n_sel[0])
                if j == 0:
                    dve.max(m8[:], a).then_inc(s_sel, 1)
                else:
                    dve.match_replace(out=a, in_to_replace=m8[:], in_values=a, imm_value=GONE).then_inc(s_sel, 1)
                n_sel[0] += 1
                if (i, j) == (TOPK // 8 - 1, 1):
                    dve.wait_ge(s_sel, n_sel[0])
                    dve.tensor_scalar(selb[:, SELB_AT[t]:SELB_AT[t + 1]], a, GONE, NEG, ALU.not_equal, ALU.mult).then_inc(s_sel, 1)
                    n_sel[0] += 1

            todo = sum(blocks_of(x, t)[1] for x, t, h in heads[:heads.index((1, NP - 1, 0))])
            done, n_halves = 0, len(halves)
            for e in plan:
                if e[0] == "score":
                    g = e[1]
                    x, t, h = heads[g]
                    n = P * blocks_of(x, t)[1]
                    if (x, t, h) == (1, 0, 0):
                        assert halves[0][0] == NP - 1
                    if x == 1 and t >= NP - 2 and h == 0:
                        assert t == NP - 2 or not halves
                        dve.wait_ge(s_sel, n_sel[0])
                    if (x, t, h) == (0, 2, 0):
                        dve.wait_ge(s_far, 2)
                    dve.wait_ge(s_s, g + 1)
                    if g >= 3:
                        dve.wait_ge(s_t, units[g - 3][-1][0] + 1)
                    if g >= 4:
                        dve.wait_ge(s_p, g - 3)
                    b = bias[:, h, BAND - n:BAND] if x == 0 else selb[:, SELB_AT[t]:SELB_AT[t] + n]
                    dve.tensor_tensor_reduce(out=sc_of(g, 0, n), in0=ps[g % 2][:, 0:n], in1=b, scale=1.0, scalar=GONE,
                                             op0=ALU.add, op1=ALU.max, accum_out=small[:, 0, g % 4:g % 4 + 1]).then_inc(s_mx, 1)
                    dve.wait_ge(s_mx, g + 1)
                    dve.tensor_scalar(small[:, 1, g % 4:g % 4 + 1], small[:, 0, g % 4:g % 4 + 1], -1.0, None, ALU.mult).then_inc(s_sc, 1)
                    done += n // P
                    while halves and (n_halves - len(halves) + 1) * todo <= n_halves * done:
                        select_half()
                elif e[0] == "turn":
                    for u, b0, nb in units[e[1]]:
                        if by_dve[u]:
                            dve.wait_ge(s_t, u + 1)
                            if e[1] >= 2:
                                dve.wait_ge(s_o, e[1] - 1)
                            dve.tensor_copy(pT[:, e[1] % 2, b0 * P:(b0 + nb) * P], pt[u % 2][:, 0:nb * P]).then_inc(s_pt[1], 1)
                elif e[0] == "value" and heads[e[1]][2] == H - 1:
                    n = e[1] // H
                    dve.wait_ge(s_o, e[1] + 1)
                    dve_out(dve, None, n)
                elif e[0] == "out":
                    m = misc[("o",) + e[1:]]
                    ts = slice(e[2] * P, (e[2] + 1) * P)
                    dve.wait_ge(s_ma, m + 1)
                    fs = slice(e[1] * HT, (e[1] + 1) * HT)
                    dve.tensor_tensor(oT_lo[:, fs, ts], pm[:].rearrange("p (f c) -> p f c", c=P),
                                      oT_hi[:, fs, ts].bitcast(F32), ALU.subtract).then_inc(s_ml, 1)
            dve.wait_ge(s_flipped, 3)
            dve.tensor_copy(bias_s[:, FAR:KS], ps[0][:, 0:KS - FAR]).then_inc(s_be[0], 1)
            dve.wait_ge(s_be[0], 2)
            dve.tensor_copy(bias_s[:, 0:FAR], bias_s[:, FAR:FAR + 1].broadcast_to([P, FAR])).then_inc(s_mask, 1)
            dve.wait_ge(s_mask, 2)
            for e, s, x, b in splan:
                g, n = NH + s, NTT + s
                if e == "keys":
                    for f, u in enumerate(kunits[s]):
                        if by_dve[u]:
                            dve.wait_ge(s_t, u + 1)
                            dve.tensor_copy(kTs[s % 2][:, f, 0:PAST], pt[u % 2][:]).then_inc(s_pt[1], 1)
                elif e == "score":
                    dve.wait_ge(s_s, g + 1)
                    if x == 0:
                        dve.wait_ge(s_t, (units[NH - 3 + s][-1][0] if s < 3 else punits[s - 3][-1]) + 1)
                        dve.tensor_tensor_reduce(out=in_halves(sc_of(g, 0, KS)), in0=both_halves(g), in1=in_halves(bias_s[:]), scale=1.0, scalar=GONE,
                                                 op0=ALU.add, op1=ALU.max, accum_out=small[:, 0, g % 4:g % 4 + 1]).then_inc(s_mx, 1)
                    else:
                        dve.tensor_reduce(out=small[:, 0, g % 4:g % 4 + 1], in_=both_halves(g), axis=AX.XY, op=ALU.max).then_inc(s_mx, 1)
                    dve.wait_ge(s_mx, g + 1)
                    dve.tensor_scalar(small[:, 1, g % 4:g % 4 + 1], small[:, 0, g % 4:g % 4 + 1], -1.0, None, ALU.mult).then_inc(s_sc, 1)
                elif e == "turn":
                    for j, u in enumerate(punits[s]):
                        if by_dve[u]:
                            dve.wait_ge(s_t, u + 1)
                            dve.wait_ge(s_o, g - 1)
                            if j == 0:
                                dve.tensor_copy(pT[:, s % 2, 0:PAST], pt[u % 2][:]).then_inc(s_pt[1], 1)
                            else:
                                dve.tensor_copy(pT[0:DEC_S, s % 2, PAST:PAST + P], pt[u % 2][0:DEC_S, 0:P]).then_inc(s_pt[1], 1)
                elif e == "value":
                    dve.wait_ge(s_o, g + 1)
                    dve.reciprocal(rec[:, n % 2, 0:1], sums[:, 0, s % H:s % H + 1]).then_inc(s_rc, 1)
                    dve.wait_ge(s_rc, n + 1)
                    if s >= 2:
                        dve.wait_ge(s_mf, misc[("so", s - 2)] + 1)
                    dve.tensor_scalar(osb[:, n % 2, :], po[:], rec[:, n % 2, 0:1], None, ALU.mult).then_inc(s_os, 1)
                else:
                    m = misc[("so", s)]
                    dve.wait_ge(s_ma, m + 1)
                    cs = slice(SEQ + b * DEC_S, SEQ + (b + 1) * DEC_S)
                    fs = slice(x * HT, (x + 1) * HT)
                    for r in range(2):
                        i = dve.tensor_tensor(oT_lo[r * HD:(r + 1) * HD, fs, cs], diag(r),
                                              oT_hi[r * HD:(r + 1) * HD, fs, cs].bitcast(F32), ALU.subtract)
                    i.then_inc(s_ml, 1)

        def act_exp(act, g, n, src, total):
            act.wait_ge(s_sc, g + 1)
            act.activation(sc_of(g, 0, n) if len(src.shape) == 2 else in_halves(sc_of(g, 0, n)), src, ACT.Exp, bias=small[:, 1, g % 4:g % 4 + 1], accum_out=total).then_inc(s_p, 1)

        @block.scalar
        def _(act):
            act.wait_ge(s_zero, 1)
            for e in plan:
                if e[0] == "prep":
                    x, t = e[1:]
                    n = x * NP + t
                    act.wait_ge(s_mf, misc[("k", x, t)] + 1)
                    act.activation(kT[x][:, :, t * P:(t + 1) * P], pm[:].rearrange("p (f c) -> p f c", c=P), ACT.Copy).then_inc(s_ma, 1)
                    act.wait_ge(s_mf, misc[("q", x, t)] + 1)
                    if n >= 2:
                        act.wait_ge(s_s, (n - 1) * H)
                    for r in range(2):
                        i = act.activation(qT[r * HD:(r + 1) * HD, n % 2, r::2, :],
                                           pm[r * HD:(r + 1) * HD, :].rearrange("p (f c) -> p f c", c=P), ACT.Copy, scale=HD ** -0.5)
                    i.then_inc(s_ma, 1)
                    if n == 0:
                        act.wait_ge(s_flipped, 2)
                        act.activation(bias[:, H // 2:H, FAR:BAND], ps[1][:].rearrange("p (h c) -> p h c", c=NEAR), ACT.Copy).then_inc(s_be[1], 1)
                elif e[0] == "score":
                    g = e[1]
                    x, t, h = heads[g]
                    n = P * blocks_of(x, t)[1]
                    if h == 0 and g >= 2 * H:
                        act.wait_ge(s_rc, g // H - 1)
                    act_exp(act, g, n, sc_of(g, 0, n), sums[:, (g // H) % 2, h:h + 1])
                elif e[0] == "turn":
                    for u, b0, nb in units[e[1]]:
                        if not by_dve[u]:
                            act.wait_ge(s_t, u + 1)
                            if e[1] >= 2:
                                act.wait_ge(s_o, e[1] - 1)
                            act.activation(pT[:, e[1] % 2, b0 * P:(b0 + nb) * P], pt[u % 2][:, 0:nb * P], ACT.Copy).then_inc(s_pt[0], 1)
                elif e[0] == "out":
                    m = misc[("o",) + e[1:]]
                    act.wait_ge(s_mf, m + 1)
                    act.activation(oT_hi[:, e[1] * HT:(e[1] + 1) * HT, e[2] * P:(e[2] + 1) * P],
                                   pm[:].rearrange("p (f c) -> p f c", c=P), ACT.Copy).then_inc(s_ma, 1)
            for x in range(2):
                for j in range(2):
                    act.wait_ge(s_mf, misc[(("sk", "sq")[j], x)] + 1)
                    act.activation(snT[:, x, j, :, :], pm[:].rearrange("p (f c) -> p f c", c=P), ACT.Copy,
                                   scale=HD ** -0.5 if j else 1.0).then_inc(s_ma, 1)
            act.wait_ge(s_rc, NTT)
            for e, s, x, b in splan:
                g = NH + s
                if e == "keys":
                    for f, u in enumerate(kunits[s]):
                        if not by_dve[u]:
                            act.wait_ge(s_t, u + 1)
                            act.activation(kTs[s % 2][:, f, 0:PAST], pt[u % 2][:], ACT.Copy).then_inc(s_pt[0], 1)
                elif e == "score":
                    if s >= H:
                        act.wait_ge(s_rc, NTT + s - H + 1)
                    if x == 1:
                        act.wait_ge(s_t, punits[s - 3][-1] + 1)
                    act_exp(act, g, KS, sc_of(g, 0, KS) if x == 0 else both_halves(g), sums[:, 0, s % H:s % H + 1])
                elif e == "turn":
                    for j, u in enumerate(punits[s]):
                        if not by_dve[u]:
                            act.wait_ge(s_t, u + 1)
                            act.wait_ge(s_o, g - 1)
                            if j == 0:
                                act.activation(pT[:, s % 2, 0:PAST], pt[u % 2][:], ACT.Copy).then_inc(s_pt[0], 1)
                            else:
                                act.activation(pT[0:DEC_S, s % 2, PAST:PAST + P], pt[u % 2][0:DEC_S, 0:P], ACT.Copy).then_inc(s_pt[0], 1)
                elif e == "out":
                    act.wait_ge(s_mf, misc[("so", s)] + 1)
                    cs = slice(SEQ + b * DEC_S, SEQ + (b + 1) * DEC_S)
                    for r in range(2):
                        i = act.activation(oT_hi[r * HD:(r + 1) * HD, x * HT:(x + 1) * HT, cs], diag(r), ACT.Copy)
                    i.then_inc(s_ma, 1)

        def wait_turned(pe, u):
            pe.wait_ge(s_pt[by_dve[u]], by_dve[0:u + 1].count(by_dve[u]))

        def pe_turn(pe, u, blocks):
            if u >= 2:
                wait_turned(pe, u - 2)
            for dst, src in blocks:
                last = pe.transpose(dst, src, ident[:])
            last.then_inc(s_t, 1)

        def pe_rows(pe, key, src):
            out = pe_misc(pe, key)
            for f in range(HT):
                last = pe.transpose(out[:, f * P:(f + 1) * P], src[:, f * P:(f + 1) * P], ident[:])
            last.then_inc(s_mf, 1)

        @block.tensor
        def _(pe):
            for e in plan:
                if e[0] == "prep":
                    x, t = e[1:]
                    n = x * NP + t
                    pe.wait_ge(s_row, 32 * (n + 1))
                    pe_rows(pe, ("k", x, t), rows[:, 0, :])
                    pe_rows(pe, ("q", x, t), rows[:, 1, :])
                    if n == 0:
                        pe.wait_ge(s_bias, 16)
                        pe.wait_ge(s_flip, 4)
                        for i in range(2):
                            for j in range(2):
                                h2 = 4 * i + 2 * j
                                last = pe.matmul(ps[i][:, j * 512:(j + 1) * 512], flip[:],
                                                 raw[:, h2:h2 + 2, :].rearrange("p h c -> p (h c)"), start=True, stop=True)
                            last.then_inc(s_flipped, 1)
                        for i in range(2):
                            pe.wait_ge(s_be[i], 1)
                elif e[0] == "score":
                    g = e[1]
                    x, t, h = heads[g]
                    k0, nb = blocks_of(x, t)
                    if h == 0:
                        pe.wait_ge(s_ma, misc[("q", x, t)] + 1)
                    if g >= 2:
                        pe.wait_ge(s_mx, g - 1)
                    for c in range(0, nb, 4):
                        c1 = min(c + 4, nb)
                        last = pe.matmul(ps[g % 2][:, c * P:c1 * P], qT[:, (x * NP + t) % 2, h, :],
                                         kT[x][:, h // 2, (k0 + c) * P:(k0 + c1) * P], start=True, stop=True)
                    last.then_inc(s_s, 1)
                elif e[0] == "turn":
                    g = e[1]
                    pe.wait_ge(s_p, g + 1)
                    for u, b0, nb in units[g]:
                        pe_turn(pe, u, [(pt[u % 2][:, j * P:(j + 1) * P], sc_of(g, (b0 + j) * P, (b0 + j + 1) * P)) for j in range(nb)])
                elif e[0] == "value":
                    g = e[1]
                    x, t, h = heads[g]
                    k0, nb = blocks_of(x, t)
                    if t == 0 and h == 0:
                        pe.wait_ge(s_v[x], 16)
                    if h == 0 and g:
                        pe.wait_ge(s_os, g // H)
                    for u, _, _ in units[g]:
                        wait_turned(pe, u)
                    for j in range(nb):
                        last = pe.matmul(po[:, h * HD:(h + 1) * HD], pT[:, g % 2, j * P:(j + 1) * P],
                                         v[x][:, k0 + j, h * HD:(h + 1) * HD], start=j == 0, stop=j == nb - 1)
                    last.then_inc(s_o, 1)
                elif e[0] == "out":
                    n = e[1] * NP + e[2]
                    pe.wait_ge(s_os, n + 1)
                    pe_rows(pe, ("o",) + e[1:], osb[:, n % 2, :])
            pe.wait_ge(s_bias, 16 * (H + 1))
            pe.wait_ge(s_mx, NH)
            pe.matmul(ps[0][:, 0:KS - FAR], flip_s[:].rearrange("p h q -> p (h q)"), raw_s[:], start=True, stop=True).then_inc(s_flipped, 1)
            pe.wait_ge(s_be[0], 2)
            pe.wait_ge(s_sr, 64)
            for x in range(2):
                for j in range(2):
                    pe_rows(pe, (("sk", "sq")[j], x), srow[:, x, j, :])

            for e, s, x, b in splan:
                g = NH + s
                if e == "keys":
                    pe.wait_ge(s_kc[s % 2], 16 * (s // 2 + 1))
                    for f, u in enumerate(kunits[s]):
                        pe_turn(pe, u, [(pt[u % 2][:, k * P:(k + 1) * P], kc[s % 2][:, k, f * P:(f + 1) * P]) for k in range(PAST // P)])
                elif e == "score":
                    pe.wait_ge(s_bd, 3 * s + 3)
                    for u in kunits[s][-2:]:
                        wait_turned(pe, u)
                    pe.wait_ge(s_mx, g - 1)
                    if x == 1:
                        pe.wait_ge(s_p, g - 1)
                        if b == 0:
                            pe.wait_ge(s_rep, 2)
                    for c0, c1 in ((0, KS // 2), (KS // 2, KS)):
                        out = ps[g % 2][:, c0 // (KS // 2) * 512:c0 // (KS // 2) * 512 + KS // 2]
                        for f in range(HT):
                            last = pe.matmul(out, bd[s % 2][:, f * P:(f + 1) * P], kTs[s % 2][:, f, c0:c1],
                                             start=f == 0, stop=f == HT - 1 and x == 0)
                        if x == 1:
                            last = pe.matmul(out, rep[:, b, :, :].rearrange("p h q -> p (h q)"),
                                             selb[:, SELB_AT[NP] + c0:SELB_AT[NP] + c1], start=False, stop=True)
                    last.then_inc(s_s, 1)
                elif e == "turn":
                    pe.wait_ge(s_p, g + 1)
                    u = punits[s][0]
                    pe_turn(pe, u, [(pt[u % 2][:, k * P:(k + 1) * P], sc_of(g, k * P, (k + 1) * P)) for k in range(PAST // P)])
                    u = punits[s][1]
                    pe_turn(pe, u, [(pt[u % 2][0:DEC_S, 0:P], sc_of(g, PAST, KS))])
                elif e == "value":
                    pe.wait_ge(s_os, NTT + s)
                    pe.wait_ge(s_vc[s % 2], 32 * (s // 2 + 1))
                    for u in punits[s]:
                        wait_turned(pe, u)
                    for k in range(PAST // P):
                        pe.matmul(po[:], pT[:, s % 2, k * P:(k + 1) * P], vc[s % 2][:, k, :], start=k == 0, stop=False)
                    pe.matmul(po[:], pT[0:DEC_S, s % 2, PAST:PAST + P], vn[s % 2][:], start=False, stop=True).then_inc(s_o, 1)
                else:
                    pe.wait_ge(s_os, NTT + s + 1)
                    pe_rows(pe, ("so", s), osb[:, (NTT + s) % 2, :])

def wo_phase(nc, at, x_sb, x_mid, w_out, T, st, ident, g_next):
    tag = "o"
    w_v = w_out.rearrange("a (k p) n -> p (a k) n", p=P)
    with ExitStack() as ctx:
        sem = lambda n: ctx.enter_context(nc.semaphore(f"{tag}_{n}"))
        keep = Plan(nc, tag, at)
        w_hi = [keep(f"w_hi{k}", [P, D], F32R) for k in range(KT)]
        w_lo = [keep(f"w_lo{k}", [P, D], F32R) for k in range(KT)]
        raw = [keep(f"raw{i}", [P, D], F32) for i in range(2)]
        after = TileNorm(nc, ctx, tag + "b", at_end(4 * D * 4), st, x_sb, T, ident, g_next)
        assert keep.at <= at_end(4 * D * 4)
        py = [ctx.enter_context(nc.psum_tensor(f"{tag}_py{i}", [P, 512], F32)) for i in range(4)]
        xp = ctx.enter_context(nc.psum_tensor(f"{tag}_xp", [P, 4, 512], F32))
        s_raw = [sem(f"w_loaded{i}") for i in range(2)]
        s_x = [sem(f"x_loaded{i}") for i in range(KT // 2)]
        s_hi, s_lo, s_y, s_acc = sem("w_hi"), sem("w_split"), sem("y_done"), sem("y_added")
        block = ctx.enter_context(nc.Block())

        def x_done(eng, t):
            eng.wait_ge(s_acc, 2 * (t + 1))

        @block.sync
        def _(sp):
            x_v = x_mid.rearrange("(t p) d -> p t d", p=P)
            for k in range(KT):
                if k >= 2:
                    sp.wait_ge(s_lo, k - 1)
                sp.dma_start(raw[k % 2][:], w_v[:, k, :]).then_inc(s_raw[k % 2], 16)
                if k % 2:
                    t0, t1 = k - 1, NT if k == KT - 1 else k + 1
                    sp.dma_start(x_sb[:, t0:t1, :], x_v[:, t0:t1, :]).then_inc(s_x[k // 2], 16)
            after.load(sp)

        @block.scalar
        def _(act):
            for k in range(KT):
                act.wait_ge(s_raw[k % 2], 16 * (k // 2 + 1))
                act.activation(w_hi[k][:], raw[k % 2][:], ACT.Copy).then_inc(s_hi, 1)
            for t in range(TileNorm.SLOTS):
                after.act(act, t, xp, x_done)

        @block.vector
        def _(dve):
            for k in range(KT):
                dve.wait_ge(s_hi, k + 1)
                dve.tensor_tensor(w_lo[k][:], raw[k % 2][:], w_hi[k][:].bitcast(F32), ALU.subtract).then_inc(s_lo, 1)
            for t in range(TileNorm.SLOTS):
                after.dve_lo(dve, t, xp)
                if t < NT:
                    dve.wait_ge(s_x[min(t // 2, KT // 2 - 1)], 16)
                for k in range(2 * t, 2 * t + 2) if t < NT else ():
                    xs = x_sb[:, t, k % 2 * 512:(k % 2 + 1) * 512]
                    dve.wait_ge(s_y, k + 1)
                    dve.tensor_tensor(xs, py[k % 4][:], xs, ALU.add).then_inc(s_acc, 1)
                after.dve(dve, t, x_done)

        @block.tensor
        def _(pe):
            def piece(k, kt):
                t, ns = k // 2, slice(k % 2 * 512, (k % 2 + 1) * 512)
                ts = slice(t * P, (t + 1) * P)
                return three_pass(pe, py[k % 4][:], (T[0][:, kt, ts], T[1][:, kt, ts]),
                                  (w_hi[kt][:, ns], w_lo[kt][:, ns]), kt == 0, kt == KT - 1)

            for kt in range(KT):
                pe.wait_ge(s_lo, kt + 1)
                for k in range(4):
                    last = piece(k, kt)
                    if kt == KT - 1:
                        last.then_inc(s_y, 1)
            after.pe(pe, 0, xp)
            after.pe(pe, 1, xp)
            for t in range(2, TileNorm.SLOTS):
                for k in range(2 * t, 2 * t + 2) if t < NT else ():
                    pe.wait_ge(s_acc, k - 3)
                    for kt in range(KT):
                        last = piece(k, kt)
                    last.then_inc(s_y, 1)
                after.pe(pe, t, xp)


def program(nc, i, o):
    with ExitStack() as outer:
        run_phases(nc, outer, i, o)


def run_phases(nc, outer, i, o):
    plan = Plan(nc, "r", SBUF_START)
    ident = plan("ident", [P, P], F32)
    st = plan("stats", [P, 6, NT], F32)
    at_selb = plan.at
    selb = plan("selb", [P, SELB_AT[NP] + KS], BF16)
    at_x = plan.at
    x_sb = plan("x", [P, NT, D], F32)
    at = plan.at
    late_acc = [Plan(nc, "r", at_x + 4 * SEQ)("late_acc6", [P, SEQ - P], F32), Plan(nc, "r", at_x)("late_acc7", [P, SEQ], F32)]
    top = Plan(nc, "r", at_end(0))
    T = top("T_hi", [P, KT, ROWS], F32R), top("T_lo", [P, KT, ROWS], F32R)
    dram = lambda n, s: nc.dram_tensor(n, s, F32, kind="Internal").ap()
    x_mid, proj, urel = dram("x_mid", [ROWS, D]), dram("proj", [ROWS, 2 * N_QKV]), dram("urel", [H, 6 * P])
    xp_v = i["x_prompt"].rearrange("b (t p) d -> p (b t) d", p=P)
    xs_v = i["x_sample"].rearrange("b s d -> (b s) d")

    def load_rows(sp, s_x, t0, t1):
        for t in range(t0, t1):
            sp.dma_start(x_sb[:, t, :], xp_v[:, t, :] if t < NP else xs_v).then_inc(s_x[t], 16)

    with ExitStack() as ctx:
        s_id = outer.enter_context(nc.semaphore("ident_step"))
        block = ctx.enter_context(nc.Block())

        @block.gpsimd
        def _(pool):
            pool.memset(ident[:], 0.0).then_inc(s_id, 1)
            pool.wait_ge(s_id, 1)
            pool.affine_select(out=ident[:], in_=ident[:], compare_op=ALU.not_equal, fill=1.0, base=0,
                               pattern=[[-1, P]], channel_multiplier=1).then_inc(s_id, 1)
            pool.wait_ge(s_id, 2)

    early = EarlyWeights(nc, outer, at, i["w_in"])
    ffn_phase(nc, "f1", at_selb, at, x_sb, T, st, ident, load_rows, i["ffn1_norm"][0], i["ffn1_w_gate"], i["ffn1_w_up"],
              i["ffn1_w_down"], i["mix_norm"][0], dict(sp=early.sp, act=early.act, dve=early.dve), None)
    wi_phase(nc, at_x, at, x_sb, T, ident, selb, late_acc, early, i["w_in"], i["rel_bias"], urel, i["rope_cos"], i["rope_sin"], i["cache_idx_k"],
             x_mid, proj, o["idx_k_prompt"], o["idx_k_sample"])
    FW = H * HD
    flat = lambda a: a.rearrange("a b s h d -> (a b s) (h d)")
    keep0 = SEQ - min(LEFT * CHUNK, SEQ)
    outs = [(flat(o["a_k_prompt"]), FW, keep0, SEQ), (flat(o["a_v_prompt"]), 2 * FW, keep0, SEQ),
            (flat(o["b_k_prompt"]), N_QKV + FW, 0, SEQ), (flat(o["b_v_prompt"]), N_QKV + 2 * FW, 0, SEQ),
            (flat(o["a_k_sample"]), FW, SEQ, ROWS), (flat(o["a_v_sample"]), 2 * FW, SEQ, ROWS),
            (flat(o["b_k_sample"]), N_QKV + FW, SEQ, ROWS), (flat(o["b_v_sample"]), N_QKV + 2 * FW, SEQ, ROWS)]
    attn_phase(nc, at_x, ident, selb, late_acc, proj, urel,
               ((i["cache_a_k"], i["cache_a_v"]), (i["cache_b_k"], i["cache_b_v"])), *T, outs)
    wo_phase(nc, at, x_sb, x_mid, i["w_out"], T, st, ident, i["ffn2_norm"][0])
    y_p, y_s = o["y_prompt"].rearrange("b s d -> (b s) d"), o["y_sample"].rearrange("b s d -> (b s) d")
    ffn_phase(nc, "f2", at_selb, at, x_sb, T, st, ident, None, None, i["ffn2_w_gate"], i["ffn2_w_up"], i["ffn2_w_down"],
              i["final_norm"], None, lambda t: y_p[t * P:(t + 1) * P, :] if t < NP else y_s)


_INS = ["x_prompt", "x_sample", "cache_a_k", "cache_a_v", "cache_b_k", "cache_b_v", "cache_idx_k",
        "ffn1_norm", "ffn1_w_gate", "ffn1_w_up", "ffn1_w_down", "mix_norm", "w_in", "rel_bias", "w_out",
        "ffn2_norm", "ffn2_w_gate", "ffn2_w_up", "ffn2_w_down", "final_norm"]
_OUTS = [("y_prompt", (1, SEQ, D)), ("y_sample", (DEC_B, DEC_S, D)),
         ("a_k_prompt", (1, 1, min(LEFT * CHUNK, SEQ), H, HD)), ("a_v_prompt", (1, 1, min(LEFT * CHUNK, SEQ), H, HD)),
         ("b_k_prompt", (1, 1, SEQ, H, HD)), ("b_v_prompt", (1, 1, SEQ, H, HD)), ("idx_k_prompt", (1, 1, SEQ, ID)),
         ("a_k_sample", (1, DEC_B, DEC_S, H, HD)), ("a_v_sample", (1, DEC_B, DEC_S, H, HD)),
         ("b_k_sample", (1, DEC_B, DEC_S, H, HD)), ("b_v_sample", (1, DEC_B, DEC_S, H, HD)),
         ("idx_k_sample", (1, DEC_B, DEC_S, ID))]


def rope_tables():
    half = HD // 2
    inv = np.power(np.float32(10000.0), -np.arange(half, dtype=np.float32) / np.float32(half)).astype(np.float32)
    pos = np.concatenate([np.arange(SEQ), PAST + np.tile(np.arange(DEC_S), DEC_B)]).astype(np.float32)
    angle = (pos[:, None] * inv[None, :]).astype(np.float32)
    return np.cos(angle), np.sin(angle)


def kernel(**inputs):
    import concourse.bacc as _bacc
    from concourse.bass_utils import run_bass_kernel_spmd as _run

    nc = _bacc.Bacc("TRN2", target_bir_lowering=False, num_devices=1)
    arrays, ins, outs = {}, {}, {}
    for name in _INS:
        a = np.ascontiguousarray(inputs[name])
        arrays[f"in_{name}"] = a
        ins[name] = nc.dram_tensor(f"in_{name}", a.shape, mybir.dt.from_np(a.dtype), kind="ExternalInput").ap()
    for name, a in zip(("rope_cos", "rope_sin"), rope_tables()):
        arrays[f"in_{name}"] = a
        ins[name] = nc.dram_tensor(f"in_{name}", a.shape, F32, kind="ExternalInput").ap()
    for name, shape in _OUTS:
        outs[name] = nc.dram_tensor(f"out_{name}", shape, F32, kind="ExternalOutput").ap()
    program(nc, ins, outs)
    r = _run(nc, [arrays], core_ids=[0])
    return tuple(r.results[0][f"out_{name}"] for name, _ in _OUTS)
```
